# Optimizing a Trainium2 kernel written in Bass

```python
import math
import jax, jax.numpy as jnp
from jax import lax
import numpy as np

D_MODEL = 1024
BATCH = 1
SEQ = 512
DEPTH = 2
DEC_BATCH = 8
DEC_SEQ = 1
PAST_LEN = 512
PAGE_SIZE = 128

N_A_LAYERS = DEPTH // 2
N_B_LAYERS = DEPTH - N_A_LAYERS
CHUNK = 128
D_GM = 3 * D_MODEL
N_SGU_GROUPS = 8
SGU_GROUP = D_GM // N_SGU_GROUPS
N_HEADS = 8
HEAD_DIM = D_MODEL // (2 * N_HEADS)
V_DIM = 2 * HEAD_DIM
Q_BLOCK = 128
N_EXPERT_GROUPS = 4
EXPERTS_PER_GROUP = 4
N_EXPERTS = N_EXPERT_GROUPS * EXPERTS_PER_GROUP
TOP_K_INNER = 2
D_EXPERT = 256
RMS_EPS = 1e-6
MASK_VALUE = -1e30

kernel_name = 'yoco_gmlp_diffattn_hmoe_step'

F32 = jnp.float32

def rms_norm(x, g):
    xf = x.astype(F32)
    y = xf * lax.rsqrt(jnp.mean(xf * xf, axis=-1, keepdims=True) + RMS_EPS)
    return (y * g.astype(F32)).astype(x.dtype)

def chunk_spatial_gate(v, w_s, b_s):
    b, t, _ = v.shape
    pad = (-t) % CHUNK
    vp = jnp.pad(v, ((0, 0), (0, pad), (0, 0)))
    nc = (t + pad) // CHUNK
    vp = vp.reshape(b, nc, CHUNK, N_SGU_GROUPS, SGU_GROUP)
    causal = jnp.tril(jnp.ones((CHUNK, CHUNK), dtype=bool))
    w = jnp.where(causal[None], w_s, jnp.zeros_like(w_s)).astype(v.dtype)
    out = jnp.einsum('gts,bcsgk->bctgk', w, vp) + b_s.T[None, None, :, :, None].astype(v.dtype)
    return out.reshape(b, nc * CHUNK, D_GM)[:, :t]

def gmlp_mixer(h, w_uv, sgu_gain, w_s, b_s, w_o):
    z = jax.nn.gelu(h @ w_uv)
    u, v = jnp.split(z, 2, axis=-1)
    v = rms_norm(v, sgu_gain)
    return (u * chunk_spatial_gate(v, w_s, b_s)) @ w_o, v

def hierarchical_moe(h, w_rg, b_rg, w_re, b_re, w_gate, w_up, w_down):
    shape = h.shape
    hf = h.reshape(-1, shape[-1])
    g_prob = jax.nn.softmax((hf @ w_rg + b_rg).astype(F32), axis=-1)
    p_grp, grp = lax.top_k(g_prob, 1)
    e_logits = (jnp.einsum('td,gde->tge', hf, w_re) + b_re).astype(F32)
    e_logits = jnp.take_along_axis(e_logits, grp[:, :, None], axis=1)[:, 0]
    e_val, e_idx = lax.top_k(e_logits, TOP_K_INNER)
    e_w = jax.nn.softmax(e_val, axis=-1) * p_grp
    inner = jnp.sum(jax.nn.one_hot(e_idx, EXPERTS_PER_GROUP, dtype=F32) * e_w[..., None], axis=1)
    gate = (jax.nn.one_hot(grp[:, 0], N_EXPERT_GROUPS, dtype=F32)[:, :, None]
            * inner[:, None, :]).reshape(-1, N_EXPERTS)
    hid = jax.nn.silu(jnp.einsum('td,edf->tef', hf, w_gate)) * jnp.einsum('td,edf->tef', hf, w_up)
    y = jnp.einsum('tef,efd->td', hid * gate[..., None].astype(hid.dtype), w_down)
    return y.reshape(shape)

def diff_attention(q, k_parts, v_parts, q_pos, k_pos, lam, slopes):
    qf = q.astype(F32) * (HEAD_DIM ** -0.5)
    s = jnp.concatenate([jnp.einsum('bqhmd,bkhmd->bmhqk', qf, k.astype(F32)) for k in k_parts], axis=-1)
    dist = (q_pos[:, None] - k_pos[None, :]).astype(F32)
    bias = jnp.where(dist >= 0, -slopes[:, None, None] * dist, MASK_VALUE)
    p = jax.nn.softmax(s + bias, axis=-1)
    a = p[:, 0] - lam * p[:, 1]
    splits = [int(c) for c in np.cumsum([k.shape[1] for k in k_parts])[:-1]]
    a_parts = jnp.split(a, splits, axis=-1)
    o = jnp.einsum('bhqk,bkhv->bqhv', a_parts[0], v_parts[0].astype(F32))
    for a_i, v_i in zip(a_parts[1:], v_parts[1:]):
        o = o + jnp.einsum('bhqk,bkhv->bqhv', a_i, v_i.astype(F32))
    return o

def channel_mixer(x, i, p):
    return hierarchical_moe(rms_norm(x, p['norm_ffn'][i]), p['w_router_group'][i], p['b_router_group'][i],
                            p['w_router_expert'][i], p['b_router_expert'][i],
                            p['w_e_gate'][i], p['w_e_up'][i], p['w_e_down'][i])

def a_layers(x, p):
    v_rows = []
    for i in range(N_A_LAYERS):
        h = rms_norm(x, p['norm_mix'][i])
        o, v = gmlp_mixer(h, p['w_uv'][i], p['sgu_gain'][i], p['w_sgu'][i], p['b_sgu'][i], p['w_gmlp_o'][i])
        x = x + o
        x = x + channel_mixer(x, i, p)
        v_rows.append(v)
    return x, v_rows

def kv_project(x, p):
    b, t, _ = x.shape
    hk = rms_norm(x, p['norm_kv'])
    k = (hk @ p['w_k']).reshape(b, t, N_HEADS, 2, HEAD_DIM)
    v = (hk @ p['w_v']).reshape(b, t, N_HEADS, V_DIM)
    return k, v

def b_layers(x, attend, p):
    for j in range(N_B_LAYERS):
        i = N_A_LAYERS + j
        lam_init = 0.8 - 0.6 * math.exp(-0.3 * i)
        h = rms_norm(x, p['norm_mix'][i])
        b, t, _ = h.shape
        q = (h @ p['w_q'][j]).reshape(b, t, N_HEADS, 2, HEAD_DIM)
        lq = p['lam_q'][j].astype(F32)
        lk = p['lam_k'][j].astype(F32)
        lam = jnp.exp(jnp.sum(lq[0] * lk[0])) - jnp.exp(jnp.sum(lq[1] * lk[1])) + lam_init
        o = attend(q, lam)
        o = rms_norm(o, p['subln_gain'][j]) * (1.0 - lam_init)
        x = x + o.reshape(b, t, N_HEADS * V_DIM).astype(x.dtype) @ p['w_attn_o'][j]
        x = x + channel_mixer(x, i, p)
    return x

def setup_inputs(seed: int = 0) -> dict:
    key = jax.random.key(seed)
    ks = jax.random.split(key, 32)
    n_pages = PAST_LEN // PAGE_SIZE
    n_used = DEC_BATCH * n_pages
    n_pool = n_used + max(1, n_used // 4)

    def nrm(k, shape, scale):
        return jax.random.normal(k, shape, F32) * scale

    page_table = jax.random.permutation(ks[4], n_pool)[:n_used].reshape(DEC_BATCH, n_pages).astype(jnp.int32)
    return {
        'x_prompt': nrm(ks[0], (BATCH, SEQ, D_MODEL), 1.0),
        'x_sample': nrm(ks[1], (DEC_BATCH, DEC_SEQ, D_MODEL), 1.0),
        'cache_k': nrm(ks[2], (n_pool, PAGE_SIZE, N_HEADS, 2, HEAD_DIM), 1.0),
        'cache_v': nrm(ks[3], (n_pool, PAGE_SIZE, N_HEADS, V_DIM), 1.0),
        'page_table': page_table,
        'norm_mix': 1.0 + nrm(ks[5], (DEPTH, D_MODEL), 0.02),
        'norm_ffn': 1.0 + nrm(ks[6], (DEPTH, D_MODEL), 0.02),
        'w_uv': nrm(ks[7], (N_A_LAYERS, D_MODEL, 2 * D_GM), D_MODEL ** -0.5),
        'sgu_gain': 1.0 + nrm(ks[8], (N_A_LAYERS, D_GM), 0.02),
        'w_sgu': nrm(ks[9], (N_A_LAYERS, N_SGU_GROUPS, CHUNK, CHUNK), CHUNK ** -0.5),
        'b_sgu': 1.0 + nrm(ks[10], (N_A_LAYERS, N_SGU_GROUPS, CHUNK), 0.1),
        'w_gmlp_o': nrm(ks[11], (N_A_LAYERS, D_GM, D_MODEL), D_GM ** -0.5),
        'norm_kv': 1.0 + nrm(ks[12], (D_MODEL,), 0.02),
        'w_k': nrm(ks[13], (D_MODEL, N_HEADS * 2 * HEAD_DIM), D_MODEL ** -0.5),
        'w_v': nrm(ks[14], (D_MODEL, N_HEADS * V_DIM), D_MODEL ** -0.5),
        'w_q': nrm(ks[15], (N_B_LAYERS, D_MODEL, N_HEADS * 2 * HEAD_DIM), D_MODEL ** -0.5),
        'lam_q': nrm(ks[16], (N_B_LAYERS, 2, HEAD_DIM), 0.1),
        'lam_k': nrm(ks[17], (N_B_LAYERS, 2, HEAD_DIM), 0.1),
        'subln_gain': 1.0 + nrm(ks[18], (N_B_LAYERS, V_DIM), 0.02),
        'w_attn_o': nrm(ks[19], (N_B_LAYERS, N_HEADS * V_DIM, D_MODEL), (N_HEADS * V_DIM) ** -0.5),
        'w_router_group': nrm(ks[20], (DEPTH, D_MODEL, N_EXPERT_GROUPS), D_MODEL ** -0.5),
        'b_router_group': nrm(ks[21], (DEPTH, N_EXPERT_GROUPS), 0.01),
        'w_router_expert': nrm(ks[22], (DEPTH, N_EXPERT_GROUPS, D_MODEL, EXPERTS_PER_GROUP), D_MODEL ** -0.5),
        'b_router_expert': nrm(ks[23], (DEPTH, N_EXPERT_GROUPS, EXPERTS_PER_GROUP), 0.01),
        'w_e_gate': nrm(ks[24], (DEPTH, N_EXPERTS, D_MODEL, D_EXPERT), D_MODEL ** -0.5),
        'w_e_up': nrm(ks[25], (DEPTH, N_EXPERTS, D_MODEL, D_EXPERT), D_MODEL ** -0.5),
        'w_e_down': nrm(ks[26], (DEPTH, N_EXPERTS, D_EXPERT, D_MODEL), D_EXPERT ** -0.5),
        'norm_final': 1.0 + nrm(ks[27], (D_MODEL,), 0.02),
    }

def reference(x_prompt, x_sample, cache_k, cache_v, page_table, norm_mix, norm_ffn, w_uv, sgu_gain,
              w_sgu, b_sgu, w_gmlp_o, norm_kv, w_k, w_v, w_q, lam_q, lam_k, subln_gain, w_attn_o,
              w_router_group, b_router_group, w_router_expert, b_router_expert, w_e_gate, w_e_up,
              w_e_down, norm_final):
    p = {'norm_mix': norm_mix, 'norm_ffn': norm_ffn, 'w_uv': w_uv, 'sgu_gain': sgu_gain, 'w_sgu': w_sgu,
         'b_sgu': b_sgu, 'w_gmlp_o': w_gmlp_o, 'norm_kv': norm_kv, 'w_k': w_k, 'w_v': w_v, 'w_q': w_q,
         'lam_q': lam_q, 'lam_k': lam_k, 'subln_gain': subln_gain, 'w_attn_o': w_attn_o,
         'w_router_group': w_router_group, 'b_router_group': b_router_group,
         'w_router_expert': w_router_expert, 'b_router_expert': b_router_expert,
         'w_e_gate': w_e_gate, 'w_e_up': w_e_up, 'w_e_down': w_e_down}
    slopes = 2.0 ** (-8.0 * jnp.arange(1, N_HEADS + 1, dtype=F32) / N_HEADS)

    bsz, seq, _ = x_prompt.shape
    xp, _ = a_layers(x_prompt, p)
    k_p, v_p = kv_project(xp, p)
    pos_p = jnp.arange(seq)
    nb = seq // Q_BLOCK

    def attend_prompt(q, lam):
        qb = jnp.moveaxis(q.reshape(bsz, nb, Q_BLOCK, N_HEADS, 2, HEAD_DIM), 1, 0)
        qpos = pos_p.reshape(nb, Q_BLOCK)

        def block(args):
            q_blk, qp = args
            return diff_attention(q_blk, (k_p,), (v_p,), qp, pos_p, lam, slopes)

        o = lax.map(block, (qb, qpos))
        return jnp.moveaxis(o, 0, 1).reshape(bsz, seq, N_HEADS, V_DIM)

    y_prompt = rms_norm(b_layers(xp, attend_prompt, p), norm_final)

    dec_b, dec_s, _ = x_sample.shape
    past_len = page_table.shape[1] * cache_k.shape[1]
    xs, gmlp_v_rows = a_layers(x_sample, p)
    k_s, v_s = kv_project(xs, p)
    k_past = cache_k[page_table].reshape(dec_b, past_len, N_HEADS, 2, HEAD_DIM)
    v_past = cache_v[page_table].reshape(dec_b, past_len, N_HEADS, V_DIM)
    q_pos_s = past_len + jnp.arange(dec_s)
    k_pos_s = jnp.arange(past_len + dec_s)

    def attend_sample(q, lam):
        return diff_attention(q, (k_past, k_s), (v_past, v_s), q_pos_s, k_pos_s, lam, slopes)

    y_sample = rms_norm(b_layers(xs, attend_sample, p), norm_final)

    n_pp = seq // PAGE_SIZE
    k_prompt = k_p.reshape(bsz, n_pp, PAGE_SIZE, N_HEADS, 2, HEAD_DIM)
    v_prompt = v_p.reshape(bsz, n_pp, PAGE_SIZE, N_HEADS, V_DIM)
    gmlp_v_sample = jnp.stack(gmlp_v_rows)
    return (y_prompt, y_sample, k_prompt, v_prompt, k_s, v_s, gmlp_v_sample)


_drawn_inputs = setup_inputs


def setup_inputs(seed=0):
    import zlib

    import numpy as np

    out = dict(_drawn_inputs(seed))
    spreads = {}
    factors = {'sgu_gain': 2.858,
     'norm_kv': 2.877,
     'lam_q': 8.0,
     'subln_gain': 3.853,
     'b_router_group': 5.115,
     'b_router_expert': 5.031,
     'norm_final': 3.092}
    for name, (base, spread) in spreads.items():
        noise = np.random.default_rng([zlib.crc32(name.encode()), seed]).standard_normal(out[name].shape)
        drawn = base * np.exp(spread * noise) if base else spread * noise
        out[name] = __import__('jax').numpy.asarray(drawn.astype(out[name].dtype))
    for name, factor in factors.items():
        out[name] = (out[name] * factor).astype(out[name].dtype)
    return out
```

```python
import math
from contextlib import ExitStack

import concourse.bass as bass
from concourse import mybir

F32 = mybir.dt.float32
I32 = mybir.dt.int32
ALU = mybir.AluOpType
ACT = mybir.ActivationFunctionType
AX_X = mybir.AxisListType.X

P = 128
D = 1024
DC = D // P
SEQ = 512
NB = 8
T = SEQ + NB
HALF = T // 2
NT = SEQ // P
DG = 3 * D
GC = DG // P
NG = 8
GCOLS = DG // NG
NH = 8
HD = 64
NE = 16
NEG = 4
TOPK = 2
DE = 256
EPS = 1e-6
PAGES = 4
BIG = 1e30
LAM_INIT = 0.8 - 0.6 * math.exp(-0.3)
RING = 6
SLOTW = 2048
SLOTS = 128
PAIRS = TOPK * T
OVF = (PAIRS - TOPK) // SLOTS
ROWS = (NE + OVF) * SLOTS
MAXT = (T - 1) // SLOTS

UV0 = 0
GO0 = UV0 + 2 * DG // 256
MOE0 = GO0 + 3 * DC
KVQ0 = MOE0 + 3 * NE
KP0 = KVQ0 + 12
VP0 = KP0 + NB * PAGES // 2
AO0 = VP0 + NB * PAGES // 2
MOE1 = AO0 + 4
END = MOE1 + 3 * NE

CONSTS = {}
_at = 0
for _name, _n in [("ident", P), ("tri", P), ("ones", P), ("causal", P), ("dist", SEQ), ("past", SEQ), ("sel", 64),
                  ("lt", NE * NE), ("slope", 1), ("even", 1), ("odd", 1), ("valid", 1), ("iota", NEG),
                  ("iota99", NEG), ("first", NE), ("eid", NE), ("tile", OVF)]:
    CONSTS[_name] = (_at, _at + _n)
    _at += _n
NCONST = _at


N_SMALL = 15


def geometry():
    import numpy as np

    k = np.zeros((P, NCONST), np.float32)
    p = np.arange(P)[:, None]

    def put(name, value):
        lo, hi = CONSTS[name]
        k[:, lo:hi] = value

    n = np.arange(P)[None]
    put("ident", p == n)
    put("tri", p < n)
    put("ones", 1)
    put("causal", p <= n)
    dist = p + (NT - 1) * P - np.arange(SEQ)[None]
    put("dist", np.where(dist >= 0, dist, BIG))
    put("past", PAGES * P - np.arange(SEQ)[None])
    put("sel", p // 2 == np.arange(64)[None])
    put("lt", np.tile((np.arange(NE)[None, :] < np.arange(NE)[:, None]).reshape(1, -1), (P, 1)))
    put("slope", -8.0 * 2.0 ** -(1.0 + p // 2 % NH))
    put("even", p % 2 == 0)
    put("odd", p % 2 == 1)
    put("valid", p < NB)
    put("iota", np.arange(NEG)[None])
    put("iota99", np.arange(NEG)[None] + 99)
    put("first", np.arange(NE)[None] * SLOTS)
    put("eid", np.arange(NE)[None])
    put("tile", np.arange(OVF)[None])
    return k


def bcast_rows(ap, pattern, n, layers):
    flat = ap.rearrange(pattern).rearrange("(o n) -> o n", o=1)
    return flat.broadcast_to([n, flat.shape[1]]).rearrange("p (l k) -> p l k", l=layers)


def loads_per_block(b):
    return 32 if KP0 <= b < AO0 else 16


def loaded_value(b):
    return sum(loads_per_block(c) for c in range(b % RING, b + 1, RING))


def build(nc, a, out):
    ctx = ExitStack()

    def sb(name, shape, dt=F32):
        return ctx.enter_context(nc.sbuf_tensor(name, shape, dt))

    def sem(name):
        return ctx.enter_context(nc.semaphore(name))

    def sems(stage, names):
        return [sem(f"{stage}_{n}") for n in names.split()]

    with ctx:
        x = sb("x", [P, 5, D])
        hT = sb("hT", [P, DC, T])
        ring = sb("ring", [P, RING, SLOTW])
        U = sb("U", [P, GC * T])
        V = sb("V", [P, NT * DG])
        K = sb("K", [P, NCONST])
        c_ = {n: K[:, lo:hi] for n, (lo, hi) in CONSTS.items()}
        ident, ones = c_["ident"], c_["ones"]
        gains = sb("gains", [P, 5, DC])
        sgain = sb("sgain", [P, GC])
        wT = sb("wT", [P, NG, P])
        wr = sb("wr", [P, 2, DC, 20])
        rbias = sb("rbias", [P, 2, 20])
        w00 = sb("w00", [NB, 2, NG])
        subg = sb("subg", [P, 1])
        neglam = sb("neglam", [P, 1])
        pt = sb("pt", [1, NB * PAGES], I32)
        ss = sb("ss", [P, 5])
        rstd = sb("rstd", [P, 5])
        root = sb("root", [P, 40])
        vtmp = sb("vtmp", [P, 2, T])
        ps = ctx.enter_context(nc.psum_tensor("ps", [P, 8, 512], F32))

        def take(region, at, shape):
            n = math.prod(shape)
            ap = region[:, at:at + n]
            if len(shape) == 2:
                ap = ap.rearrange("p (a b) -> p a b", a=shape[0])
            if len(shape) == 3:
                ap = ap.rearrange("p (a b c) -> p a b c", a=shape[0], b=shape[1])
            return ap

        xflat = x[:, :, :].rearrange("p t f -> p (t f)")
        VS = xflat[0:NB, 0:DG]
        gtmp = take(xflat, DG, (2, SEQ))
        bsg = take(xflat, DG + 2 * SEQ, (NG, P))
        u = take(U, 0, (GC, T))
        xn = take(U, 0, (5, DC, P))
        e0 = 5 * D
        xs = take(U, e0, (2, DC, P))
        xsT = take(U, e0 + 2 * D, (2, DC, SLOTS))
        e1 = e0 + 2 * D + 2 * DC * SLOTS
        sg = take(U, e1, (2, 2, SLOTS))
        hid = take(U, e1 + 4 * SLOTS, (2, 2, SLOTS))
        ye = take(U, e1 + 8 * SLOTS, (2, D))
        assert e1 + 8 * SLOTS + 2 * D <= GC * T
        vtok = take(U, 0, (NT, D))
        ktok = take(U, NT * D, (2, 512))
        hqT = take(U, 5 * D, (DC, T))
        tok8 = take(U, 5 * D + DC * T, (3, D))[0:NB]
        assert 5 * D + DC * T + 3 * D <= GC * T
        otok = take(U, NT * D, (NT, D))
        st = take(U, 2 * NT * D, (2, 2 * SEQ))
        qbc = take(U, 2 * NT * D + 4 * SEQ, (2, D))
        s0 = 2 * NT * D
        dS = U[:, s0:s0 + SEQ + 1]
        dbias = U[:, s0 + 520:s0 + 520 + SEQ]
        dC = U[:, s0 + 1032:s0 + 1096]
        daT = take(U, s0 + 1096, (PAGES, NB * NH))
        doT = U[:, s0 + 1352:s0 + 1416]
        do64 = U[0:NB * NH, s0 + 1416:s0 + 1544]
        dvown = U[0:NB * NH, s0 + 1544:s0 + 1672]
        daown = U[0:NB * NH, s0 + 1672:s0 + 1673]
        v = take(V, 0, (NT, DG))
        yg = take(V, 0, (5, TOPK, D))
        ow = take(V, 0, (3, SLOTW))
        kT = take(V, 0, (DC, T))
        qT = take(V, DC * T, (DC, T))
        v0 = 2 * DC * T
        prod = take(V, v0, (2, D))
        aT = take(V, v0 + 2 * D, (2, SEQ))
        sK = take(V, v0 + 3 * D, (PAGES, P))
        v1 = v0 + 3 * D + PAGES * P
        mx = take(V, v1, (2, 2))
        nm = take(V, v1 + 4, (2, 2))
        zz = take(V, v1 + 8, (2, 2))
        rz = take(V, v1 + 12, (2, 2))
        oss = take(V, v1 + 16, (NT, NH))
        orr = take(V, v1 + 48, (NT, NH))
        dsm = V[:, v1 + 80:v1 + 96]
        down_ = V[0:NB, v1 + 96:v1 + 112]
        downc = V[:, v1 + 112:v1 + 113]
        assert v1 + 120 <= NT * DG
        oT = hT
        bias8 = wT[:, :, :].rearrange("p g t -> p (g t)").rearrange("p (b f) -> p b f", b=2)
        slot_f = sb("slot_f", [P, 5, TOPK])
        slot_i = sb("slot_i", [P, 5 * TOPK], I32)
        pair_w = sb("pair_w", [P, 5, TOPK])
        ovf_i = sb("ovf_i", [1, 1 + OVF], I32)
        zeros = V[:, 4 * D:5 * D]
        vss = sb("vss", [P, 5, GC])
        gfin = hT[:, :, :].rearrange("p j t -> p (j t)")[:, 0:D]
        gainb = hT[:, :, :].rearrange("p j t -> p (j t)")[0:NB, D:D + DG]
        R, r0 = {}, 10 * D
        for name, shape in (("l", (5, 20)), ("eg", (5, NEG)), ("cand", (5, NEG)), ("oh", (5, NEG)),
                            ("oh1", (5, NEG)), ("oh2", (5, NEG)), ("el", (5, NEG)), ("el2", (5, NEG)),
                            ("gmax", (5,)), ("m1", (5,)), ("m2", (5,)), ("e2", (5,)), ("gs", (5,)), ("den", (5,)),
                            ("least", (5,)), ("pick", (5, NE)), ("m", (5, NE)), ("mm", (2, 5, NE)),
                            ("ov", (NE,)), ("ov1", (NE,)), ("ob", (NE,)), ("dl", (NE,)), ("oend", (NE,)),
                            ("big", (NE, NE)), ("ge", (5, NE)), ("oe", (OVF, NE)), ("oe2", (OVF, NE)),
                            ("of", (1 + OVF,))):
            R[name] = take(V, r0, shape)
            r0 += math.prod(shape)
        assert r0 <= NT * DG
        for name in ("oend", "oe", "oe2", "of"):
            R[name] = R[name][0:1]
        w_st = take(V, D, (NG, P))
        wre_st = V[:, 2 * D:2 * D + 256].rearrange("p (l g f) -> p l g f", l=2, g=NEG)
        wrg_st = V[:, 2 * D + 256:2 * D + 320].rearrange("p (l f) -> p l f", l=2)
        sg_st = V[0:GC, 2 * D + 320:2 * D + 448]
        lam_st = take(V, 2 * D + 448, (2, 2 * HD))
        lam_s = V[:, 2 * D + 704:2 * D + 712]

        slots_dram = nc.dram_tensor("slots_dram", [ROWS, D], F32, kind="Internal").ap()
        q_dram = nc.dram_tensor("q_dram", [NB, D], F32, kind="Internal").ap()
        own_dram = nc.dram_tensor("own_dram", [NB, 2 * NH], F32, kind="Internal").ap()

        loaded = [sem(f"loaded{s}") for s in range(RING)]
        ld_x = [sem(f"ld_x{t}") for t in range(5)]
        again_x = sem("again_x")
        ld_c, ld_w, ld_pt, ld_bs = sem("ld_c"), sem("ld_w"), sem("ld_pt"), sem("ld_bs")
        (prep_init, prep_tp, prep_v, prep_lam, prep_lame) = sems(
            "prep", "init tp v lam lame")
        zero_set, zeroed = sem("zero_set"), sem("zeroed")
        chain = sem("chain")
        (norm_sq_a, norm_sq_v, norm_var, norm_root, norm_rs, norm_xn, norm_tp, norm_ev) = sems(
            "norm", "sq_a sq_v var root rs xn tp ev")
        (uv_mm, uv_gelu, uv_tp, uv_ev, uv_sq) = sems(
            "uv", "mm gelu tp ev sq")
        (gate_var, gate_root, gate_rs, gate_vn_v, gate_vn_a, gate_vs, gate_vs_out, gate_sp, gate_tmp, gate_u,
         gate_gb, gate_s, gate_tp, gate_su) = sems(
            "gate", "var root rs vn_v vn_a vs vs_out sp tmp u gb s tp su")
        (back_mm, back_cp, back_tp, back_add) = sems(
            "back", "mm cp tp add")
        (moe_lg, moe_rt, moe_ex, moe_mk, moe_cum, moe_idx, moe_scat, moe_ld0, moe_ld1, moe_tp, moe_tev, moe_gu,
         moe_silu, moe_hid, moe_dn, moe_ya, moe_yv, moe_st0, moe_st1, moe_gat0, moe_gat1, moe_gat2, moe_gat3,
         moe_gat4, moe_comb, moe_over) = sems(
            "moe", "lg rt ex mk cum idx scat ld0 ld1 tp tev gu silu hid dn ya yv st0 st1 gat0 gat1 gat2 "
            "gat3 gat4 comb over")
        gathered = [moe_gat0, moe_gat1, moe_gat2, moe_gat3, moe_gat4]
        ovfs = [{k: sem(f"ovf{n}_{k}") for k in "ld tp tev gu silu hid dn y st".split()} for n in range(2)]
        (kvq_mm, kvq_cp, kvq_tp, kvq_ev, kvq_kst0, kvq_kst1, kvq_vst, kvq_qst, kvq_qld0, kvq_qld1) = sems(
            "kvq", "mm cp tp ev kst0 kst1 vst qst qld0 qld1")
        (att_bias, att_qk, att_neg, att_ex, att_a, att_tp, att_aT, att_pv, att_o, att_sq, att_osq, att_var,
         att_root, att_on, att_tp2, att_ev) = sems(
            "att", "bias qk neg ex a tp aT pv o sq osq var root on tp2 ev")
        (dec_prod, dec_red, dec_own, dec_ownw, dec_ownr, dec_tp, dec_max, dec_ex, dec_c, dec_aTp, dec_aT, dec_pv,
         dec_o, dec_otp, dec_sq, dec_root, dec_o2, dec_otp2, dec_ev, dec_vown) = sems(
            "dec", "prod red own ownw ownr tp max ex c aTp aT pv o otp sq root o2 otp2 ev vown")
        fin_y, fin_st, fin_g = sem("fin_y"), sem("fin_st"), sem("fin_g")

        block = ctx.enter_context(nc.Block())
        chained = [0]

        def link(eng, ins):
            ins.then_inc(chain, 1)
            chained[0] += 1
            eng.wait_ge(chain, chained[0])

        def slot_loaded(eng, b, i=0):
            eng.wait_ge(loaded[b % RING], i * 16 + loaded_value(b))

        def ringslot(b, shape):
            return take(ring[:, b % RING, :], 0, shape)

        def rows_of(t):
            return P if t < NT else NB

        def cols_of(t):
            return slice(t * P, t * P + rows_of(t))

        def last_use(b):
            if b < GO0:
                return uv_mm, 2 * (b - UV0) + 2
            if b < MOE0:
                return back_mm, (b - GO0) // 3 + 1
            if KVQ0 <= b < KP0:
                return kvq_mm, 2 * (b - KVQ0) + 2
            if KP0 <= b < VP0:
                return dec_prod, 2 * (b - KP0) + 2
            if VP0 <= b < AO0:
                return dec_pv, (b - VP0) // 2 + 1
            if AO0 <= b < MOE1:
                return back_mm, DC + 2 * (b - AO0) + 2
            r, before = (b - MOE0, 0) if b < KVQ0 else (b - MOE1, NE)
            if r < 2:
                return moe_gu, before + 1
            if r >= 44:
                return ((moe_gu, 16), (moe_gu, 16), (moe_dn, 15), (moe_dn, 16))[r - 44][0], \
                    before + (16, 16, 15, 16)[r - 44]
            q, s = divmod(r - 2, 3)
            return (moe_dn, before + q + 1) if s == 2 else (moe_gu, before + q + 2)

        @block.sync
        def _(sp):
            def free(b, i=0, per_loop=0):
                if b >= RING:
                    used, value = last_use(b - RING)
                    sp.wait_ge(used, i * per_loop + value)

            def load(b, src, shape, i=0, per_loop=0):
                free(b, i, per_loop)
                sp.dma_start(ringslot(b, shape), src).then_inc(loaded[b % RING], 16)

            for t in range(5):
                src = a["x_prompt"][0, t * P:(t + 1) * P, :] if t < NT else a["x_sample"][:, 0, :]
                sp.dma_start(x[0:rows_of(t), t, :], src).then_inc(ld_x[t], 16)
            w_uv = a["w_uv"][0].rearrange("(p c) n -> p c n", c=DC)
            for k in range(RING):
                load(UV0 + k, w_uv[:, :, k * 256:(k + 1) * 256], (DC, 256))
            with sp.Fori(0, 3) as i:
                for k in range(RING):
                    load(UV0 + RING + k, w_uv[:, :, bass.ds(i * (RING * 256) + (RING + k) * 256, 256)],
                         (DC, 256), i, 2 * RING)
            w_go = a["w_gmlp_o"][0].rearrange("(b c p) n -> p b c n", c=DC, p=P)
            for k in range(RING):
                load(GO0 + k, w_go[:, k % 3, :, (k // 3) * P:(k // 3 + 1) * P], (DC, P))
            with sp.Fori(0, 3) as i:
                for k in range(RING):
                    load(GO0 + RING + k, w_go[:, k % 3, :, bass.ds(i * (2 * P) + (2 + k // 3) * P, P)],
                         (DC, P), i, 2)

            def kvq_load(k):
                w = (a["w_k"], a["w_v"], a["w_q"][0])[k // 4].rearrange("(p c) n -> p c n", c=DC)
                load(KVQ0 + k, w[:, :, (k % 4) * 256:(k % 4 + 1) * 256], (DC, 256))

            def experts(base, layer, behind):
                wg = a["w_e_gate"][layer].rearrange("e (p c) f -> e p c f", c=DC)
                wu = a["w_e_up"][layer].rearrange("e (p c) f -> e p c f", c=DC)
                wd = a["w_e_down"][layer].rearrange("e (f p) n -> e p f n", p=P)
                before = NE * layer
                ld, stored = (moe_ld0, moe_ld1), (moe_st0, moe_st1)

                def one(w, e):
                    return w[bass.ds(e, 1)].rearrange("o p c f -> (o p) c f")

                def rows(e):
                    return slots_dram[bass.ds(e * SLOTS, SLOTS), :]

                def load_rows(i, k):
                    if not (isinstance(i, int) and k < 2):
                        sp.wait_ge(moe_tp, i * 2 + (before + k - 1))
                    sp.dma_start(xs[0:SLOTS, k % 2].rearrange("p c f -> p (c f)"), rows(i * 2 + k))\
                        .then_inc(ld[k % 2], 16)

                def store_rows(i, k):
                    sp.wait_ge(moe_ya, i * 2 + (before + k + 1))
                    sp.wait_ge(moe_yv, i * 2 + (before + k + 1))
                    sp.dma_start(rows(i * 2 + k), ye[0:SLOTS, k % 2, :]).then_inc(stored[k % 2], 16)

                load(base, wg[0], (DC, DE))
                load(base + 1, wu[0], (DC, DE))
                for k in range(2):
                    b = base + 2 + 3 * k
                    if k == 0:
                        load(b, wg[1], (DC, DE))
                        load(b + 1, wu[1], (DC, DE))
                        load(b + 2, wd[0], (2, D))
                        sp.wait_ge(moe_scat, 160 * (layer + 1))
                        load_rows(0, 0)
                        load_rows(0, 1)
                    else:
                        load(b, wg[2], (DC, DE))
                        load_rows(0, 2)
                        load(b + 1, wu[2], (DC, DE))
                        load(b + 2, wd[1], (2, D))
                with sp.Fori(0, 6) as i:
                    for k in range(2):
                        b = base + 8 + 3 * k
                        load(b, one(wg, i * 2 + (3 + k)), (DC, DE), i, 2)
                        load_rows(i, 3 + k)
                        load(b + 1, one(wu, i * 2 + (3 + k)), (DC, DE), i, 2)
                        load(b + 2, one(wd, i * 2 + (2 + k)), (2, D), i, 2)
                        store_rows(i, k)
                load(base + 44, wg[15], (DC, DE))
                load_rows(0, 15)
                load(base + 45, wu[15], (DC, DE))
                load(base + 46, wd[14], (2, D))
                store_rows(0, 12)
                load(base + 47, wd[15], (2, D))
                store_rows(0, 13)
                behind(0, 4)
                behind(4, 5)
                store_rows(0, 14)
                behind(5, 6)
                store_rows(0, 15)

            experts(MOE0, 0, lambda lo, hi: [kvq_load(k) for k in range(lo, hi)])
            for k in range(6, 12):
                kvq_load(k)
            sp.wait_ge(ld_pt, 16)
            for first, cache in ((KP0, a["cache_k"].rearrange("g s h m d -> g s (h m d)")),
                                 (VP0, a["cache_v"].rearrange("g s h d -> g s (h d)"))):
                for n in range(NB * PAGES):
                    b = first + n // 2
                    if n % 2 == 0:
                        free(b)
                    page = sp.value_load(pt[0:1, n:n + 1], min_val=0, max_val=cache.shape[0] - 1)
                    sp.dma_start(ringslot(b, (2, D))[:, n % 2, :],
                                 cache[bass.ds(page, 1)].rearrange("o s f -> (o s) f"))\
                        .then_inc(loaded[b % RING], 16)
            w_ao = a["w_attn_o"][0].rearrange("(c p) n -> p c n", p=P)
            for k in range(4):
                load(AO0 + k, w_ao[:, :, k * 256:(k + 1) * 256], (DC, 256))
            experts(MOE1, 1, lambda lo, hi: None)
            for t in range(5):
                dst = out["y_prompt"][0, t * P:(t + 1) * P, :] if t < NT else out["y_sample"][:, 0, :]
                sp.wait_ge(fin_y, t + 1)
                sp.dma_start(dst, xn[0:rows_of(t), t].rearrange("p c f -> p (c f)")).then_inc(fin_st, 16)
            sp.wait_ge(fin_st, 16 * 5)

        @block.gpsimd
        def _(g):
            g.memset(zeros[:, :], 0.0).then_inc(zero_set, 1)
            g.wait_ge(zero_set, 1)
            g.wait_ge(uv_mm, 1)
            for r in range(0, ROWS, P):
                n = min(P, ROWS - r)
                g.dma_start(slots_dram[r:r + n, :], zeros[0:n, :]).then_inc(zeroed, 16)
            g.wait_ge(norm_xn, 5)
            g.dma_start(bsg.rearrange("p g t -> p (g t)"),
                        a["b_sgu"][0].rearrange("(o g) t -> o (g t)", o=1).broadcast_to([P, NG * P]))\
                .then_inc(ld_bs, 16)
            g.wait_ge(uv_mm, 2 * GC)
            g.dma_start(gainb, a["sgu_gain"].broadcast_to([NB, DG])).then_inc(gate_gb, 16)
            g.wait_ge(gate_vs, 1)
            g.dma_start(out["gmlp_v_sample"][0, :, 0, :], VS).then_inc(gate_vs_out, 16)
            for j in range(GC):
                g.wait_ge(gate_tmp, j + 1)
                g.tensor_tensor(u[:, j, 0:SEQ], gtmp[:, j % 2, :], u[:, j, 0:SEQ], ALU.mult)\
                    .then_inc(gate_u, 1)
            g.wait_ge(gate_vs_out, 16)
            g.wait_ge(gate_s, 1)
            g.wait_ge(gate_u, GC)
            for t in range(5):
                src = a["x_prompt"][0, t * P:(t + 1) * P, :] if t < NT else a["x_sample"][:, 0, :]
                g.dma_start(x[0:rows_of(t), t, :], src).then_inc(again_x, 16)

            def moe_rows(layer):
                before = layer * NE
                g.wait_ge(moe_idx, layer + 1)
                for t in range(5):
                    for j in range(TOPK):
                        g.indirect_dma_start(
                            slots_dram, bass.IndirectOffsetOnAxis(
                                ap=slot_i[0:rows_of(t), 2 * t + j:2 * t + j + 1], axis=0),
                            xn[0:rows_of(t), t].rearrange("p c f -> p (c f)"), None).then_inc(moe_scat, 16)
                g.wait_ge(moe_st0, 16 * (before + NE) // 2)
                g.wait_ge(moe_st1, 16 * (before + NE) // 2)
                g.wait_ge(moe_over, layer + 1)
                if layer == 1:
                    g.dma_start(gfin, a["norm_final"].rearrange("(o n) -> o n", o=1).broadcast_to([P, D]))\
                        .then_inc(fin_g, 16)
                for t in range(5):
                    for j in range(TOPK):
                        g.indirect_dma_start(
                            yg[0:rows_of(t), t, j, :], None, slots_dram, bass.IndirectOffsetOnAxis(
                                ap=slot_i[0:rows_of(t), 2 * t + j:2 * t + j + 1], axis=0))\
                            .then_inc(gathered[t], 16)

            moe_rows(0)
            kout = out["k_prompt"].rearrange("b g s h m d -> (b g) s (h m d)")
            vout = out["v_prompt"].rearrange("b g s h d -> (b g) s (h d)")
            kst = (kvq_kst0, kvq_kst1)
            for n in range(DC):
                g.wait_ge(kvq_ev, n + 1)
                g.dma_start(kout[:, :, n * P:(n + 1) * P].rearrange("g s f -> s g f"),
                            ktok[:, n % 2].rearrange("p (t f) -> p t f", t=NT)).then_inc(kst[n % 2], 16)
            g.wait_ge(kvq_ev, 2 * DC)
            for t in range(NT):
                g.dma_start(vout[t], vtok[:, t, :]).then_inc(kvq_vst, 16)
            g.wait_ge(kvq_ev, 3 * DC)
            g.dma_start(q_dram, tok8[:, 2, :]).then_inc(kvq_qst, 16)
            g.dma_start(out["k_sample"].rearrange("b o h m d -> (b o) (h m d)"), tok8[:, 0, :])\
                .then_inc(kvq_vst, 16)
            g.dma_start(out["v_sample"].rearrange("b o h d -> (b o) (h d)"), tok8[:, 1, :])\
                .then_inc(kvq_vst, 16)
            g.wait_ge(kvq_qst, 16)
            g.wait_ge(kvq_vst, 16 * (NT + 2))
            g.wait_ge(kvq_kst0, 16 * DC // 2)
            g.wait_ge(kvq_kst1, 16 * DC // 2)
            g.wait_ge(dec_own, 1)
            g.dma_start(own_dram, down_).then_inc(dec_ownw, 16)
            qld = (kvq_qld0, kvq_qld1)

            def load_q(b):
                if b >= 2:
                    g.wait_ge(dec_prod, PAGES * (b - 1))
                g.dma_start(qbc[:, b % 2, :], q_dram[b:b + 1, :].broadcast_to([P, D])).then_inc(qld[b % 2], 16)

            load_q(0)
            load_q(1)
            for n in range(NB * PAGES):
                b, page = divmod(n, PAGES)
                if page == 0:
                    g.wait_ge(qld[b % 2], 16 * (b // 2 + 1))
                slot_loaded(g, KP0 + n // 2)
                if n >= 2:
                    g.wait_ge(dec_red, n - 1)
                g.tensor_tensor(prod[:, n % 2, :], ringslot(KP0 + n // 2, (2, D))[:, n % 2, :],
                                qbc[:, b % 2, :], ALU.mult).then_inc(dec_prod, 1)
                if page == PAGES - 1 and b + 2 < NB:
                    load_q(b + 2)
            g.wait_ge(dec_ownw, 16)
            g.dma_start(downc, own_dram.rearrange("b (h o) -> (b h) o", o=1)).then_inc(dec_ownr, 16)
            g.wait_ge(att_ev, 8)
            g.dma_start(dvown, out["v_sample"].rearrange("b o h d -> (b o h) d")).then_inc(dec_vown, 16)
            moe_rows(1)

        @block.scalar
        def _(s):
            s.dma_start(K[:, :], a["geometry"]).then_inc(ld_c, 16)
            mats = [(gains[:, 0:2, :], a["norm_mix"].rearrange("l (p c) -> p l c", c=DC)),
                    (gains[:, 2:4, :], a["norm_ffn"].rearrange("l (p c) -> p l c", c=DC)),
                    (gains[:, 4, :], a["norm_kv"].rearrange("(p c) -> p c", c=DC)),
                    (sg_st, a["sgu_gain"].rearrange("o (j p) -> (o j) p", p=P)),
                    (w_st, a["w_sgu"][0].rearrange("g t s -> t g s")),
                    (wrg_st, a["w_router_group"].rearrange("l (p c) g -> p l (c g)", c=DC)),
                    (wre_st[:, 0], a["w_router_expert"][0].rearrange("g (p c) e -> p g (c e)", c=DC)),
                    (wre_st[:, 1], a["w_router_expert"][1].rearrange("g (p c) e -> p g (c e)", c=DC)),
                    (rbias[:, :, 0:NEG], bcast_rows(a["b_router_group"], "l g -> (l g)", P, 2)),
                    (rbias[:, :, NEG:20], bcast_rows(a["b_router_expert"], "l g e -> (l g e)", P, 2)),
                    (w00[:, 0, :], a["w_sgu"][0, :, 0, 0:1].rearrange("g o -> o g").broadcast_to([NB, NG])),
                    (w00[:, 1, :], a["b_sgu"][0, :, 0:1].rearrange("g o -> o g").broadcast_to([NB, NG])),
                    (lam_st[:, 0, :], a["lam_q"][0].rearrange("(o m) d -> o (m d)", o=1).broadcast_to([P, 2 * HD])),
                    (lam_st[:, 1, :], a["lam_k"][0].rearrange("(o m) d -> o (m d)", o=1).broadcast_to([P, 2 * HD])),
                    (subg[:, :], a["subln_gain"].rearrange("o p -> p o"))]
            for dst, src in mats:
                s.dma_start(dst, src, allow_slow_non_contiguous=True).then_inc(ld_w, 16)
            assert len(mats) == N_SMALL
            s.dma_start(pt[:, :], a["page_table"].rearrange("(o b) p -> o (b p)", o=1)).then_inc(ld_pt, 16)

            def norm_a(n, ready, normed=True):
                for t in (0, 2, 4):
                    ready(s, t)
                    r = rows_of(t)
                    s.activation(xn[0:r, t].rearrange("p c f -> p (c f)"), x[0:r, t, :], ACT.Square,
                                 accum_out=ss[0:r, t:t + 1]).then_inc(norm_sq_a, 1)
                s.wait_ge(norm_var, n + 1)
                s.activation(root[:, 0:5], ss[:, :], ACT.Sqrt).then_inc(norm_root, 1)
                if normed:
                    s.wait_ge(norm_rs, n + 1)
                    for t in range(5):
                        r = rows_of(t)
                        s.activation(xn[0:r, t], x[0:r, t, :].rearrange("p (f c) -> p c f", c=DC), ACT.Copy,
                                     scale=rstd[0:r, t:t + 1]).then_inc(norm_xn, 1)

            s.wait_ge(prep_init, 1)
            norm_a(0, lambda e, t: e.wait_ge(ld_x[t], 16))
            s.wait_ge(prep_lam, 1)
            s.activation(lam_s[:, 2:4], lam_s[:, 0:2], ACT.Exp).then_inc(prep_lame, 1)

            for part in range(2):
                with s.Fori(0, 2) as i:
                    def squares(c):
                        s.wait_ge(uv_ev, i * 12 + (c + 1))
                        s.wait_ge(uv_sq, i * 12 + c)
                        for t in range(5):
                            r = rows_of(t)
                            src = v[:, t, bass.ds(i * (12 * P) + c * P, P)] if t < NT else \
                                VS[:, bass.ds(i * (12 * P) + c * P, P)]
                            ins = s.activation(gtmp[0:r, t % 2, (t // 2) * P:(t // 2 + 1) * P],
                                               src, ACT.Square,
                                               accum_out=vss[0:r, t, bass.ds(i * 12 + c, 1)])
                        ins.then_inc(uv_sq, 1)

                    for c in range(12):
                        s.wait_ge(uv_mm, i * 12 + (24 * part + c + 1))
                        if part == 1:
                            s.wait_ge(uv_tp, i * 12 + max(c - 1, 0))
                        bank = 2 * (c % 2)
                        dst = vtmp[:, c % 2, :] if part else u[:, bass.ds(i * 12 + c, 1), :]\
                            .rearrange("p o t -> p (o t)")
                        s.activation(dst.rearrange("p (h t) -> p h t", h=2), ps[:, bank:bank + 2, 0:HALF],
                                     ACT.Gelu_apprx_tanh).then_inc(uv_gelu, 1)
                        if part == 1 and c >= 1:
                            squares(c - 1)
                    if part == 1:
                        squares(11)
            s.wait_ge(gate_var, 1)
            s.activation(root[:, 0:5], ss[:, :], ACT.Sqrt).then_inc(gate_root, 1)
            s.wait_ge(gate_rs, 1)
            for t in (1, 3):
                s.activation(v[:, t, :], v[:, t, :], ACT.Copy, scale=rstd[:, t:t + 1]).then_inc(gate_vn_a, 1)
            with s.Fori(0, 4) as i:
                for k in range(2):
                    s.wait_ge(back_mm, i * 2 + (k + 1))
                    s.wait_ge(back_tp, i * 2)
                    s.activation(vtmp[:, k, :].rearrange("p (h t) -> p h t", h=2),
                                 ps[:, 2 * k:2 * k + 2, 0:HALF], ACT.Copy).then_inc(back_cp, 1)

            def moe_a(layer):
                o, before = ovfs[layer], layer * NE
                s.wait_ge(moe_rt, 2 * layer + 1)
                s.activation(R["eg"], R["eg"], ACT.Exp).then_inc(moe_ex, 1)
                s.wait_ge(moe_rt, 2 * layer + 2)
                s.activation(R["e2"], R["e2"], ACT.Exp).then_inc(moe_ex, 1)

                def silu(i, k):
                    s.wait_ge(moe_gu, i * 2 + (before + k + 1))
                    s.activation(sg[:, k % 2].rearrange("p f s -> p (f s)"), ps[:, 2 + k % 2, 0:2 * SLOTS], ACT.Silu)\
                        .then_inc(moe_silu, 1)

                def y_half(i, k):
                    s.wait_ge(moe_dn, i * 2 + (before + k + 1))
                    s.wait_ge((moe_st0, moe_st1)[k % 2], i * 16 + (8 * before + k // 2 * 16))
                    s.activation(ye[0:SLOTS, k % 2, 0:512], ps[0:SLOTS, 4 + 2 * (k % 2), :], ACT.Copy)\
                        .then_inc(moe_ya, 1)

                silu(0, 0)
                for k in (1, 2):
                    silu(0, k)
                    y_half(0, k - 1)
                with s.Fori(0, 6) as i:
                    for k in range(2):
                        silu(i, 3 + k)
                        y_half(i, 2 + k)
                silu(0, 15)
                y_half(0, 14)
                y_half(0, 15)
                n_ovf = s.value_load(ovf_i[0:1, 0:1], min_val=0, max_val=OVF)
                with s.If(n_ovf > 0):
                    wg = a["w_e_gate"][layer].rearrange("e (p c) f -> e p (c f)", c=DC)
                    wu = a["w_e_up"][layer].rearrange("e (p c) f -> e p (c f)", c=DC)
                    wd = a["w_e_down"][layer].rearrange("e (f p) n -> e p f n", p=P)
                    s.wait_ge(moe_st0, 16 * (before + NE) // 2)
                    with s.Fori(0, OVF) as t:
                        e = s.value_load(ovf_i[0:1, bass.ds(t + 1, 1)], min_val=0, max_val=NE - 1)
                        s.dma_start(ow[:, 0, :], wg[bass.ds(e, 1)].rearrange("o p f -> (o p) f")).then_inc(o["ld"], 16)
                        s.dma_start(ow[:, 1, :], wu[bass.ds(e, 1)].rearrange("o p f -> (o p) f")).then_inc(o["ld"], 16)
                        s.dma_start(ow[:, 2, :].rearrange("p (f n) -> p f n", f=2),
                                    wd[bass.ds(e, 1)].rearrange("o p f n -> (o p) f n")).then_inc(o["ld"], 16)
                        here = slots_dram[bass.ds(t * SLOTS + NE * SLOTS, SLOTS), :]
                        s.dma_start(xs[0:SLOTS, 0].rearrange("p c f -> p (c f)"), here).then_inc(o["ld"], 16)
                        s.wait_ge(o["gu"], t + 1)
                        s.activation(sg[:, 0].rearrange("p f s -> p (f s)"), ps[:, 2, 0:2 * SLOTS], ACT.Silu)\
                            .then_inc(o["silu"], 1)
                        s.wait_ge(o["dn"], t + 1)
                        s.activation(ye[0:SLOTS, 0, 0:512], ps[0:SLOTS, 4, :], ACT.Copy).then_inc(o["y"], 1)
                        s.wait_ge(o["y"], t * 2 + 2)
                        s.dma_start(here, ye[0:SLOTS, 0, :]).then_inc(o["st"], 16)
                        s.wait_ge(o["st"], t * 16 + 16)
                s.sem_inc(moe_over, 1)

            norm_a(1, lambda e, t: e.wait_ge(back_add, DC) if t == 0 else None)
            moe_a(0)
            norm_a(2, lambda e, t: e.wait_ge(moe_comb, t + 1))
            for n in range(3 * DC):
                kind, h = divmod(n, DC)
                s.wait_ge(kvq_mm, n + 1)
                if kind == 1 and n >= DC + 2:
                    s.wait_ge(kvq_tp, n - 1)
                dst = (kT[:, h, :], vtmp[:, n % 2, :], qT[:, h, :])[kind]
                bank = 2 * (n % 2)
                s.activation(dst.rearrange("p (h t) -> p h t", h=2), ps[:, bank:bank + 2, 0:HALF], ACT.Copy)\
                    .then_inc(kvq_cp, 1)
            def make_bias(h):
                if h >= 2:
                    s.wait_ge(att_neg, 4 * (h - 1))
                s.activation(bias8[:, h % 2, :], c_["dist"], ACT.Copy, scale=-8.0 * 2.0 ** -(h + 1))\
                    .then_inc(att_bias, 1)

            make_bias(0)
            steps = NH * NT
            for k in range(steps + 2):
                if k < steps:
                    h, q = divmod(k, NT)
                    w = (q + 1) * P
                    if q == 1 and h + 1 < NH:
                        make_bias(h + 1)
                    s.wait_ge(att_neg, k + 1)
                    for mp in range(2):
                        ins = s.activation(st[:, k % 2, mp * SEQ:mp * SEQ + w], st[:, k % 2, mp * SEQ:mp * SEQ + w],
                                           ACT.Exp, bias=nm[:, k % 2, mp:mp + 1],
                                           accum_out=zz[:, k % 2, mp:mp + 1])
                    ins.then_inc(att_ex, 1)
                if 1 <= k <= steps:
                    n = k - 1
                    w = (n % NT + 1) * P
                    s.wait_ge(att_tp, n + 1)
                    if n >= 2:
                        s.wait_ge(att_pv, n - 1)
                    s.activation(aT[:, n % 2, 0:w], ps[:, 4 + n % 2, 0:w], ACT.Copy).then_inc(att_aT, 1)
                if k >= 2:
                    n = k - 2
                    h, q = divmod(n, NT)
                    s.wait_ge(att_pv, n + 1)
                    s.activation(otok[:, q, h * P:(h + 1) * P], ps[:, 6 + n % 2, 0:P], ACT.Copy)\
                        .then_inc(att_o, 1)
            s.wait_ge(att_o, steps)
            for t in range(NT):
                if t >= 2:
                    s.wait_ge(att_osq, t - 1)
                else:
                    s.wait_ge(att_tp, steps)
                s.activation(st[:, t % 2, :], otok[:, t, :], ACT.Square).then_inc(att_sq, 1)
            s.wait_ge(att_var, 1)
            s.activation(root[:, 0:NT * NH], oss.rearrange("p t h -> p (t h)"), ACT.Sqrt).then_inc(att_root, 1)
            for t in range(NT):
                for half in range(2):
                    s.wait_ge(att_tp2, 2 * t + half + 1)
                    s.activation(oT[:, 4 * half:4 * half + 4, t * P:(t + 1) * P],
                                 ps[:, 4 + (2 * t + half) % 4, :].rearrange("p (c f) -> p c f", c=4), ACT.Copy,
                                 scale=subg[:, 0:1]).then_inc(att_ev, 1)
            s.wait_ge(dec_max, 1)
            s.activation(dS, dS, ACT.Exp, bias=dsm[:, 2:3], accum_out=dsm[:, 3:4]).then_inc(dec_ex, 1)
            s.wait_ge(dec_aTp, 1)
            s.activation(daT.rearrange("p g c -> p (g c)"), ps[:, 1, 0:PAGES * NB * NH], ACT.Copy)
            s.activation(daown, ps[0:NB * NH, 2, 0:1], ACT.Copy).then_inc(dec_aT, 1)
            s.wait_ge(dec_pv, NB)
            s.activation(doT, ps[:, 3, 0:NB * NH], ACT.Copy).then_inc(dec_o, 1)
            s.wait_ge(dec_sq, 1)
            s.activation(dsm[0:64, 9:10], dsm[0:64, 8:9], ACT.Sqrt).then_inc(dec_root, 1)
            s.wait_ge(dec_otp2, 1)
            s.activation(oT[:, :, SEQ:T], ps[:, 1, 0:NB * NH].rearrange("p (b h) -> p h b", b=NB), ACT.Copy,
                         scale=subg[:, 0:1]).then_inc(dec_ev, 1)
            for n in range(DC):
                s.wait_ge(back_mm, DC + n + 1)
                if n >= 2:
                    s.wait_ge(back_tp, DC + n - 1)
                s.activation(vtmp[:, n % 2, :].rearrange("p (h t) -> p h t", h=2),
                             ps[:, 2 * (n % 2):2 * (n % 2) + 2, 0:HALF], ACT.Copy).then_inc(back_cp, 1)
            norm_a(3, lambda e, t: e.wait_ge(back_add, 2 * DC) if t == 0 else None)
            moe_a(1)
            norm_a(4, lambda e, t: e.wait_ge(moe_comb, 5 + t + 1), normed=False)

        @block.tensor
        def _(pe):
            def product(pair, w, c0, rhs, done=None, first=True, last=True):
                for c in range(DC):
                    for half in range(2):
                        ins = pe.matmul(ps[:, 2 * pair + half, 0:HALF], w[:, c, c0:c0 + P],
                                        rhs(c, half), start=first and c == 0, stop=last and c == DC - 1)
                if done is not None:
                    ins.then_inc(done, 1)

            def of(t):
                return lambda c, half: t[:, c, half * HALF:(half + 1) * HALF]

            def turn(src, bank, sbank, prompt=True):
                if prompt:
                    for t in range(NT):
                        pe.transpose(ps[:, bank, t * P:(t + 1) * P], src[:, t * P:(t + 1) * P], ident)
                return pe.transpose(ps[0:NB, sbank, 0:P], src[:, SEQ:T], ident)

            def norm_t(n, evs, passes=1):
                for t in range(5):
                    pe.wait_ge(norm_xn, 5 * n + t + 1)
                    r = rows_of(t)
                    if t == NT:
                        for c in range(DC):
                            ins = pe.transpose(ps[:, 4, c * NB:(c + 1) * NB], xn[0:r, t, c, :], ident[0:r, 0:r])
                        ins.then_inc(norm_tp, 1)
                        continue
                    for half in range(2):
                        if t >= 2:
                            pe.wait_ge(norm_ev, evs + passes * (2 * (t - 2) + half + 1))
                        for c in range(4):
                            ins = pe.transpose(ps[:, 2 * (t % 2) + half, c * P:(c + 1) * P],
                                               xn[:, t, 4 * half + c, :], ident)
                        ins.then_inc(norm_tp, 1)

            pe.wait_ge(ld_c, 16)
            pe.wait_ge(ld_w, 16 * N_SMALL)
            for g in range(NG):
                ins = pe.transpose(ps[:, 5 + g // 4, (g % 4) * P:(g % 4 + 1) * P], w_st[:, g, :], ident)
            ins = pe.transpose(ps[:, 7, 0:GC], sg_st, ident[0:GC, 0:GC])
            ins.then_inc(prep_tp, 1)
            norm_t(0, 0)
            pe.wait_ge(norm_ev, 9)
            pe.wait_ge(prep_v, 1)
            for part in range(2):
                with pe.Fori(0, 2) as i:
                    def turn_v(c):
                        pe.wait_ge(uv_gelu, i * 12 + (24 + c + 1))
                        pe.wait_ge(uv_ev, i * 12 + max(c - 1, 0))
                        turn(vtmp[:, c % 2, :], 4 + c % 2, 6 + c % 2).then_inc(uv_tp, 1)

                    for c in range(12):
                        b = UV0 + 12 * part + c // 2
                        if c % 2 == 0:
                            slot_loaded(pe, b, i)
                        if part == 0:
                            pe.wait_ge(uv_gelu, i * 12 + max(c - 1, 0))
                        else:
                            pe.wait_ge(uv_gelu, i * 12 + (24 + c - 1))
                        product(c % 2, ringslot(b, (DC, 256)), (c % 2) * P, of(hT), uv_mm)
                        if part == 1 and c >= 1:
                            turn_v(c - 1)
                    if part == 1:
                        turn_v(11)
            pe.wait_ge(gate_vn_v, 2)
            pe.wait_ge(gate_vn_a, 2)
            for j in range(GC):
                if j >= 4:
                    pe.wait_ge(gate_tmp, j - 3)
                for t in range(NT):
                    ins = pe.matmul(ps[:, j % 4, t * P:(t + 1) * P], v[:, t, j * P:(j + 1) * P],
                                    wT[:, j * P // GCOLS, :], start=True, stop=True)
                ins.then_inc(gate_sp, 1)
                if j == 3:
                    pe.wait_ge(gate_s, 1)
                    for k in range(GC):
                        ins = pe.transpose(ps[:, 4, k * NB:(k + 1) * NB], gainb[:, k * P:(k + 1) * P],
                                           ident[0:NB, 0:NB])
                    ins.then_inc(gate_tp, 1)
            pe.wait_ge(gate_u, GC)
            pe.wait_ge(gate_su, 1)
            with pe.Fori(0, 4) as i:
                for k in range(2):
                    pe.wait_ge(back_cp, i * 2)
                    for kb in range(3):
                        b = GO0 + 3 * k + kb
                        slot_loaded(pe, b, i)
                        product(k, ringslot(b, (DC, P)), 0,
                                lambda c, half: u[:, 8 * kb + c, half * HALF:(half + 1) * HALF],
                                back_mm if kb == 2 else None, kb == 0, kb == 2)
                for k in range(2):
                    pe.wait_ge(back_cp, i * 2 + (k + 1))
                    pe.wait_ge(back_add, i * 2)
                    turn(vtmp[:, k, :], 4 + k, 6 + k).then_inc(back_tp, 1)

            def moe_t(layer):
                o, before = ovfs[layer], layer * NE
                for t in range(5):
                    for c in range(DC):
                        ins = pe.matmul(ps[0:rows_of(t), 5, t * 20:(t + 1) * 20], hT[:, c, cols_of(t)],
                                        wr[:, layer, c, :], start=c == 0, stop=c == DC - 1)
                ins.then_inc(moe_lg, 1)
                pe.wait_ge(moe_mk, layer + 1)
                for t in range(5):
                    for q in range(t + 1):
                        pe.matmul(ps[:, 6, t * NE:(t + 1) * NE], c_["tri"] if q == t else ones,
                                  R["m"][:, q, :], start=q == 0, stop=q == t)
                for q in range(5):
                    ins = pe.matmul(ps[:, 6, 5 * NE:6 * NE], ones, R["m"][:, q, :], start=q == 0, stop=q == 4)
                ins.then_inc(moe_cum, 1)

                def turn_rows(i, k):
                    pe.wait_ge((moe_ld0, moe_ld1)[k % 2], i * 16 + (8 * before + k // 2 * 16 + 16))
                    if not (isinstance(i, int) and k == 0):
                        pe.wait_ge(moe_tev, i * 2 + (before + k))
                    for c in range(DC):
                        ins = pe.transpose(ps[:, c // 4, (c % 4) * SLOTS:(c % 4 + 1) * SLOTS],
                                           xs[0:SLOTS, k % 2, c, :], ident[0:SLOTS, 0:SLOTS])
                    ins.then_inc(moe_tp, 1)

                def gate_up(i, k, b):
                    q = k % 2
                    slot_loaded(pe, b, i)
                    slot_loaded(pe, b + 1, i)
                    pe.wait_ge(moe_tev, i * 2 + (before + k + 1))
                    if k >= 1:
                        pe.wait_ge(moe_hid, i * 2 + (before + k - 1))
                    for f in range(4):
                        w = ringslot(b + f // 2, (DC, DE))
                        for c in range(DC):
                            ins = pe.matmul(ps[:, 2 + q, f * SLOTS:(f + 1) * SLOTS],
                                            w[:, c, (f % 2) * P:(f % 2 + 1) * P], xsT[:, q, c, :],
                                            start=c == 0, stop=c == DC - 1)
                    ins.then_inc(moe_gu, 1)

                def down(i, k, b):
                    q = k % 2
                    slot_loaded(pe, b, i)
                    pe.wait_ge(moe_hid, i * 2 + (before + k + 1))
                    if isinstance(i, int) and k >= 2:
                        pe.wait_ge(moe_ya, before + k - 1)
                        pe.wait_ge(moe_yv, before + k - 1)
                    if not isinstance(i, int):
                        pe.wait_ge(moe_ya, i * 2 + (before + max(k - 1, 0)))
                        pe.wait_ge(moe_yv, i * 2 + (before + max(k - 1, 0)))
                    w = ringslot(b, (2, D))
                    for half in range(2):
                        for f in range(2):
                            ins = pe.matmul(ps[0:SLOTS, 4 + 2 * q + half, :], hid[:, q, f, :],
                                            w[:, f, half * 512:(half + 1) * 512], start=f == 0, stop=f == 1)
                    ins.then_inc(moe_dn, 1)

                base = MOE0 if layer == 0 else MOE1
                turn_rows(0, 0)
                gate_up(0, 0, base)
                turn_rows(0, 1)
                pe.wait_ge(moe_idx, layer + 1)
                gate_up(0, 1, base + 2)
                down(0, 0, base + 4)
                turn_rows(0, 2)
                gate_up(0, 2, base + 5)
                down(0, 1, base + 7)
                turn_rows(0, 3)
                with pe.Fori(0, 6) as i:
                    for k in range(2):
                        b = base + 8 + 3 * k
                        gate_up(i, 3 + k, b)
                        down(i, 2 + k, b + 2)
                        turn_rows(i, 4 + k)
                gate_up(0, 15, base + 44)
                down(0, 14, base + 46)
                down(0, 15, base + 47)
                n_ovf = pe.value_load(ovf_i[0:1, 0:1], min_val=0, max_val=OVF)
                with pe.If(n_ovf > 0):
                    with pe.Fori(0, OVF) as t:
                        pe.wait_ge(o["ld"], t * 64 + 64)
                        for c in range(DC):
                            ins = pe.transpose(ps[:, c // 4, (c % 4) * SLOTS:(c % 4 + 1) * SLOTS],
                                               xs[0:SLOTS, 0, c, :], ident[0:SLOTS, 0:SLOTS])
                        ins.then_inc(o["tp"], 1)
                        pe.wait_ge(o["tev"], t + 1)
                        for f in range(4):
                            w = ow[:, f // 2, :].rearrange("p (c n) -> p c n", c=DC)
                            for c in range(DC):
                                ins = pe.matmul(ps[:, 2, f * SLOTS:(f + 1) * SLOTS],
                                                w[:, c, (f % 2) * P:(f % 2 + 1) * P], xsT[:, 0, c, :],
                                                start=c == 0, stop=c == DC - 1)
                        ins.then_inc(o["gu"], 1)
                        pe.wait_ge(o["hid"], t + 1)
                        w = ow[:, 2, :].rearrange("p (f n) -> p f n", f=2)
                        for half in range(2):
                            for f in range(2):
                                ins = pe.matmul(ps[0:SLOTS, 4 + half, :], hid[:, 0, f, :],
                                                w[:, f, half * 512:(half + 1) * 512], start=f == 0, stop=f == 1)
                        ins.then_inc(o["dn"], 1)

            norm_t(1, 9)
            pe.wait_ge(norm_ev, 18)
            moe_t(0)
            norm_t(2, 18, 2)
            pe.wait_ge(norm_ev, 18 + 18)

            def turn_kvq(n):
                kind, h = divmod(n, DC)
                pe.wait_ge(kvq_cp, n + 1)
                if n >= 2:
                    pe.wait_ge(kvq_ev, n - 1)
                src = (kT[:, h, :], vtmp[:, n % 2, :], qT[:, h, :])[kind]
                turn(src, 4 + n % 2, 6 + n % 2, kind < 2).then_inc(kvq_tp, 1)

            for n in range(3 * DC):
                if n % 2 == 0:
                    slot_loaded(pe, KVQ0 + n // 2)
                if n >= 2:
                    pe.wait_ge(kvq_cp, n - 1)
                product(n % 2, ringslot(KVQ0 + n // 2, (DC, 256)), (n % 2) * P,
                        of(hT if n < 2 * DC else hqT), kvq_mm)
                if n >= 1:
                    turn_kvq(n - 1)
            turn_kvq(3 * DC - 1)
            pe.wait_ge(kvq_cp, 3 * DC)
            pe.wait_ge(kvq_ev, 3 * DC)
            steps = NH * NT
            for k in range(steps + 2):
                if k < steps:
                    h, q = divmod(k, NT)
                    if k >= 2:
                        pe.wait_ge(att_neg, k - 1)
                    for mp in range(2):
                        ins = pe.matmul(ps[:, 2 * (k % 2) + mp, 0:(q + 1) * P],
                                        qT[mp * HD:(mp + 1) * HD, h, q * P:(q + 1) * P],
                                        kT[mp * HD:(mp + 1) * HD, h, 0:(q + 1) * P], start=True, stop=True)
                    ins.then_inc(att_qk, 1)
                if 1 <= k <= steps:
                    n = k - 1
                    pe.wait_ge(att_a, n + 1)
                    if n >= 2:
                        pe.wait_ge(att_aT, n - 1)
                    for c in range(n % NT + 1):
                        ins = pe.transpose(ps[:, 4 + n % 2, c * P:(c + 1) * P], st[:, n % 2, c * P:(c + 1) * P],
                                           ident)
                    ins.then_inc(att_tp, 1)
                if k >= 2:
                    n = k - 2
                    h, q = divmod(n, NT)
                    pe.wait_ge(att_aT, n + 1)
                    if n >= 2:
                        pe.wait_ge(att_o, n - 1)
                    for c in range(q + 1):
                        ins = pe.matmul(ps[:, 6 + n % 2, 0:P], aT[:, n % 2, c * P:(c + 1) * P],
                                        vtok[:, c, h * P:(h + 1) * P], start=c == 0, stop=c == q)
                    ins.then_inc(att_pv, 1)
            pe.wait_ge(att_neg, steps)
            pe.wait_ge(dec_red, NB * PAGES)
            for c in range(PAGES):
                ins = pe.transpose(ps[:, 0, c * P:(c + 1) * P], sK[:, c, :], ident)
            ins.then_inc(dec_tp, 1)
            pe.wait_ge(att_o, steps)
            for t in range(NT):
                pe.wait_ge(att_on, t + 1)
                for half in range(2):
                    if t >= 2:
                        pe.wait_ge(att_ev, 2 * (t - 2) + half + 1)
                    for c in range(4):
                        ins = pe.transpose(ps[:, 4 + (2 * t + half) % 4, c * P:(c + 1) * P],
                                           otok[:, t, (4 * half + c) * P:(4 * half + c + 1) * P], ident)
                    ins.then_inc(att_tp2, 1)
            pe.wait_ge(dec_c, 1)
            for c in range(PAGES):
                pe.matmul(ps[:, 1, c * 64:(c + 1) * 64], dS[:, c * P:(c + 1) * P], dC, start=True, stop=True)
            pe.matmul(ps[0:64, 2, 0:1], dC, dS[:, SEQ:SEQ + 1], start=True, stop=True).then_inc(dec_aTp, 1)
            pe.wait_ge(dec_aT, 1)
            for b in range(NB):
                slot_loaded(pe, VP0 + 2 * b)
                slot_loaded(pe, VP0 + 2 * b + 1)
                for h in range(NH):
                    for c in range(PAGES):
                        ins = pe.matmul(ps[:, 3, b * NH + h:b * NH + h + 1],
                                        ringslot(VP0 + 2 * b + c // 2, (2, D))[:, c % 2, h * P:(h + 1) * P],
                                        daT[:, c, b * NH + h:b * NH + h + 1], start=c == 0, stop=c == PAGES - 1)
                ins.then_inc(dec_pv, 1)
            pe.wait_ge(dec_o, 1)
            pe.transpose(ps[0:64, 2, 0:P], doT, ident).then_inc(dec_otp, 1)
            pe.wait_ge(dec_o2, 1)
            pe.transpose(ps[:, 1, 0:64], do64, ident[0:64, 0:64]).then_inc(dec_otp2, 1)
            pe.wait_ge(dec_ev, 1)
            pe.wait_ge(att_ev, 2 * NT)

            def turn_back(n):
                pe.wait_ge(back_cp, DC + n + 1)
                if n >= 2:
                    pe.wait_ge(back_add, DC + n - 1)
                turn(vtmp[:, n % 2, :], 4 + n % 2, 6 + n % 2).then_inc(back_tp, 1)

            for n in range(DC):
                if n % 2 == 0:
                    slot_loaded(pe, AO0 + n // 2)
                if n >= 2:
                    pe.wait_ge(back_cp, DC + n - 1)
                product(n % 2, ringslot(AO0 + n // 2, (DC, 256)), (n % 2) * P, of(oT), back_mm)
                if n >= 1:
                    turn_back(n - 1)
            turn_back(DC - 1)
            norm_t(3, 36)
            pe.wait_ge(norm_ev, 45)
            moe_t(1)

        @block.vector
        def _(e):
            def norm_v(n, ready, gain, into, normed=True):
                for t in (1, 3):
                    ready(e, t)
                    e.tensor_tensor_reduce(xn[:, t].rearrange("p c f -> p (c f)"), x[:, t, :], x[:, t, :], 1.0, 0.0,
                                           ALU.mult, ALU.add, ss[:, t:t + 1]).then_inc(norm_sq_v, 1)
                e.wait_ge(norm_sq_a, 3 * n + 3)
                e.wait_ge(norm_sq_v, 2 * n + 2)
                e.tensor_scalar(ss[:, :], ss[:, :], 1.0 / D, EPS, ALU.mult, ALU.add).then_inc(norm_var, 1)
                e.wait_ge(norm_root, n + 1)
                e.reciprocal(rstd[:, :], root[:, 0:5]).then_inc(norm_rs, 1)
                if not normed:
                    return
                before = (0, 9, 18, 27)[n]
                for t in range(5):
                    for half in range(2 if t < NT else 1):
                        e.wait_ge(norm_tp, before + 2 * t + half + 1)
                        for g_row, dst in zip(gain, into):
                            if t < NT:
                                src = ps[:, 2 * (t % 2) + half, :].rearrange("p (c f) -> p c f", c=4)
                                to = dst[:, 4 * half:4 * half + 4, t * P:(t + 1) * P]
                                gb = gains[:, g_row, 4 * half:4 * half + 4].unsqueeze(2).broadcast_to([P, 4, P])
                            else:
                                src = ps[:, 4, 0:DC * NB].rearrange("p (c f) -> p c f", c=DC)
                                to = dst[:, :, SEQ:T]
                                gb = gains[:, g_row, :].unsqueeze(2).broadcast_to([P, DC, NB])
                            e.tensor_tensor(to, src, gb, ALU.mult).then_inc(norm_ev, 1)

            e.memset(ss[:, :], 1.0)
            e.memset(vss[:, :, :], 0.0).then_inc(prep_init, 1)
            e.wait_ge(prep_init, 1)
            norm_v(0, lambda q, t: (q.wait_ge(ld_x[t], 16), q.wait_ge(ld_w, 16 * N_SMALL)), [0], [hT])
            e.wait_ge(ld_c, 16)
            e.wait_ge(prep_tp, 1)
            for half in range(2):
                e.tensor_tensor(wT[:, 4 * half:4 * half + 4, :],
                                ps[:, 5 + half, :].rearrange("p (g t) -> p g t", g=4),
                                c_["causal"].unsqueeze(1).broadcast_to([P, 4, P]), ALU.mult)
            e.tensor_copy(sgain[:, :], ps[:, 7, 0:GC])
            for layer in range(2):
                e.tensor_copy(wr[:, layer, :, 0:NEG], wrg_st[:, layer, :].rearrange("p (c g) -> p c g", c=DC))
                for q in range(NEG):
                    e.tensor_copy(wr[:, layer, :, NEG + 4 * q:NEG + 4 * q + 4],
                                  wre_st[:, layer, q, :].rearrange("p (c k) -> p c k", c=DC))
            link(e, e.tensor_tensor(lam_st[:, 0, :], lam_st[:, 0, :], lam_st[:, 1, :], ALU.mult))
            e.tensor_reduce(lam_s[:, 0:2], lam_st[:, 0, :].rearrange("p (m d) -> p m d", m=2), AX_X, ALU.add)\
                .then_inc(prep_lam, 1)
            e.wait_ge(prep_lame, 1)
            link(e, e.tensor_tensor(lam_s[:, 4:5], lam_s[:, 3:4], lam_s[:, 2:3], ALU.subtract))
            e.tensor_scalar(neglam[:, :], lam_s[:, 4:5], -LAM_INIT, None, ALU.add)
            e.tensor_scalar(subg[:, :], subg[:, :], 1.0 - LAM_INIT, None, ALU.mult).then_inc(prep_v, 1)

            e.wait_ge(zeroed, 16 * -(-ROWS // P))
            with e.Fori(0, 2) as i:
                for c in range(12):
                    e.wait_ge(uv_tp, i * 12 + (c + 1))
                    e.tensor_copy(v[:, :, bass.ds(i * (12 * P) + c * P, P)],
                                  ps[:, 4 + c % 2, :].rearrange("p (t f) -> p t f", t=NT))
                    e.tensor_copy(VS[:, bass.ds(i * (12 * P) + c * P, P)], ps[0:NB, 6 + c % 2, 0:P])\
                        .then_inc(uv_ev, 1)
            e.wait_ge(uv_sq, GC)
            link(e, e.tensor_reduce(ss[:, :], vss[:, :, :], AX_X, ALU.add))
            e.tensor_scalar(ss[:, :], ss[:, :], 1.0 / DG, EPS, ALU.mult, ALU.add).then_inc(gate_var, 1)
            e.wait_ge(gate_root, 1)
            e.reciprocal(rstd[:, :], root[:, 0:5]).then_inc(gate_rs, 1)
            e.wait_ge(gate_rs, 1)
            for t in (0, 2):
                e.tensor_scalar(v[:, t, :], v[:, t, :], rstd[:, t:t + 1], None, ALU.mult).then_inc(gate_vn_v, 1)
            e.wait_ge(gate_gb, 16)
            e.scalar_tensor_tensor(VS, VS, rstd[0:NB, 4:5], gainb, ALU.mult, ALU.mult).then_inc(gate_vs, 1)
            e.wait_ge(gate_vs, 1)
            for g in range(NG):
                ins = e.tensor_scalar(gainb[:, g * GCOLS:(g + 1) * GCOLS], VS[:, g * GCOLS:(g + 1) * GCOLS],
                                      w00[:, 0, g:g + 1], w00[:, 1, g:g + 1], ALU.mult, ALU.add)
            ins.then_inc(gate_s, 1)
            e.wait_ge(ld_bs, 16)
            for j in range(GC):
                e.wait_ge(gate_sp, j + 1)
                if j >= 2:
                    e.wait_ge(gate_u, j - 1)
                e.scalar_tensor_tensor(gtmp[:, j % 2, :].rearrange("p (t f) -> p t f", t=NT),
                                       ps[:, j % 4, :].rearrange("p (t f) -> p t f", t=NT), sgain[:, j:j + 1],
                                       bsg[:, j * P // GCOLS, :].unsqueeze(1).broadcast_to([P, NT, P]),
                                       ALU.mult, ALU.add).then_inc(gate_tmp, 1)
                if j == 5:
                    e.wait_ge(gate_tp, 1)
                    e.tensor_tensor(u[:, :, SEQ:T], ps[:, 4, 0:GC * NB].rearrange("p (j b) -> p j b", b=NB),
                                    u[:, :, SEQ:T], ALU.mult).then_inc(gate_su, 1)

            def add_chunk(n, q):
                e.tensor_tensor(x[:, 0:NT, n], x[:, 0:NT, n], ps[:, 4 + q, :].rearrange("p (t f) -> p t f", t=NT),
                                ALU.add)
                e.tensor_tensor(x[0:NB, NT, n], x[0:NB, NT, n], ps[0:NB, 6 + q, 0:P], ALU.add)\
                    .then_inc(back_add, 1)

            e.wait_ge(again_x, 16 * 5)
            with e.Fori(0, 4) as i:
                for k in range(2):
                    e.wait_ge(back_tp, i * 2 + (k + 1))
                    add_chunk(bass.ds(i * (2 * P) + k * P, P), k)

            def moe_v(layer):
                o, before = ovfs[layer], layer * NE
                grow = 2 + layer
                L, oh, cand = R["l"], R["oh"], R["cand"]

                def first_max(vals, top, onehot, k=NEG):
                    link(e, e.tensor_reduce(top, vals, AX_X, ALU.max))
                    link(e, e.tensor_tensor(cand, vals, top.unsqueeze(2).broadcast_to([P, 5, NEG]), ALU.is_ge))
                    link(e, e.scalar_tensor_tensor(cand, cand, -99.0, iota99, ALU.mult, ALU.add))
                    link(e, e.tensor_reduce(R["least"], cand, AX_X, ALU.min))
                    link(e, e.tensor_tensor(onehot, iota, R["least"].unsqueeze(2).broadcast_to([P, 5, NEG]),
                                            ALU.is_equal))

                iota = c_["iota"].unsqueeze(1).broadcast_to([P, 5, NEG])
                iota99 = c_["iota99"].unsqueeze(1).broadcast_to([P, 5, NEG])
                link(e, e.memset(R["l"][:, NT, :], 0.0))
                e.wait_ge(moe_lg, layer + 1)
                e.tensor_tensor(L[:, 0:NT, :], ps[:, 5, 0:NT * 20].rearrange("p (t k) -> p t k", t=NT),
                                rbias[:, layer, :].unsqueeze(1).broadcast_to([P, NT, 20]), ALU.add)
                link(e, e.tensor_tensor(L[0:NB, NT, :], ps[0:NB, 5, NT * 20:5 * 20], rbias[0:NB, layer, :], ALU.add))
                first_max(L[:, :, 0:NEG], R["gmax"], oh)
                e.tensor_tensor(R["eg"], L[:, :, 0:NEG],
                                R["gmax"].unsqueeze(2).broadcast_to([P, 5, NEG]), ALU.subtract).then_inc(moe_rt, 1)
                link(e, e.tensor_tensor(
                    R["pick"].rearrange("p t (k g) -> p t k g", g=NEG),
                    L[:, :, NEG:20].rearrange("p t (g k) -> p t k g", g=NEG),
                    oh.unsqueeze(2).broadcast_to([P, 5, NEG, NEG]), ALU.mult))
                link(e, e.tensor_reduce(R["el"], R["pick"].rearrange("p t (k g) -> p t k g", g=NEG), AX_X, ALU.add))
                first_max(R["el"], R["m1"], R["oh1"])
                link(e, e.scalar_tensor_tensor(R["el2"], R["oh1"], -BIG, R["el"], ALU.mult, ALU.add))
                first_max(R["el2"], R["m2"], R["oh2"])
                e.tensor_tensor(R["e2"], R["m2"], R["m1"], ALU.subtract).then_inc(moe_rt, 1)
                for j, name in enumerate(("oh1", "oh2")):
                    link(e, e.tensor_tensor(
                        R["mm"][:, j].rearrange("p t (g k) -> p t g k", g=NEG),
                        oh.unsqueeze(3).broadcast_to([P, 5, NEG, NEG]),
                        R[name].unsqueeze(2).broadcast_to([P, 5, NEG, NEG]), ALU.mult))
                for j in range(2):
                    link(e, e.tensor_scalar(R["mm"][:, j, NT, :], R["mm"][:, j, NT, :], c_["valid"], None, ALU.mult))
                e.tensor_tensor(R["m"], R["mm"][:, 0], R["mm"][:, 1], ALU.add).then_inc(moe_mk, 1)
                e.wait_ge(moe_ex, 2 * layer + 2)
                link(e, e.tensor_reduce(R["gs"], R["eg"], AX_X, ALU.add))
                link(e, e.tensor_scalar(R["den"], R["e2"], 1.0, None, ALU.add))
                link(e, e.tensor_tensor(R["den"], R["den"], R["gs"], ALU.mult))
                link(e, e.reciprocal(R["den"], R["den"]))
                e.tensor_copy(pair_w[:, :, 0], R["den"])
                e.tensor_tensor(pair_w[:, :, 1], R["den"], R["e2"], ALU.mult)
                e.wait_ge(moe_cum, layer + 1)
                cnt = ps[:, 6, 5 * NE:6 * NE]
                link(e, e.tensor_scalar(R["ov"], cnt, float(SLOTS), None, ALU.is_gt))
                for q in range(2, MAXT + 1):
                    link(e, e.tensor_scalar(R["ov1"], cnt, float(q * SLOTS), None, ALU.is_gt))
                    link(e, e.tensor_tensor(R["ov"], R["ov"], R["ov1"], ALU.add))
                lt = c_["lt"].rearrange("p (a b) -> p a b", a=NE)
                link(e, e.tensor_tensor(R["big"], lt,
                                        R["ov"].unsqueeze(1).broadcast_to([P, NE, NE]), ALU.mult))
                link(e, e.tensor_reduce(R["ob"], R["big"], AX_X, ALU.add))
                link(e, e.tensor_scalar(R["dl"], R["ob"], float(SLOTS), float((NE - 1) * SLOTS), ALU.mult, ALU.add))
                link(e, e.tensor_tensor(R["dl"], R["dl"], c_["first"], ALU.subtract))
                pos = ps[:, 6, 0:5 * NE].rearrange("p (t k) -> p t k", t=5)
                link(e, e.tensor_scalar(R["ge"], pos, float(SLOTS), None, ALU.is_ge))
                link(e, e.tensor_tensor(R["ge"], R["ge"], R["dl"].unsqueeze(1).broadcast_to([P, 5, NE]), ALU.mult))
                link(e, e.tensor_tensor(R["ge"], R["ge"], c_["first"].unsqueeze(1).broadcast_to([P, 5, NE]), ALU.add))
                link(e, e.tensor_tensor(R["ge"], R["ge"], pos, ALU.add))
                for j in range(2):
                    link(e, e.tensor_tensor(R["mm"][:, j], R["mm"][:, j], R["ge"], ALU.mult))
                    link(e, e.tensor_reduce(slot_f[:, :, j], R["mm"][:, j], AX_X, ALU.add))
                tile_ = c_["tile"][0:1].unsqueeze(2).broadcast_to([1, OVF, NE])
                link(e, e.tensor_tensor(R["oe"], tile_, R["ob"][0:1].unsqueeze(1).broadcast_to([1, OVF, NE]),
                                        ALU.is_ge))
                link(e, e.tensor_tensor(R["oend"], R["ob"][0:1], R["ov"][0:1], ALU.add))
                link(e, e.tensor_tensor(R["oe2"], tile_, R["oend"].unsqueeze(1).broadcast_to([1, OVF, NE]),
                                        ALU.is_lt))
                link(e, e.tensor_tensor(R["oe"], R["oe"], R["oe2"], ALU.mult))
                link(e, e.tensor_tensor(R["oe"], R["oe"], c_["eid"][0:1].unsqueeze(1).broadcast_to([1, OVF, NE]),
                                        ALU.mult))
                link(e, e.tensor_reduce(R["of"][:, 1:1 + OVF], R["oe"], AX_X, ALU.add))
                link(e, e.tensor_reduce(R["of"][:, 0:1], R["ov"][0:1], AX_X, ALU.add))
                link(e, e.tensor_copy(ovf_i[:, :], R["of"]))
                e.tensor_copy(slot_i[:, :].rearrange("p (t j) -> p t j", j=2), slot_f[:, :, :]).then_inc(moe_idx, 1)

                gainx = gains[:, grow, :].rearrange("p (h c) -> p h c", h=2).unsqueeze(3)\
                    .broadcast_to([P, 2, 4, SLOTS])

                def evac_rows(i, k):
                    e.wait_ge(moe_tp, i * 2 + (before + k + 1))
                    if k >= 2:
                        e.wait_ge(moe_gu, i * 2 + (before + k - 1))
                    e.tensor_tensor(xsT[:, k % 2].rearrange("p (h c) s -> p h c s", h=2),
                                    ps[:, 0:2, 0:4 * SLOTS].rearrange("p h (c s) -> p h c s", c=4), gainx,
                                    ALU.mult).then_inc(moe_tev, 1)

                def hidden(i, k):
                    q = k % 2
                    e.wait_ge(moe_silu, i * 2 + (before + k + 1))
                    if k >= 2:
                        e.wait_ge(moe_dn, i * 2 + (before + k - 1))
                    e.tensor_tensor(hid[:, q].rearrange("p f s -> p (f s)"), sg[:, q].rearrange("p f s -> p (f s)"),
                                    ps[:, 2 + q, 2 * SLOTS:4 * SLOTS], ALU.mult).then_inc(moe_hid, 1)

                def y_half(i, k):
                    e.wait_ge(moe_dn, i * 2 + (before + k + 1))
                    e.wait_ge((moe_st0, moe_st1)[k % 2], i * 16 + (8 * before + k // 2 * 16))
                    e.tensor_copy(ye[0:SLOTS, k % 2, 512:1024], ps[0:SLOTS, 5 + 2 * (k % 2), :]).then_inc(moe_yv, 1)

                evac_rows(0, 0)
                hidden(0, 0)
                evac_rows(0, 1)
                for k in (1, 2):
                    hidden(0, k)
                    y_half(0, k - 1)
                    evac_rows(0, k + 1)
                with e.Fori(0, 6) as i:
                    for k in range(2):
                        hidden(i, 3 + k)
                        y_half(i, 2 + k)
                        evac_rows(i, 4 + k)
                hidden(0, 15)
                y_half(0, 14)
                y_half(0, 15)
                n_ovf = e.value_load(ovf_i[0:1, 0:1], min_val=0, max_val=OVF)
                with e.If(n_ovf > 0):
                    with e.Fori(0, OVF) as t:
                        e.wait_ge(o["tp"], t + 1)
                        e.tensor_tensor(xsT[:, 0].rearrange("p (h c) s -> p h c s", h=2),
                                        ps[:, 0:2, 0:4 * SLOTS].rearrange("p h (c s) -> p h c s", c=4), gainx,
                                        ALU.mult).then_inc(o["tev"], 1)
                        e.wait_ge(o["silu"], t + 1)
                        e.tensor_tensor(hid[:, 0].rearrange("p f s -> p (f s)"),
                                        sg[:, 0].rearrange("p f s -> p (f s)"), ps[:, 2, 2 * SLOTS:4 * SLOTS],
                                        ALU.mult).then_inc(o["hid"], 1)
                        e.wait_ge(o["dn"], t + 1)
                        e.tensor_copy(ye[0:SLOTS, 0, 512:1024], ps[0:SLOTS, 5, :]).then_inc(o["y"], 1)
                for t in range(5):
                    r = rows_of(t)
                    e.wait_ge(gathered[t], 32 * (layer + 1))
                    link(e, e.scalar_tensor_tensor(x[0:r, t, :], yg[0:r, t, 0, :], pair_w[0:r, t, 0:1], x[0:r, t, :],
                                                   ALU.mult, ALU.add))
                    e.scalar_tensor_tensor(x[0:r, t, :], yg[0:r, t, 1, :], pair_w[0:r, t, 1:2], x[0:r, t, :],
                                           ALU.mult, ALU.add).then_inc(moe_comb, 1)

            norm_v(1, lambda q, t: q.wait_ge(back_add, DC), [2], [hT])
            moe_v(0)
            norm_v(2, lambda q, t: q.wait_ge(moe_comb, t + 1), [4, 1], [hT, hqT])
            kst = (kvq_kst0, kvq_kst1)
            for n in range(3 * DC):
                kind, h = divmod(n, DC)
                e.wait_ge(kvq_tp, n + 1)
                if kind == 0 and n >= 2:
                    e.wait_ge(kst[n % 2], 16 * (n // 2))
                src = ps[:, 4 + n % 2, :].rearrange("p (t f) -> p t f", t=NT)
                if kind == 0:
                    e.tensor_copy(ktok[:, n % 2].rearrange("p (t f) -> p t f", t=NT), src)
                if kind == 1:
                    e.tensor_copy(vtok[:, :, h * P:(h + 1) * P], src)
                e.tensor_copy(tok8[:, kind, h * P:(h + 1) * P], ps[0:NB, 6 + n % 2, 0:P]).then_inc(kvq_ev, 1)
            e.wait_ge(kvq_ev, 3 * DC)
            link(e, e.tensor_tensor(prod[0:NB, 0, :], tok8[:, 2, :], tok8[:, 0, :], ALU.mult))
            e.tensor_reduce(down_, prod[0:NB, 0, :].rearrange("p (k d) -> p k d", d=HD), AX_X, ALU.add)\
                .then_inc(dec_own, 1)
            e.wait_ge(kvq_vst, 16 * (NT + 2))
            e.wait_ge(kvq_qst, 16)
            steps = NH * NT
            for k in range(steps + 1):
                if k < steps:
                    h, q = divmod(k, NT)
                    w = (q + 1) * P
                    e.wait_ge(att_qk, k + 1)
                    e.wait_ge(att_bias, h + 1)
                    if k >= 2:
                        e.wait_ge(att_tp, k - 1)
                    for mp in range(2):
                        ins = e.tensor_tensor_reduce(st[:, k % 2, mp * SEQ:mp * SEQ + w],
                                                     ps[:, 2 * (k % 2) + mp, 0:w], bias8[:, h % 2, SEQ - w:SEQ],
                                                     HD ** -0.5, -3e38, ALU.add, ALU.max, mx[:, k % 2, mp:mp + 1])
                    link(e, ins)
                    e.tensor_scalar(nm[:, k % 2, :], mx[:, k % 2, :], -1.0, None, ALU.mult).then_inc(att_neg, 1)
                if k >= 1:
                    n = k - 1
                    w = (n % NT + 1) * P
                    q = n % 2
                    e.wait_ge(att_ex, n + 1)
                    link(e, e.reciprocal(rz[:, q, :], zz[:, q, :]))
                    link(e, e.tensor_tensor(rz[:, q, 1:2], rz[:, q, 1:2], neglam[:, :], ALU.mult))
                    link(e, e.tensor_scalar(st[:, q, 0:w], st[:, q, 0:w], rz[:, q, 0:1], None, ALU.mult))
                    e.scalar_tensor_tensor(st[:, q, 0:w], st[:, q, SEQ:SEQ + w], rz[:, q, 1:2], st[:, q, 0:w],
                                           ALU.mult, ALU.add).then_inc(att_a, 1)
                    b, page = divmod(n, PAGES)
                    e.wait_ge(dec_prod, n + 1)
                    e.tensor_reduce(sK[:, page, b * 16:(b + 1) * 16],
                                    prod[:, n % 2, :].rearrange("p (k d) -> p k d", d=HD), AX_X, ALU.add)\
                        .then_inc(dec_red, 1)
            for t in range(NT):
                e.wait_ge(att_sq, t + 1)
                e.tensor_reduce(oss[:, t, :], st[:, t % 2, :].rearrange("p (h d) -> p h d", h=NH), AX_X, ALU.add)\
                    .then_inc(att_osq, 1)
            e.wait_ge(att_osq, NT)
            e.tensor_scalar(oss, oss, 1.0 / P, EPS, ALU.mult, ALU.add).then_inc(att_var, 1)
            e.wait_ge(att_root, 1)
            link(e, e.reciprocal(orr.rearrange("p t h -> p (t h)"), root[:, 0:NT * NH]))
            for t in range(NT):
                e.tensor_tensor(otok[:, t, :].rearrange("p (h d) -> p h d", h=NH),
                                otok[:, t, :].rearrange("p (h d) -> p h d", h=NH),
                                orr[:, t, :].unsqueeze(2).broadcast_to([P, NH, P]), ALU.mult).then_inc(att_on, 1)
            link(e, e.tensor_scalar(dbias, c_["past"], c_["slope"], None, ALU.mult))
            e.wait_ge(dec_tp, 1)
            e.wait_ge(dec_ownr, 16)
            e.tensor_tensor_reduce(dS[:, 0:SEQ], ps[:, 0, :], dbias, HD ** -0.5, -3e38, ALU.add, ALU.max,
                                   dsm[:, 0:1])
            link(e, e.tensor_scalar(dS[:, SEQ:SEQ + 1], downc, HD ** -0.5, None, ALU.mult))
            link(e, e.tensor_tensor(dsm[:, 1:2], dsm[:, 0:1], dS[:, SEQ:SEQ + 1], ALU.max))
            e.tensor_scalar(dsm[:, 2:3], dsm[:, 1:2], -1.0, None, ALU.mult).then_inc(dec_max, 1)
            link(e, e.scalar_tensor_tensor(dsm[:, 4:5], c_["odd"], neglam[:, 0:1], c_["even"], ALU.mult, ALU.add))
            e.wait_ge(dec_ex, 1)
            link(e, e.reciprocal(dsm[:, 5:6], dsm[:, 3:4]))
            link(e, e.tensor_tensor(dsm[:, 6:7], dsm[:, 4:5], dsm[:, 5:6], ALU.mult))
            e.tensor_scalar(dC, c_["sel"], dsm[:, 6:7], None, ALU.mult).then_inc(dec_c, 1)
            e.wait_ge(dec_otp, 1)
            e.wait_ge(dec_vown, 16)
            link(e, e.scalar_tensor_tensor(do64, dvown, daown, ps[0:64, 2, 0:P], ALU.mult, ALU.add))
            link(e, e.tensor_tensor_reduce(dvown, do64, do64, 1.0, 0.0, ALU.mult, ALU.add, dsm[0:64, 7:8]))
            e.tensor_scalar(dsm[0:64, 8:9], dsm[0:64, 7:8], 1.0 / P, EPS, ALU.mult, ALU.add).then_inc(dec_sq, 1)
            e.wait_ge(dec_root, 1)
            link(e, e.reciprocal(dsm[0:64, 10:11], dsm[0:64, 9:10]))
            e.tensor_scalar(do64, do64, dsm[0:64, 10:11], None, ALU.mult).then_inc(dec_o2, 1)
            for n in range(DC):
                e.wait_ge(back_tp, DC + n + 1)
                add_chunk(slice(n * P, (n + 1) * P), n % 2)
            norm_v(3, lambda q, t: q.wait_ge(back_add, 2 * DC), [3], [hT])
            moe_v(1)
            norm_v(4, lambda q, t: q.wait_ge(moe_comb, 5 + t + 1), [], [], normed=False)
            e.wait_ge(norm_rs, 5)
            e.wait_ge(fin_g, 16)
            for t in range(5):
                r = rows_of(t)
                e.scalar_tensor_tensor(xn[0:r, t].rearrange("p c f -> p (c f)"), x[0:r, t, :],
                                       rstd[0:r, t:t + 1], gfin[0:r, :], ALU.mult, ALU.mult).then_inc(fin_y, 1)


INS = ["x_prompt", "x_sample", "cache_k", "cache_v", "page_table", "norm_mix", "norm_ffn", "w_uv", "sgu_gain",
       "w_sgu", "b_sgu", "w_gmlp_o", "norm_kv", "w_k", "w_v", "w_q", "lam_q", "lam_k", "subln_gain", "w_attn_o",
       "w_router_group", "b_router_group", "w_router_expert", "b_router_expert", "w_e_gate", "w_e_up", "w_e_down",
       "norm_final"]
OUTS = {"y_prompt": (1, SEQ, D), "y_sample": (NB, 1, D), "k_prompt": (1, NT, P, NH, 2, HD),
        "v_prompt": (1, NT, P, NH, P), "k_sample": (NB, 1, NH, 2, HD), "v_sample": (NB, 1, NH, P),
        "gmlp_v_sample": (1, NB, 1, DG)}


def kernel(**inputs):
    import numpy as np
    import concourse.bacc as bacc
    from concourse.bass_utils import run_bass_kernel_spmd

    nc = bacc.Bacc("TRN2", target_bir_lowering=False, num_devices=1)
    arrays = {"in_" + n: np.ascontiguousarray(inputs[n]) for n in INS}
    arrays["in_geometry"] = geometry()
    a = {n[3:]: nc.dram_tensor(n, v.shape, mybir.dt.from_np(v.dtype), kind="ExternalInput").ap()
         for n, v in arrays.items()}
    out = {n: nc.dram_tensor("out_" + n, shape, F32, kind="ExternalOutput").ap() for n, shape in OUTS.items()}
    build(nc, a, out)
    r = run_bass_kernel_spmd(nc, [arrays], core_ids=[0])
    return tuple(r.results[0]["out_" + n] for n in OUTS)
```

```python
import math
from contextlib import ExitStack

import concourse.bass as bass
from concourse import mybir

F32 = mybir.dt.float32
I32 = mybir.dt.int32
ALU = mybir.AluOpType
ACT = mybir.ActivationFunctionType
AX_X = mybir.AxisListType.X

P = 128
D = 1024
DC = D // P
SEQ = 512
NB = 8
T = SEQ + NB
HALF = T // 2
NT = SEQ // P
DG = 3 * D
GC = DG // P
NG = 8
GCOLS = DG // NG
NH = 8
HD = 64
NE = 16
NEG = 4
TOPK = 2
DE = 256
EPS = 1e-6
PAGES = 4
BIG = 1e30
LAM_INIT = 0.8 - 0.6 * math.exp(-0.3)
RING = 6
SLOTW = 2048
SLOTS = 128
PAIRS = TOPK * T
OVF = (PAIRS - TOPK) // SLOTS
ROWS = (NE + OVF) * SLOTS
MAXT = (T - 1) // SLOTS

UV0 = 0
GO0 = UV0 + 2 * DG // 256
MOE0 = GO0 + 3 * DC
KVQ0 = MOE0 + 3 * NE
VP0 = KVQ0 + 4 + 8 * 3
AO0 = VP0 + NB * PAGES // 2
MOE1 = AO0 + 4
END = MOE1 + 3 * NE

CONSTS = {}
_at = 0
for _name, _n in [("ident", P), ("tri", P), ("ones", P), ("causal", P), ("dist", SEQ), ("past", SEQ), ("sel", 64),
                  ("lt", NE * NE), ("slope", 1), ("even", 1), ("odd", 1), ("valid", 1), ("iota", NEG),
                  ("iota99", NEG), ("first", NE), ("eid", NE), ("tile", OVF)]:
    CONSTS[_name] = (_at, _at + _n)
    _at += _n
NCONST = _at


DEC_JOIN = 7
DEC_STEPS = [9 + 3 * b for b in range(NB)]
N_SMALL = 15


def geometry():
    import numpy as np

    k = np.zeros((P, NCONST), np.float32)
    p = np.arange(P)[:, None]

    def put(name, value):
        lo, hi = CONSTS[name]
        k[:, lo:hi] = value

    n = np.arange(P)[None]
    put("ident", p == n)
    put("tri", p < n)
    put("ones", 1)
    put("causal", p <= n)
    dist = p + (NT - 1) * P - np.arange(SEQ)[None]
    put("dist", np.where(dist >= 0, dist, BIG))
    put("past", PAGES * P - np.arange(SEQ)[None])
    put("sel", p // 2 == np.arange(64)[None])
    put("lt", np.tile((np.arange(NE)[None, :] < np.arange(NE)[:, None]).reshape(1, -1), (P, 1)))
    put("slope", -8.0 * 2.0 ** -(1.0 + p // 2 % NH))
    put("even", p % 2 == 0)
    put("odd", p % 2 == 1)
    put("valid", p < NB)
    put("iota", np.arange(NEG)[None])
    put("iota99", np.arange(NEG)[None] + 99)
    put("first", np.arange(NE)[None] * SLOTS)
    put("eid", np.arange(NE)[None])
    put("tile", np.arange(OVF)[None])
    return k


def bcast_rows(ap, pattern, n, layers):
    flat = ap.rearrange(pattern).rearrange("(o n) -> o n", o=1)
    return flat.broadcast_to([n, flat.shape[1]]).rearrange("p (l k) -> p l k", l=layers)


def kvq_block(k):
    return KVQ0 + (k if k < 4 else 4 + 3 * (k - 4))


def kpage_block(n):
    return KVQ0 + 5 + n // 4 * 3 + n // 2 % 2


def kpages(b):
    j, r = divmod(b - KVQ0 - 4, 3)
    return [4 * j + 2 * r - 2, 4 * j + 2 * r - 1] if KVQ0 + 4 <= b < VP0 and r else []


def loads_per_block(b):
    return 32 if kpages(b) or VP0 <= b < AO0 else 16


def loaded_value(b):
    return sum(loads_per_block(c) for c in range(b % RING, b + 1, RING))


def build(nc, a, out):
    ctx = ExitStack()

    def sb(name, shape, dt=F32):
        return ctx.enter_context(nc.sbuf_tensor(name, shape, dt))

    def sem(name):
        return ctx.enter_context(nc.semaphore(name))

    def sems(stage, names):
        return [sem(f"{stage}_{n}") for n in names.split()]

    with ctx:
        x = sb("x", [P, 5, D])
        hT = sb("hT", [P, DC, T])
        ring = sb("ring", [P, RING, SLOTW])
        U = sb("U", [P, GC * T])
        V = sb("V", [P, NT * DG])
        K = sb("K", [P, NCONST])
        c_ = {n: K[:, lo:hi] for n, (lo, hi) in CONSTS.items()}
        ident, ones = c_["ident"], c_["ones"]
        gains = sb("gains", [P, 5, DC])
        sgain = sb("sgain", [P, GC])
        wT = sb("wT", [P, NG, P])
        wr = sb("wr", [P, 2, DC, 20])
        rbias = sb("rbias", [P, 2, 20])
        w00 = sb("w00", [NB, 2, NG])
        subg = sb("subg", [P, 1])
        neglam = sb("neglam", [P, 1])
        pt = sb("pt", [1, NB * PAGES], I32)
        ss = sb("ss", [P, 5])
        rstd = sb("rstd", [P, 5])
        root = sb("root", [P, 40])
        vtmp = sb("vtmp", [P, 2, T])
        ps = ctx.enter_context(nc.psum_tensor("ps", [P, 8, 512], F32))

        def take(region, at, shape):
            n = math.prod(shape)
            ap = region[:, at:at + n]
            if len(shape) == 2:
                ap = ap.rearrange("p (a b) -> p a b", a=shape[0])
            if len(shape) == 3:
                ap = ap.rearrange("p (a b c) -> p a b c", a=shape[0], b=shape[1])
            return ap

        xflat = x[:, :, :].rearrange("p t f -> p (t f)")
        VS = xflat[0:NB, 0:DG]
        gtmp = take(xflat, DG, (2, SEQ))
        bsg = take(xflat, DG + 2 * SEQ, (NG, P))
        u = take(U, 0, (GC, T))
        xn = take(U, 0, (5, DC, P))
        e0 = 5 * D
        xs = take(U, e0, (2, DC, P))
        xsT = take(U, e0 + 2 * D, (2, DC, SLOTS))
        e1 = e0 + 2 * D + 2 * DC * SLOTS
        sg = take(U, e1, (2, 2, SLOTS))
        hid = take(U, e1 + 4 * SLOTS, (2, 2, SLOTS))
        ye = take(U, e1 + 8 * SLOTS, (2, D))
        assert e1 + 8 * SLOTS + 2 * D <= GC * T
        vtok = take(U, 0, (NT, D))
        ktok = take(U, NT * D, (2, 512))
        hqT = take(U, 5 * D, (DC, T))
        tok8 = take(U, 5 * D + DC * T, (3, D))[0:NB]
        assert 5 * D + DC * T + 3 * D <= GC * T
        otok = take(U, NT * D, (NT, D))
        st = take(U, 2 * NT * D, (3, 2 * SEQ))
        qbc = take(U, 5 * D, (2, D))
        s0 = 2 * NT * D + 3 * 2 * SEQ
        dC = U[:, s0:s0 + 64]
        daT = take(U, s0 + 64, (PAGES, NB * NH))
        doT = U[:, s0 + 320:s0 + 384]
        do64 = U[0:NB * NH, s0 + 384:s0 + 512]
        dvown = U[0:NB * NH, s0 + 512:s0 + 640]
        daown = U[0:NB * NH, s0 + 640:s0 + 641]
        dsq = U[0:NB * NH, s0 + 648:s0 + 776]
        assert s0 + 776 <= GC * T
        v = take(V, 0, (NT, DG))
        yg = take(V, 0, (5, TOPK, D))
        ow = take(V, 0, (3, SLOTW))
        kT = take(V, 0, (DC, T))
        qT = take(V, DC * T, (DC, T))
        v0 = 2 * DC * T
        prod = take(V, v0, (2, D))
        aT = take(V, v0 + 2 * D, (2, SEQ))
        sK = take(V, v0 + 3 * D, (PAGES, P))
        v1 = v0 + 3 * D + PAGES * P
        mx = take(V, v1, (2, 2))
        nm = take(V, v1 + 4, (2, 2))
        zz = take(V, v1 + 8, (2, 2))
        rz = take(V, v1 + 12, (4, 2))
        oss = take(V, v1 + 24, (NT, NH))
        orr = take(V, v1 + 56, (NT, NH))
        dsm = V[:, v1 + 88:v1 + 104]
        down_ = V[0:NB, v1 + 104:v1 + 120]
        downc = V[:, v1 + 120:v1 + 121]
        osq = V[:, v1 + 124:v1 + 124 + P]
        assert v1 + 124 + P <= NT * DG
        hTflat = hT[:, :, :].rearrange("p j t -> p (j t)")
        dS = hTflat[:, 0:SEQ + 1]
        dbias = hTflat[:, 520:520 + SEQ]
        oT = hT
        bias8 = wT[:, :, :].rearrange("p g t -> p (g t)").rearrange("p (b f) -> p b f", b=2)
        slot_f = sb("slot_f", [P, 5, TOPK])
        slot_i = sb("slot_i", [P, 5 * TOPK], I32)
        pair_w = sb("pair_w", [P, 5, TOPK])
        ovf_i = sb("ovf_i", [1, 1 + OVF], I32)
        zeros = V[:, 4 * D:5 * D]
        vss = sb("vss", [P, 5, GC])
        gfin = hTflat[:, 0:D]
        gainb = hTflat[0:NB, D:D + DG]
        R, r0 = {}, 10 * D
        for name, shape in (("l", (5, 20)), ("eg", (5, NEG)), ("cand", (5, NEG)), ("oh", (5, NEG)),
                            ("oh1", (5, NEG)), ("oh2", (5, NEG)), ("el", (5, NEG)), ("el2", (5, NEG)),
                            ("gmax", (5,)), ("m1", (5,)), ("m2", (5,)), ("e2", (5,)), ("gs", (5,)), ("den", (5,)),
                            ("least", (5,)), ("pick", (5, NE)), ("m", (5, NE)), ("mm", (2, 5, NE)),
                            ("ov", (NE,)), ("ov1", (NE,)), ("ob", (NE,)), ("dl", (NE,)), ("oend", (NE,)),
                            ("big", (NE, NE)), ("ge", (5, NE)), ("oe", (OVF, NE)), ("oe2", (OVF, NE)),
                            ("of", (1 + OVF,))):
            R[name] = take(V, r0, shape)
            r0 += math.prod(shape)
        assert r0 <= NT * DG
        for name in ("oend", "oe", "oe2", "of"):
            R[name] = R[name][0:1]
        w_st = take(V, D, (NG, P))
        wre_st = V[:, 2 * D:2 * D + 256].rearrange("p (l g f) -> p l g f", l=2, g=NEG)
        wrg_st = V[:, 2 * D + 256:2 * D + 320].rearrange("p (l f) -> p l f", l=2)
        sg_st = V[0:GC, 2 * D + 320:2 * D + 448]
        lam_st = take(V, 2 * D + 448, (2, 2 * HD))
        lam_s = V[:, 2 * D + 704:2 * D + 712]

        slots_dram = nc.dram_tensor("slots_dram", [ROWS, D], F32, kind="Internal").ap()
        q_dram = nc.dram_tensor("q_dram", [NB, D], F32, kind="Internal").ap()
        own_dram = nc.dram_tensor("own_dram", [NB, 2 * NH], F32, kind="Internal").ap()

        loaded = [sem(f"loaded{s}") for s in range(RING)]
        ld_x = [sem(f"ld_x{t}") for t in range(5)]
        again_x = sem("again_x")
        ld_c, ld_w, ld_pt, ld_bs = sem("ld_c"), sem("ld_w"), sem("ld_pt"), sem("ld_bs")
        (prep_init, prep_tp, prep_v, prep_lam, prep_lame) = sems(
            "prep", "init tp v lam lame")
        zero_set, zeroed = sem("zero_set"), sem("zeroed")
        chain = sem("chain")
        (norm_sq_a, norm_sq_v, norm_var, norm_root, norm_rs, norm_xn, norm_tp, norm_ev) = sems(
            "norm", "sq_a sq_v var root rs xn tp ev")
        (uv_mm, uv_gelu, uv_tp, uv_ev, uv_sq) = sems(
            "uv", "mm gelu tp ev sq")
        (gate_var, gate_root, gate_rs, gate_vn_v, gate_vn_a, gate_vs, gate_vs_out, gate_sp, gate_tmp, gate_u,
         gate_gb, gate_s, gate_tp, gate_su) = sems(
            "gate", "var root rs vn_v vn_a vs vs_out sp tmp u gb s tp su")
        (back_mm, back_cp, back_tp, back_add) = sems(
            "back", "mm cp tp add")
        (moe_lg, moe_rt, moe_ex, moe_mk, moe_cum, moe_idx, moe_scat, moe_ld0, moe_ld1, moe_tp, moe_tev, moe_gu,
         moe_silu, moe_hid, moe_dn, moe_ya, moe_yv, moe_st0, moe_st1, moe_gat0, moe_gat1, moe_gat2, moe_gat3,
         moe_gat4, moe_comb, moe_over) = sems(
            "moe", "lg rt ex mk cum idx scat ld0 ld1 tp tev gu silu hid dn ya yv st0 st1 gat0 gat1 gat2 "
            "gat3 gat4 comb over")
        gathered = [moe_gat0, moe_gat1, moe_gat2, moe_gat3, moe_gat4]
        ovfs = [{k: sem(f"ovf{n}_{k}") for k in "ld tp tev gu silu hid dn y st".split()} for n in range(2)]
        (kvq_mm, kvq_cp, kvq_tp, kvq_ev, kvq_kst0, kvq_kst1, kvq_vst, kvq_qst, kvq_qld0, kvq_qld1) = sems(
            "kvq", "mm cp tp ev kst0 kst1 vst qst qld0 qld1")
        (att_bias, att_qk, att_neg, att_ex, att_a, att_tp, att_aT, att_pv, att_o, att_var,
         att_root, att_on, att_tp2, att_ev) = sems(
            "att", "bias qk neg ex a tp aT pv o var root on tp2 ev")
        (dec_prod, dec_red, dec_own, dec_ownw, dec_ownr, dec_tp, dec_max0, dec_max, dec_ex, dec_c, dec_aTp, dec_aT, dec_pv,
         dec_o, dec_otp, dec_sq, dec_root, dec_o2, dec_otp2, dec_ev, dec_vown) = sems(
            "dec", "prod red own ownw ownr tp max0 max ex c aTp aT pv o otp sq root o2 otp2 ev vown")
        fin_y, fin_st, fin_g = sem("fin_y"), sem("fin_st"), sem("fin_g")

        block = ctx.enter_context(nc.Block())
        chained = [0]

        def link(eng, ins):
            ins.then_inc(chain, 1)
            chained[0] += 1
            eng.wait_ge(chain, chained[0])

        def slot_loaded(eng, b, i=0):
            eng.wait_ge(loaded[b % RING], i * 16 + loaded_value(b))

        def ringslot(b, shape):
            return take(ring[:, b % RING, :], 0, shape)

        def rows_of(t):
            return P if t < NT else NB

        def cols_of(t):
            return slice(t * P, t * P + rows_of(t))

        def last_use(b):
            if b < GO0:
                return uv_mm, 2 * (b - UV0) + 2
            if b < MOE0:
                return back_mm, (b - GO0) // 3 + 1
            if KVQ0 <= b < VP0:
                if kpages(b):
                    return dec_prod, kpages(b)[1] + 1
                return kvq_mm, 2 * [kvq_block(k) for k in range(12)].index(b) + 2
            if VP0 <= b < AO0:
                return dec_pv, (b - VP0) // 2 + 1
            if AO0 <= b < MOE1:
                return back_mm, DC + 2 * (b - AO0) + 2
            r, before = (b - MOE0, 0) if b < KVQ0 else (b - MOE1, NE)
            if r < 2:
                return moe_gu, before + 1
            if r >= 44:
                return ((moe_gu, 16), (moe_gu, 16), (moe_dn, 15), (moe_dn, 16))[r - 44][0], \
                    before + (16, 16, 15, 16)[r - 44]
            q, s = divmod(r - 2, 3)
            return (moe_dn, before + q + 1) if s == 2 else (moe_gu, before + q + 2)

        @block.sync
        def _(sp):
            def free(b, i=0, per_loop=0):
                if b >= RING:
                    used, value = last_use(b - RING)
                    sp.wait_ge(used, i * per_loop + value)

            def load(b, src, shape, i=0, per_loop=0):
                free(b, i, per_loop)
                sp.dma_start(ringslot(b, shape), src).then_inc(loaded[b % RING], 16)

            for t in range(5):
                src = a["x_prompt"][0, t * P:(t + 1) * P, :] if t < NT else a["x_sample"][:, 0, :]
                sp.dma_start(x[0:rows_of(t), t, :], src).then_inc(ld_x[t], 16)
            w_uv = a["w_uv"][0].rearrange("(p c) n -> p c n", c=DC)
            for k in range(RING):
                load(UV0 + k, w_uv[:, :, k * 256:(k + 1) * 256], (DC, 256))
            sp.wait_ge(ld_pt, 16)
            pages = [sp.value_load(pt[0:1, n:n + 1], min_val=0, max_val=a["cache_k"].shape[0] - 1)
                     for n in range(NB * PAGES)]
            with sp.Fori(0, 3) as i:
                for k in range(RING):
                    load(UV0 + RING + k, w_uv[:, :, bass.ds(i * (RING * 256) + (RING + k) * 256, 256)],
                         (DC, 256), i, 2 * RING)
            w_go = a["w_gmlp_o"][0].rearrange("(b c p) n -> p b c n", c=DC, p=P)
            for k in range(RING):
                load(GO0 + k, w_go[:, k % 3, :, (k // 3) * P:(k // 3 + 1) * P], (DC, P))
            with sp.Fori(0, 3) as i:
                for k in range(RING):
                    load(GO0 + RING + k, w_go[:, k % 3, :, bass.ds(i * (2 * P) + (2 + k // 3) * P, P)],
                         (DC, P), i, 2)

            cache_k = a["cache_k"].rearrange("g s h m d -> g s (h m d)")
            cache_v = a["cache_v"].rearrange("g s h d -> g s (h d)")

            def page_load(b, half, cache, n):
                page = pages[n]
                sp.dma_start(ringslot(b, (2, D))[:, half, :],
                             cache[bass.ds(page, 1)].rearrange("o s f -> (o s) f")).then_inc(loaded[b % RING], 16)

            def kvq_load(b):
                free(b)
                if kpages(b):
                    for half, n in enumerate(kpages(b)):
                        page_load(b, half, cache_k, n)
                    return
                k = [kvq_block(k) for k in range(12)].index(b)
                w = (a["w_q"][0], a["w_k"], a["w_v"])[k // 4].rearrange("(p c) n -> p c n", c=DC)
                sp.dma_start(ringslot(b, (DC, 256)), w[:, :, (k % 4) * 256:(k % 4 + 1) * 256])\
                    .then_inc(loaded[b % RING], 16)

            def experts(base, layer, behind):
                wg = a["w_e_gate"][layer].rearrange("e (p c) f -> e p c f", c=DC)
                wu = a["w_e_up"][layer].rearrange("e (p c) f -> e p c f", c=DC)
                wd = a["w_e_down"][layer].rearrange("e (f p) n -> e p f n", p=P)
                before = NE * layer
                ld, stored = (moe_ld0, moe_ld1), (moe_st0, moe_st1)

                def one(w, e):
                    return w[bass.ds(e, 1)].rearrange("o p c f -> (o p) c f")

                def rows(e):
                    return slots_dram[bass.ds(e * SLOTS, SLOTS), :]

                def load_rows(i, k):
                    if not (isinstance(i, int) and k < 2):
                        sp.wait_ge(moe_tp, i * 2 + (before + k - 1))
                    sp.dma_start(xs[0:SLOTS, k % 2].rearrange("p c f -> p (c f)"), rows(i * 2 + k))\
                        .then_inc(ld[k % 2], 16)

                def store_rows(i, k):
                    sp.wait_ge(moe_ya, i * 2 + (before + k + 1))
                    sp.wait_ge(moe_yv, i * 2 + (before + k + 1))
                    sp.dma_start(rows(i * 2 + k), ye[0:SLOTS, k % 2, :]).then_inc(stored[k % 2], 16)

                load(base, wg[0], (DC, DE))
                load(base + 1, wu[0], (DC, DE))
                for k in range(2):
                    b = base + 2 + 3 * k
                    if k == 0:
                        load(b, wg[1], (DC, DE))
                        load(b + 1, wu[1], (DC, DE))
                        load(b + 2, wd[0], (2, D))
                        sp.wait_ge(moe_scat, 160 * (layer + 1))
                        load_rows(0, 0)
                        load_rows(0, 1)
                    else:
                        load(b, wg[2], (DC, DE))
                        load_rows(0, 2)
                        load(b + 1, wu[2], (DC, DE))
                        load(b + 2, wd[1], (2, D))
                with sp.Fori(0, 6) as i:
                    for k in range(2):
                        b = base + 8 + 3 * k
                        load(b, one(wg, i * 2 + (3 + k)), (DC, DE), i, 2)
                        load_rows(i, 3 + k)
                        load(b + 1, one(wu, i * 2 + (3 + k)), (DC, DE), i, 2)
                        load(b + 2, one(wd, i * 2 + (2 + k)), (2, D), i, 2)
                        store_rows(i, k)
                load(base + 44, wg[15], (DC, DE))
                load_rows(0, 15)
                load(base + 45, wu[15], (DC, DE))
                load(base + 46, wd[14], (2, D))
                store_rows(0, 12)
                load(base + 47, wd[15], (2, D))
                store_rows(0, 13)
                behind(0, 4)
                behind(4, 5)
                store_rows(0, 14)
                behind(5, 6)
                store_rows(0, 15)

            experts(MOE0, 0, lambda lo, hi: [kvq_load(KVQ0 + k) for k in range(lo, hi)])
            for b in range(KVQ0 + 6, VP0):
                kvq_load(b)
            for n in range(NB * PAGES):
                b = VP0 + n // 2
                if n % 2 == 0:
                    free(b)
                page_load(b, n % 2, cache_v, n)
            w_ao = a["w_attn_o"][0].rearrange("(c p) n -> p c n", p=P)
            for k in range(4):
                load(AO0 + k, w_ao[:, :, k * 256:(k + 1) * 256], (DC, 256))
            experts(MOE1, 1, lambda lo, hi: None)
            for t in range(5):
                dst = out["y_prompt"][0, t * P:(t + 1) * P, :] if t < NT else out["y_sample"][:, 0, :]
                sp.wait_ge(fin_y, t + 1)
                sp.dma_start(dst, xn[0:rows_of(t), t].rearrange("p c f -> p (c f)")).then_inc(fin_st, 16)
            sp.wait_ge(fin_st, 16 * 5)

        @block.gpsimd
        def _(g):
            g.memset(zeros[:, :], 0.0).then_inc(zero_set, 1)
            g.wait_ge(zero_set, 1)
            g.wait_ge(uv_mm, 1)
            for r in range(0, ROWS, P):
                n = min(P, ROWS - r)
                g.dma_start(slots_dram[r:r + n, :], zeros[0:n, :]).then_inc(zeroed, 16)
            g.wait_ge(norm_xn, 5)
            g.dma_start(bsg.rearrange("p g t -> p (g t)"),
                        a["b_sgu"][0].rearrange("(o g) t -> o (g t)", o=1).broadcast_to([P, NG * P]))\
                .then_inc(ld_bs, 16)
            g.wait_ge(uv_mm, 2 * GC)
            g.dma_start(gainb, a["sgu_gain"].broadcast_to([NB, DG])).then_inc(gate_gb, 16)
            g.wait_ge(gate_vs, 1)
            g.dma_start(out["gmlp_v_sample"][0, :, 0, :], VS).then_inc(gate_vs_out, 16)
            for j in range(GC):
                g.wait_ge(gate_tmp, j + 1)
                g.tensor_tensor(u[:, j, 0:SEQ], gtmp[:, j % 2, :], u[:, j, 0:SEQ], ALU.mult)\
                    .then_inc(gate_u, 1)
            g.wait_ge(gate_vs_out, 16)
            g.wait_ge(gate_s, 1)
            g.wait_ge(gate_u, GC)
            for t in range(5):
                src = a["x_prompt"][0, t * P:(t + 1) * P, :] if t < NT else a["x_sample"][:, 0, :]
                g.dma_start(x[0:rows_of(t), t, :], src).then_inc(again_x, 16)

            def moe_rows(layer):
                before = layer * NE
                g.wait_ge(moe_idx, layer + 1)
                for t in range(5):
                    for j in range(TOPK):
                        g.indirect_dma_start(
                            slots_dram, bass.IndirectOffsetOnAxis(
                                ap=slot_i[0:rows_of(t), 2 * t + j:2 * t + j + 1], axis=0),
                            xn[0:rows_of(t), t].rearrange("p c f -> p (c f)"), None).then_inc(moe_scat, 16)
                g.wait_ge(moe_st0, 16 * (before + NE) // 2)
                g.wait_ge(moe_st1, 16 * (before + NE) // 2)
                g.wait_ge(moe_over, layer + 1)
                if layer == 1:
                    g.dma_start(gfin, a["norm_final"].rearrange("(o n) -> o n", o=1).broadcast_to([P, D]))\
                        .then_inc(fin_g, 16)
                for t in range(5):
                    for j in range(TOPK):
                        g.indirect_dma_start(
                            yg[0:rows_of(t), t, j, :], None, slots_dram, bass.IndirectOffsetOnAxis(
                                ap=slot_i[0:rows_of(t), 2 * t + j:2 * t + j + 1], axis=0))\
                            .then_inc(gathered[t], 16)

            moe_rows(0)
            kout = out["k_prompt"].rearrange("b g s h m d -> (b g) s (h m d)")
            vout = out["v_prompt"].rearrange("b g s h d -> (b g) s (h d)")
            kst = (kvq_kst0, kvq_kst1)
            qld = (kvq_qld0, kvq_qld1)

            def load_q(b):
                if b >= 2:
                    g.wait_ge(dec_prod, PAGES * (b - 1))
                g.dma_start(qbc[:, b % 2, :], q_dram[b:b + 1, :].broadcast_to([P, D])).then_inc(qld[b % 2], 16)

            g.wait_ge(kvq_ev, DC)
            g.dma_start(q_dram, tok8[:, 2, :]).then_inc(kvq_qst, 16)
            g.wait_ge(kvq_qst, 16)
            load_q(0)
            load_q(1)
            for n in range(NB * PAGES):
                b, page = divmod(n, PAGES)
                if page == 0:
                    g.wait_ge(qld[b % 2], 16 * (b // 2 + 1))
                slot_loaded(g, kpage_block(n))
                if n >= 2:
                    g.wait_ge(dec_red, n - 1)
                g.tensor_tensor(prod[:, n % 2, :], ringslot(kpage_block(n), (2, D))[:, n % 2, :],
                                qbc[:, b % 2, :], ALU.mult).then_inc(dec_prod, 1)
                if page == PAGES - 1 and b + 2 < NB:
                    load_q(b + 2)
                if n % 2 == 1 and n < 2 * DC:
                    h = n // 2
                    g.wait_ge(kvq_ev, DC + h + 1)
                    g.dma_start(kout[:, :, h * P:(h + 1) * P].rearrange("g s f -> s g f"),
                                ktok[:, h % 2].rearrange("p (t f) -> p t f", t=NT)).then_inc(kst[h % 2], 16)
            g.wait_ge(kvq_ev, 3 * DC)
            for t in range(NT):
                g.dma_start(vout[t], vtok[:, t, :]).then_inc(kvq_vst, 16)
            g.dma_start(out["k_sample"].rearrange("b o h m d -> (b o) (h m d)"), tok8[:, 0, :])\
                .then_inc(kvq_vst, 16)
            g.dma_start(out["v_sample"].rearrange("b o h d -> (b o) (h d)"), tok8[:, 1, :])\
                .then_inc(kvq_vst, 16)
            g.wait_ge(dec_own, 1)
            g.dma_start(own_dram, down_).then_inc(dec_ownw, 16)
            g.wait_ge(dec_ownw, 16)
            g.dma_start(downc, own_dram.rearrange("b (h o) -> (b h) o", o=1)).then_inc(dec_ownr, 16)
            g.wait_ge(kvq_vst, 16 * (NT + 2))
            g.wait_ge(kvq_kst0, 16 * DC // 2)
            g.wait_ge(kvq_kst1, 16 * DC // 2)
            g.dma_start(dvown, out["v_sample"].rearrange("b o h d -> (b o h) d")).then_inc(dec_vown, 16)
            moe_rows(1)

        @block.scalar
        def _(s):
            s.dma_start(K[:, :], a["geometry"]).then_inc(ld_c, 16)
            mats = [(gains[:, 0:2, :], a["norm_mix"].rearrange("l (p c) -> p l c", c=DC)),
                    (gains[:, 2:4, :], a["norm_ffn"].rearrange("l (p c) -> p l c", c=DC)),
                    (gains[:, 4, :], a["norm_kv"].rearrange("(p c) -> p c", c=DC)),
                    (sg_st, a["sgu_gain"].rearrange("o (j p) -> (o j) p", p=P)),
                    (w_st, a["w_sgu"][0].rearrange("g t s -> t g s")),
                    (wrg_st, a["w_router_group"].rearrange("l (p c) g -> p l (c g)", c=DC)),
                    (wre_st[:, 0], a["w_router_expert"][0].rearrange("g (p c) e -> p g (c e)", c=DC)),
                    (wre_st[:, 1], a["w_router_expert"][1].rearrange("g (p c) e -> p g (c e)", c=DC)),
                    (rbias[:, :, 0:NEG], bcast_rows(a["b_router_group"], "l g -> (l g)", P, 2)),
                    (rbias[:, :, NEG:20], bcast_rows(a["b_router_expert"], "l g e -> (l g e)", P, 2)),
                    (w00[:, 0, :], a["w_sgu"][0, :, 0, 0:1].rearrange("g o -> o g").broadcast_to([NB, NG])),
                    (w00[:, 1, :], a["b_sgu"][0, :, 0:1].rearrange("g o -> o g").broadcast_to([NB, NG])),
                    (lam_st[:, 0, :], a["lam_q"][0].rearrange("(o m) d -> o (m d)", o=1).broadcast_to([P, 2 * HD])),
                    (lam_st[:, 1, :], a["lam_k"][0].rearrange("(o m) d -> o (m d)", o=1).broadcast_to([P, 2 * HD])),
                    (subg[:, :], a["subln_gain"].rearrange("o p -> p o"))]
            for dst, src in mats:
                s.dma_start(dst, src, allow_slow_non_contiguous=True).then_inc(ld_w, 16)
            assert len(mats) == N_SMALL
            s.dma_start(pt[:, :], a["page_table"].rearrange("(o b) p -> o (b p)", o=1)).then_inc(ld_pt, 16)

            def norm_a(n, ready, normed=True):
                for t in (0, 2, 4):
                    ready(s, t)
                    r = rows_of(t)
                    s.activation(xn[0:r, t].rearrange("p c f -> p (c f)"), x[0:r, t, :], ACT.Square,
                                 accum_out=ss[0:r, t:t + 1]).then_inc(norm_sq_a, 1)
                s.wait_ge(norm_var, n + 1)
                s.activation(root[:, 0:5], ss[:, :], ACT.Sqrt).then_inc(norm_root, 1)
                if normed:
                    s.wait_ge(norm_rs, n + 1)
                    for t in range(5):
                        r = rows_of(t)
                        s.activation(xn[0:r, t], x[0:r, t, :].rearrange("p (f c) -> p c f", c=DC), ACT.Copy,
                                     scale=rstd[0:r, t:t + 1]).then_inc(norm_xn, 1)

            s.wait_ge(prep_init, 1)
            norm_a(0, lambda e, t: e.wait_ge(ld_x[t], 16))
            s.wait_ge(prep_lam, 1)
            s.activation(lam_s[:, 2:4], lam_s[:, 0:2], ACT.Exp).then_inc(prep_lame, 1)

            for part in range(2):
                with s.Fori(0, 2) as i:
                    def squares(c):
                        s.wait_ge(uv_ev, i * 12 + (c + 1))
                        s.wait_ge(uv_sq, i * 12 + c)
                        for t in range(5):
                            r = rows_of(t)
                            src = v[:, t, bass.ds(i * (12 * P) + c * P, P)] if t < NT else \
                                VS[:, bass.ds(i * (12 * P) + c * P, P)]
                            ins = s.activation(gtmp[0:r, t % 2, (t // 2) * P:(t // 2 + 1) * P],
                                               src, ACT.Square,
                                               accum_out=vss[0:r, t, bass.ds(i * 12 + c, 1)])
                        ins.then_inc(uv_sq, 1)

                    for c in range(12):
                        s.wait_ge(uv_mm, i * 12 + (24 * part + c + 1))
                        if part == 1:
                            s.wait_ge(uv_tp, i * 12 + max(c - 1, 0))
                        bank = 2 * (c % 2)
                        dst = vtmp[:, c % 2, :] if part else u[:, bass.ds(i * 12 + c, 1), :]\
                            .rearrange("p o t -> p (o t)")
                        s.activation(dst.rearrange("p (h t) -> p h t", h=2), ps[:, bank:bank + 2, 0:HALF],
                                     ACT.Gelu_apprx_tanh).then_inc(uv_gelu, 1)
                        if part == 1 and c >= 1:
                            squares(c - 1)
                    if part == 1:
                        squares(11)
            s.wait_ge(gate_var, 1)
            s.activation(root[:, 0:5], ss[:, :], ACT.Sqrt).then_inc(gate_root, 1)
            s.wait_ge(gate_rs, 1)
            for t in (1, 3):
                s.activation(v[:, t, :], v[:, t, :], ACT.Copy, scale=rstd[:, t:t + 1]).then_inc(gate_vn_a, 1)
            with s.Fori(0, 4) as i:
                for k in range(2):
                    s.wait_ge(back_mm, i * 2 + (k + 1))
                    s.wait_ge(back_tp, i * 2)
                    s.activation(vtmp[:, k, :].rearrange("p (h t) -> p h t", h=2),
                                 ps[:, 2 * k:2 * k + 2, 0:HALF], ACT.Copy).then_inc(back_cp, 1)

            def moe_a(layer):
                o, before = ovfs[layer], layer * NE
                s.wait_ge(moe_rt, 2 * layer + 1)
                s.activation(R["eg"], R["eg"], ACT.Exp).then_inc(moe_ex, 1)
                s.wait_ge(moe_rt, 2 * layer + 2)
                s.activation(R["e2"], R["e2"], ACT.Exp).then_inc(moe_ex, 1)

                def silu(i, k):
                    s.wait_ge(moe_gu, i * 2 + (before + k + 1))
                    s.activation(sg[:, k % 2].rearrange("p f s -> p (f s)"), ps[:, 2 + k % 2, 0:2 * SLOTS], ACT.Silu)\
                        .then_inc(moe_silu, 1)

                def y_half(i, k):
                    s.wait_ge(moe_dn, i * 2 + (before + k + 1))
                    s.wait_ge((moe_st0, moe_st1)[k % 2], i * 16 + (8 * before + k // 2 * 16))
                    s.activation(ye[0:SLOTS, k % 2, 0:512], ps[0:SLOTS, 4 + 2 * (k % 2), :], ACT.Copy)\
                        .then_inc(moe_ya, 1)

                silu(0, 0)
                for k in (1, 2):
                    silu(0, k)
                    y_half(0, k - 1)
                with s.Fori(0, 6) as i:
                    for k in range(2):
                        silu(i, 3 + k)
                        y_half(i, 2 + k)
                silu(0, 15)
                y_half(0, 14)
                y_half(0, 15)
                n_ovf = s.value_load(ovf_i[0:1, 0:1], min_val=0, max_val=OVF)
                with s.If(n_ovf > 0):
                    wg = a["w_e_gate"][layer].rearrange("e (p c) f -> e p (c f)", c=DC)
                    wu = a["w_e_up"][layer].rearrange("e (p c) f -> e p (c f)", c=DC)
                    wd = a["w_e_down"][layer].rearrange("e (f p) n -> e p f n", p=P)
                    s.wait_ge(moe_st0, 16 * (before + NE) // 2)
                    with s.Fori(0, OVF) as t:
                        e = s.value_load(ovf_i[0:1, bass.ds(t + 1, 1)], min_val=0, max_val=NE - 1)
                        s.dma_start(ow[:, 0, :], wg[bass.ds(e, 1)].rearrange("o p f -> (o p) f")).then_inc(o["ld"], 16)
                        s.dma_start(ow[:, 1, :], wu[bass.ds(e, 1)].rearrange("o p f -> (o p) f")).then_inc(o["ld"], 16)
                        s.dma_start(ow[:, 2, :].rearrange("p (f n) -> p f n", f=2),
                                    wd[bass.ds(e, 1)].rearrange("o p f n -> (o p) f n")).then_inc(o["ld"], 16)
                        here = slots_dram[bass.ds(t * SLOTS + NE * SLOTS, SLOTS), :]
                        s.dma_start(xs[0:SLOTS, 0].rearrange("p c f -> p (c f)"), here).then_inc(o["ld"], 16)
                        s.wait_ge(o["gu"], t + 1)
                        s.activation(sg[:, 0].rearrange("p f s -> p (f s)"), ps[:, 2, 0:2 * SLOTS], ACT.Silu)\
                            .then_inc(o["silu"], 1)
                        s.wait_ge(o["dn"], t + 1)
                        s.activation(ye[0:SLOTS, 0, 0:512], ps[0:SLOTS, 4, :], ACT.Copy).then_inc(o["y"], 1)
                        s.wait_ge(o["y"], t * 2 + 2)
                        s.dma_start(here, ye[0:SLOTS, 0, :]).then_inc(o["st"], 16)
                        s.wait_ge(o["st"], t * 16 + 16)
                s.sem_inc(moe_over, 1)

            norm_a(1, lambda e, t: e.wait_ge(back_add, DC) if t == 0 else None)
            moe_a(0)
            norm_a(2, lambda e, t: e.wait_ge(moe_comb, t + 1))
            for n in range(3 * DC):
                kind, h = divmod(n, DC)
                s.wait_ge(kvq_mm, n + 1)
                if n >= 2 * DC + 2:
                    s.wait_ge(kvq_tp, n - 1)
                dst = (qT[:, h, :], kT[:, h, :], vtmp[:, n % 2, :])[kind]
                bank = 2 * (n % 2)
                s.activation(dst.rearrange("p (h t) -> p h t", h=2), ps[:, bank:bank + 2, 0:HALF], ACT.Copy)\
                    .then_inc(kvq_cp, 1)
            def make_bias(h):
                if h >= 2:
                    s.wait_ge(att_neg, 4 * (h - 1))
                s.activation(bias8[:, h % 2, :], c_["dist"], ACT.Copy, scale=-8.0 * 2.0 ** -(h + 1))\
                    .then_inc(att_bias, 1)

            make_bias(0)
            steps = NH * NT
            for k in range(steps + 2):
                if k < steps:
                    h, q = divmod(k, NT)
                    w = (q + 1) * P
                    if q == 1 and h + 1 < NH:
                        make_bias(h + 1)
                    s.wait_ge(att_neg, k + 1)
                    for mp in range(2):
                        ins = s.activation(st[:, k % 3, mp * SEQ:mp * SEQ + w], st[:, k % 3, mp * SEQ:mp * SEQ + w],
                                           ACT.Exp, bias=nm[:, k % 2, mp:mp + 1],
                                           accum_out=zz[:, k % 2, mp:mp + 1])
                    ins.then_inc(att_ex, 1)
                if k == DEC_JOIN:
                    s.wait_ge(dec_aTp, 1)
                    s.activation(daT.rearrange("p g c -> p (g c)"), ps[:, 6 + k % 2, 0:PAGES * NB * NH], ACT.Copy)
                    s.activation(daown, ps[0:NB * NH, 6 + k % 2, 256:257], ACT.Copy).then_inc(dec_aT, 1)
                if k in DEC_STEPS:
                    b = DEC_STEPS.index(k)
                    s.wait_ge(dec_pv, b + 1)
                    s.activation(doT[:, b * NH:(b + 1) * NH], ps[:, 6 + k % 2, 0:NH], ACT.Copy).then_inc(dec_o, 1)
                if 1 <= k <= steps:
                    n = k - 1
                    w = (n % NT + 1) * P
                    s.wait_ge(att_tp, n + 1)
                    if n >= 2:
                        s.wait_ge(att_pv, n - 1)
                    s.activation(aT[:, n % 2, 0:w], ps[:, 4 + n % 2, 0:w], ACT.Copy).then_inc(att_aT, 1)
                if k >= 2:
                    n = k - 2
                    h, q = divmod(n, NT)
                    s.wait_ge(att_pv, n + 1)
                    s.activation(otok[:, q, h * P:(h + 1) * P], ps[:, 6 + n % 2, 0:P], ACT.Copy,
                                 scale=rz[:, n % 4, 0:1])
                    if n >= 1:
                        s.wait_ge(att_o, n)
                    s.activation(osq, ps[:, 6 + n % 2, 0:P], ACT.Square, scale=rz[:, n % 4, 0:1],
                                 accum_out=oss[:, q, h:h + 1]).then_inc(att_o, 1)
                if k == DEC_JOIN - 2:
                    s.wait_ge(dec_max, 1)
                    s.activation(dS, dS, ACT.Exp, bias=dsm[:, 2:3], accum_out=dsm[:, 3:4]).then_inc(dec_ex, 1)
            s.wait_ge(att_var, 1)
            s.activation(root[:, 0:NT * NH], oss.rearrange("p t h -> p (t h)"), ACT.Sqrt).then_inc(att_root, 1)
            for t in range(NT):
                for half in range(2):
                    s.wait_ge(att_tp2, 2 * t + half + 1)
                    s.activation(oT[:, 4 * half:4 * half + 4, t * P:(t + 1) * P],
                                 ps[:, (2 * t + half) % 4, :].rearrange("p (c f) -> p c f", c=4), ACT.Copy,
                                 scale=subg[:, 0:1]).then_inc(att_ev, 1)
                if t == 0:
                    s.wait_ge(dec_sq, 1)
                    s.activation(dsm[0:64, 9:10], dsm[0:64, 8:9], ACT.Sqrt).then_inc(dec_root, 1)
            s.wait_ge(dec_otp2, 1)
            s.activation(oT[:, :, SEQ:T], ps[:, 7, 0:NB * NH].rearrange("p (b h) -> p h b", b=NB), ACT.Copy,
                         scale=subg[:, 0:1]).then_inc(dec_ev, 1)
            for n in range(DC):
                s.wait_ge(back_mm, DC + n + 1)
                if n >= 2:
                    s.wait_ge(back_tp, DC + n - 1)
                s.activation(vtmp[:, n % 2, :].rearrange("p (h t) -> p h t", h=2),
                             ps[:, 2 * (n % 2):2 * (n % 2) + 2, 0:HALF], ACT.Copy).then_inc(back_cp, 1)
            norm_a(3, lambda e, t: e.wait_ge(back_add, 2 * DC) if t == 0 else None)
            moe_a(1)
            norm_a(4, lambda e, t: e.wait_ge(moe_comb, 5 + t + 1), normed=False)

        @block.tensor
        def _(pe):
            def product(pair, w, c0, rhs, done=None, first=True, last=True):
                for c in range(DC):
                    for half in range(2):
                        ins = pe.matmul(ps[:, 2 * pair + half, 0:HALF], w[:, c, c0:c0 + P],
                                        rhs(c, half), start=first and c == 0, stop=last and c == DC - 1)
                if done is not None:
                    ins.then_inc(done, 1)

            def of(t):
                return lambda c, half: t[:, c, half * HALF:(half + 1) * HALF]

            def turn(src, bank, sbank, prompt=True):
                if prompt:
                    for t in range(NT):
                        pe.transpose(ps[:, bank, t * P:(t + 1) * P], src[:, t * P:(t + 1) * P], ident)
                return pe.transpose(ps[0:NB, sbank, 0:P], src[:, SEQ:T], ident)

            def norm_t(n, evs, passes=1):
                for t in range(5):
                    pe.wait_ge(norm_xn, 5 * n + t + 1)
                    r = rows_of(t)
                    if t == NT:
                        for c in range(DC):
                            ins = pe.transpose(ps[:, 4, c * NB:(c + 1) * NB], xn[0:r, t, c, :], ident[0:r, 0:r])
                        ins.then_inc(norm_tp, 1)
                        continue
                    for half in range(2):
                        if t >= 2:
                            pe.wait_ge(norm_ev, evs + passes * (2 * (t - 2) + half + 1))
                        for c in range(4):
                            ins = pe.transpose(ps[:, 2 * (t % 2) + half, c * P:(c + 1) * P],
                                               xn[:, t, 4 * half + c, :], ident)
                        ins.then_inc(norm_tp, 1)

            pe.wait_ge(ld_c, 16)
            pe.wait_ge(ld_w, 16 * N_SMALL)
            for g in range(NG):
                ins = pe.transpose(ps[:, 5 + g // 4, (g % 4) * P:(g % 4 + 1) * P], w_st[:, g, :], ident)
            ins = pe.transpose(ps[:, 7, 0:GC], sg_st, ident[0:GC, 0:GC])
            ins.then_inc(prep_tp, 1)
            norm_t(0, 0)
            pe.wait_ge(norm_ev, 9)
            pe.wait_ge(prep_v, 1)
            for part in range(2):
                with pe.Fori(0, 2) as i:
                    def turn_v(c):
                        pe.wait_ge(uv_gelu, i * 12 + (24 + c + 1))
                        pe.wait_ge(uv_ev, i * 12 + max(c - 1, 0))
                        turn(vtmp[:, c % 2, :], 4 + c % 2, 6 + c % 2).then_inc(uv_tp, 1)

                    for c in range(12):
                        b = UV0 + 12 * part + c // 2
                        if c % 2 == 0:
                            slot_loaded(pe, b, i)
                        if part == 0:
                            pe.wait_ge(uv_gelu, i * 12 + max(c - 1, 0))
                        else:
                            pe.wait_ge(uv_gelu, i * 12 + (24 + c - 1))
                        product(c % 2, ringslot(b, (DC, 256)), (c % 2) * P, of(hT), uv_mm)
                        if part == 1 and c >= 1:
                            turn_v(c - 1)
                    if part == 1:
                        turn_v(11)
            pe.wait_ge(gate_vn_v, 2)
            pe.wait_ge(gate_vn_a, 2)
            for j in range(GC):
                if j >= 4:
                    pe.wait_ge(gate_tmp, j - 3)
                for t in range(NT):
                    ins = pe.matmul(ps[:, j % 4, t * P:(t + 1) * P], v[:, t, j * P:(j + 1) * P],
                                    wT[:, j * P // GCOLS, :], start=True, stop=True)
                ins.then_inc(gate_sp, 1)
                if j == 3:
                    pe.wait_ge(gate_s, 1)
                    for k in range(GC):
                        ins = pe.transpose(ps[:, 4, k * NB:(k + 1) * NB], gainb[:, k * P:(k + 1) * P],
                                           ident[0:NB, 0:NB])
                    ins.then_inc(gate_tp, 1)
            pe.wait_ge(gate_u, GC)
            pe.wait_ge(gate_su, 1)
            with pe.Fori(0, 4) as i:
                for k in range(2):
                    pe.wait_ge(back_cp, i * 2)
                    for kb in range(3):
                        b = GO0 + 3 * k + kb
                        slot_loaded(pe, b, i)
                        product(k, ringslot(b, (DC, P)), 0,
                                lambda c, half: u[:, 8 * kb + c, half * HALF:(half + 1) * HALF],
                                back_mm if kb == 2 else None, kb == 0, kb == 2)
                for k in range(2):
                    pe.wait_ge(back_cp, i * 2 + (k + 1))
                    pe.wait_ge(back_add, i * 2)
                    turn(vtmp[:, k, :], 4 + k, 6 + k).then_inc(back_tp, 1)

            def moe_t(layer):
                o, before = ovfs[layer], layer * NE
                for t in range(5):
                    for c in range(DC):
                        ins = pe.matmul(ps[0:rows_of(t), 5, t * 20:(t + 1) * 20], hT[:, c, cols_of(t)],
                                        wr[:, layer, c, :], start=c == 0, stop=c == DC - 1)
                ins.then_inc(moe_lg, 1)
                pe.wait_ge(moe_mk, layer + 1)
                for t in range(5):
                    for q in range(t + 1):
                        pe.matmul(ps[:, 6, t * NE:(t + 1) * NE], c_["tri"] if q == t else ones,
                                  R["m"][:, q, :], start=q == 0, stop=q == t)
                for q in range(5):
                    ins = pe.matmul(ps[:, 6, 5 * NE:6 * NE], ones, R["m"][:, q, :], start=q == 0, stop=q == 4)
                ins.then_inc(moe_cum, 1)

                def turn_rows(i, k):
                    pe.wait_ge((moe_ld0, moe_ld1)[k % 2], i * 16 + (8 * before + k // 2 * 16 + 16))
                    if not (isinstance(i, int) and k == 0):
                        pe.wait_ge(moe_tev, i * 2 + (before + k))
                    for c in range(DC):
                        ins = pe.transpose(ps[:, c // 4, (c % 4) * SLOTS:(c % 4 + 1) * SLOTS],
                                           xs[0:SLOTS, k % 2, c, :], ident[0:SLOTS, 0:SLOTS])
                    ins.then_inc(moe_tp, 1)

                def gate_up(i, k, b):
                    q = k % 2
                    slot_loaded(pe, b, i)
                    slot_loaded(pe, b + 1, i)
                    pe.wait_ge(moe_tev, i * 2 + (before + k + 1))
                    if k >= 1:
                        pe.wait_ge(moe_hid, i * 2 + (before + k - 1))
                    for f in range(4):
                        w = ringslot(b + f // 2, (DC, DE))
                        for c in range(DC):
                            ins = pe.matmul(ps[:, 2 + q, f * SLOTS:(f + 1) * SLOTS],
                                            w[:, c, (f % 2) * P:(f % 2 + 1) * P], xsT[:, q, c, :],
                                            start=c == 0, stop=c == DC - 1)
                    ins.then_inc(moe_gu, 1)

                def down(i, k, b):
                    q = k % 2
                    slot_loaded(pe, b, i)
                    pe.wait_ge(moe_hid, i * 2 + (before + k + 1))
                    if isinstance(i, int) and k >= 2:
                        pe.wait_ge(moe_ya, before + k - 1)
                        pe.wait_ge(moe_yv, before + k - 1)
                    if not isinstance(i, int):
                        pe.wait_ge(moe_ya, i * 2 + (before + max(k - 1, 0)))
                        pe.wait_ge(moe_yv, i * 2 + (before + max(k - 1, 0)))
                    w = ringslot(b, (2, D))
                    for half in range(2):
                        for f in range(2):
                            ins = pe.matmul(ps[0:SLOTS, 4 + 2 * q + half, :], hid[:, q, f, :],
                                            w[:, f, half * 512:(half + 1) * 512], start=f == 0, stop=f == 1)
                    ins.then_inc(moe_dn, 1)

                base = MOE0 if layer == 0 else MOE1
                turn_rows(0, 0)
                gate_up(0, 0, base)
                turn_rows(0, 1)
                pe.wait_ge(moe_idx, layer + 1)
                gate_up(0, 1, base + 2)
                down(0, 0, base + 4)
                turn_rows(0, 2)
                gate_up(0, 2, base + 5)
                down(0, 1, base + 7)
                turn_rows(0, 3)
                with pe.Fori(0, 6) as i:
                    for k in range(2):
                        b = base + 8 + 3 * k
                        gate_up(i, 3 + k, b)
                        down(i, 2 + k, b + 2)
                        turn_rows(i, 4 + k)
                gate_up(0, 15, base + 44)
                down(0, 14, base + 46)
                down(0, 15, base + 47)
                n_ovf = pe.value_load(ovf_i[0:1, 0:1], min_val=0, max_val=OVF)
                with pe.If(n_ovf > 0):
                    with pe.Fori(0, OVF) as t:
                        pe.wait_ge(o["ld"], t * 64 + 64)
                        for c in range(DC):
                            ins = pe.transpose(ps[:, c // 4, (c % 4) * SLOTS:(c % 4 + 1) * SLOTS],
                                               xs[0:SLOTS, 0, c, :], ident[0:SLOTS, 0:SLOTS])
                        ins.then_inc(o["tp"], 1)
                        pe.wait_ge(o["tev"], t + 1)
                        for f in range(4):
                            w = ow[:, f // 2, :].rearrange("p (c n) -> p c n", c=DC)
                            for c in range(DC):
                                ins = pe.matmul(ps[:, 2, f * SLOTS:(f + 1) * SLOTS],
                                                w[:, c, (f % 2) * P:(f % 2 + 1) * P], xsT[:, 0, c, :],
                                                start=c == 0, stop=c == DC - 1)
                        ins.then_inc(o["gu"], 1)
                        pe.wait_ge(o["hid"], t + 1)
                        w = ow[:, 2, :].rearrange("p (f n) -> p f n", f=2)
                        for half in range(2):
                            for f in range(2):
                                ins = pe.matmul(ps[0:SLOTS, 4 + half, :], hid[:, 0, f, :],
                                                w[:, f, half * 512:(half + 1) * 512], start=f == 0, stop=f == 1)
                        ins.then_inc(o["dn"], 1)

            norm_t(1, 9)
            pe.wait_ge(norm_ev, 18)
            moe_t(0)
            norm_t(2, 18, 2)
            pe.wait_ge(norm_ev, 18 + 18)

            def turn_kvq(n):
                kind, h = divmod(n, DC)
                pe.wait_ge(kvq_cp, n + 1)
                if n >= 2:
                    pe.wait_ge(kvq_ev, n - 1)
                src = (qT[:, h, :], kT[:, h, :], vtmp[:, n % 2, :])[kind]
                turn(src, 4 + n % 2, 6 + n % 2, kind > 0).then_inc(kvq_tp, 1)

            for n in range(3 * DC):
                if n % 2 == 0:
                    slot_loaded(pe, kvq_block(n // 2))
                if n >= 2:
                    pe.wait_ge(kvq_cp, n - 1)
                product(n % 2, ringslot(kvq_block(n // 2), (DC, 256)), (n % 2) * P,
                        of(hqT if n < DC else hT), kvq_mm)
                if n >= 1:
                    turn_kvq(n - 1)
            turn_kvq(3 * DC - 1)
            pe.wait_ge(kvq_cp, 3 * DC)
            pe.wait_ge(kvq_ev, 3 * DC)
            steps = NH * NT
            for k in range(steps + 3):
                if k < steps:
                    h, q = divmod(k, NT)
                    if k >= 2:
                        pe.wait_ge(att_neg, k - 1)
                    for mp in range(2):
                        ins = pe.matmul(ps[:, 2 * (k % 2) + mp, 0:(q + 1) * P],
                                        qT[mp * HD:(mp + 1) * HD, h, q * P:(q + 1) * P],
                                        kT[mp * HD:(mp + 1) * HD, h, 0:(q + 1) * P], start=True, stop=True)
                    ins.then_inc(att_qk, 1)
                if 2 <= k < steps + 2:
                    n = k - 2
                    pe.wait_ge(att_a, n + 1)
                    if n >= 2:
                        pe.wait_ge(att_aT, n - 1)
                    for c in range(n % NT + 1):
                        ins = pe.transpose(ps[:, 4 + n % 2, c * P:(c + 1) * P], st[:, n % 3, c * P:(c + 1) * P],
                                           ident)
                    ins.then_inc(att_tp, 1)
                if k >= 3:
                    n = k - 3
                    h, q = divmod(n, NT)
                    pe.wait_ge(att_aT, n + 1)
                    if n >= 2:
                        pe.wait_ge(att_o, n - 1)
                    if n == 0:
                        pe.wait_ge(dec_max0, 1)
                    if k - 1 == DEC_JOIN:
                        pe.wait_ge(dec_aT, 1)
                    if k - 1 in DEC_STEPS:
                        pe.wait_ge(dec_o, DEC_STEPS.index(k - 1) + 1)
                    for c in range(q + 1):
                        ins = pe.matmul(ps[:, 6 + n % 2, 0:P], aT[:, n % 2, c * P:(c + 1) * P],
                                        vtok[:, c, h * P:(h + 1) * P], start=c == 0, stop=c == q)
                    ins.then_inc(att_pv, 1)
                if k == 0:
                    pe.wait_ge(dec_red, NB * PAGES)
                    for c in range(PAGES):
                        ins = pe.transpose(ps[:, 6, c * P:(c + 1) * P], sK[:, c, :], ident)
                    ins.then_inc(dec_tp, 1)
                if k == DEC_JOIN:
                    pe.wait_ge(dec_c, 1)
                    pe.wait_ge(att_o, k - 3)
                    for c in range(PAGES):
                        pe.matmul(ps[:, 6 + k % 2, c * 64:(c + 1) * 64], dS[:, c * P:(c + 1) * P], dC,
                                  start=True, stop=True)
                    pe.matmul(ps[0:64, 6 + k % 2, 256:257], dC, dS[:, SEQ:SEQ + 1], start=True, stop=True)\
                        .then_inc(dec_aTp, 1)
                if k in DEC_STEPS:
                    b = DEC_STEPS.index(k)
                    pe.wait_ge(att_o, k - 3)
                    slot_loaded(pe, VP0 + 2 * b)
                    slot_loaded(pe, VP0 + 2 * b + 1)
                    for h in range(NH):
                        for c in range(PAGES):
                            ins = pe.matmul(ps[:, 6 + k % 2, h:h + 1],
                                            ringslot(VP0 + 2 * b + c // 2, (2, D))[:, c % 2, h * P:(h + 1) * P],
                                            daT[:, c, b * NH + h:b * NH + h + 1], start=c == 0, stop=c == PAGES - 1)
                    ins.then_inc(dec_pv, 1)
            pe.wait_ge(dec_o, NB)
            pe.wait_ge(att_o, steps)
            pe.transpose(ps[0:64, 6, 0:P], doT, ident).then_inc(dec_otp, 1)
            pe.wait_ge(att_neg, steps)
            for t in range(NT):
                pe.wait_ge(att_on, t + 1)
                for half in range(2):
                    if t >= 2:
                        pe.wait_ge(att_ev, 2 * (t - 2) + half + 1)
                    for c in range(4):
                        ins = pe.transpose(ps[:, (2 * t + half) % 4, c * P:(c + 1) * P],
                                           otok[:, t, (4 * half + c) * P:(4 * half + c + 1) * P], ident)
                    ins.then_inc(att_tp2, 1)
            pe.wait_ge(dec_o2, 1)
            pe.transpose(ps[:, 7, 0:64], do64, ident[0:64, 0:64]).then_inc(dec_otp2, 1)
            pe.wait_ge(dec_ev, 1)
            pe.wait_ge(att_ev, 2 * NT)

            def turn_back(n):
                pe.wait_ge(back_cp, DC + n + 1)
                if n >= 2:
                    pe.wait_ge(back_add, DC + n - 1)
                turn(vtmp[:, n % 2, :], 4 + n % 2, 6 + n % 2).then_inc(back_tp, 1)

            for n in range(DC):
                if n % 2 == 0:
                    slot_loaded(pe, AO0 + n // 2)
                if n >= 2:
                    pe.wait_ge(back_cp, DC + n - 1)
                product(n % 2, ringslot(AO0 + n // 2, (DC, 256)), (n % 2) * P, of(oT), back_mm)
                if n >= 1:
                    turn_back(n - 1)
            turn_back(DC - 1)
            norm_t(3, 36)
            pe.wait_ge(norm_ev, 45)
            moe_t(1)

        @block.vector
        def _(e):
            def norm_v(n, ready, gain, into, normed=True):
                for t in (1, 3):
                    ready(e, t)
                    e.tensor_tensor_reduce(xn[:, t].rearrange("p c f -> p (c f)"), x[:, t, :], x[:, t, :], 1.0, 0.0,
                                           ALU.mult, ALU.add, ss[:, t:t + 1]).then_inc(norm_sq_v, 1)
                e.wait_ge(norm_sq_a, 3 * n + 3)
                e.wait_ge(norm_sq_v, 2 * n + 2)
                e.tensor_scalar(ss[:, :], ss[:, :], 1.0 / D, EPS, ALU.mult, ALU.add).then_inc(norm_var, 1)
                e.wait_ge(norm_root, n + 1)
                e.reciprocal(rstd[:, :], root[:, 0:5]).then_inc(norm_rs, 1)
                if not normed:
                    return
                before = (0, 9, 18, 27)[n]
                for t in range(5):
                    for half in range(2 if t < NT else 1):
                        e.wait_ge(norm_tp, before + 2 * t + half + 1)
                        for g_row, dst in zip(gain, into):
                            if t < NT:
                                src = ps[:, 2 * (t % 2) + half, :].rearrange("p (c f) -> p c f", c=4)
                                to = dst[:, 4 * half:4 * half + 4, t * P:(t + 1) * P]
                                gb = gains[:, g_row, 4 * half:4 * half + 4].unsqueeze(2).broadcast_to([P, 4, P])
                            else:
                                src = ps[:, 4, 0:DC * NB].rearrange("p (c f) -> p c f", c=DC)
                                to = dst[:, :, SEQ:T]
                                gb = gains[:, g_row, :].unsqueeze(2).broadcast_to([P, DC, NB])
                            e.tensor_tensor(to, src, gb, ALU.mult).then_inc(norm_ev, 1)

            e.memset(ss[:, :], 1.0)
            e.memset(vss[:, :, :], 0.0).then_inc(prep_init, 1)
            e.wait_ge(prep_init, 1)
            norm_v(0, lambda q, t: (q.wait_ge(ld_x[t], 16), q.wait_ge(ld_w, 16 * N_SMALL)), [0], [hT])
            e.wait_ge(ld_c, 16)
            e.wait_ge(prep_tp, 1)
            for half in range(2):
                e.tensor_tensor(wT[:, 4 * half:4 * half + 4, :],
                                ps[:, 5 + half, :].rearrange("p (g t) -> p g t", g=4),
                                c_["causal"].unsqueeze(1).broadcast_to([P, 4, P]), ALU.mult)
            e.tensor_copy(sgain[:, :], ps[:, 7, 0:GC])
            for layer in range(2):
                e.tensor_copy(wr[:, layer, :, 0:NEG], wrg_st[:, layer, :].rearrange("p (c g) -> p c g", c=DC))
                for q in range(NEG):
                    e.tensor_copy(wr[:, layer, :, NEG + 4 * q:NEG + 4 * q + 4],
                                  wre_st[:, layer, q, :].rearrange("p (c k) -> p c k", c=DC))
            link(e, e.tensor_tensor(lam_st[:, 0, :], lam_st[:, 0, :], lam_st[:, 1, :], ALU.mult))
            e.tensor_reduce(lam_s[:, 0:2], lam_st[:, 0, :].rearrange("p (m d) -> p m d", m=2), AX_X, ALU.add)\
                .then_inc(prep_lam, 1)
            e.wait_ge(prep_lame, 1)
            link(e, e.tensor_tensor(lam_s[:, 4:5], lam_s[:, 3:4], lam_s[:, 2:3], ALU.subtract))
            e.tensor_scalar(neglam[:, :], lam_s[:, 4:5], -LAM_INIT, None, ALU.add)
            e.tensor_scalar(subg[:, :], subg[:, :], 1.0 - LAM_INIT, None, ALU.mult).then_inc(prep_v, 1)

            e.wait_ge(zeroed, 16 * -(-ROWS // P))
            with e.Fori(0, 2) as i:
                for c in range(12):
                    e.wait_ge(uv_tp, i * 12 + (c + 1))
                    e.tensor_copy(v[:, :, bass.ds(i * (12 * P) + c * P, P)],
                                  ps[:, 4 + c % 2, :].rearrange("p (t f) -> p t f", t=NT))
                    e.tensor_copy(VS[:, bass.ds(i * (12 * P) + c * P, P)], ps[0:NB, 6 + c % 2, 0:P])\
                        .then_inc(uv_ev, 1)
            e.wait_ge(uv_sq, GC)
            link(e, e.tensor_reduce(ss[:, :], vss[:, :, :], AX_X, ALU.add))
            e.tensor_scalar(ss[:, :], ss[:, :], 1.0 / DG, EPS, ALU.mult, ALU.add).then_inc(gate_var, 1)
            e.wait_ge(gate_root, 1)
            e.reciprocal(rstd[:, :], root[:, 0:5]).then_inc(gate_rs, 1)
            e.wait_ge(gate_rs, 1)
            for t in (0, 2):
                e.tensor_scalar(v[:, t, :], v[:, t, :], rstd[:, t:t + 1], None, ALU.mult).then_inc(gate_vn_v, 1)
            e.wait_ge(gate_gb, 16)
            e.scalar_tensor_tensor(VS, VS, rstd[0:NB, 4:5], gainb, ALU.mult, ALU.mult).then_inc(gate_vs, 1)
            e.wait_ge(gate_vs, 1)
            for g in range(NG):
                ins = e.tensor_scalar(gainb[:, g * GCOLS:(g + 1) * GCOLS], VS[:, g * GCOLS:(g + 1) * GCOLS],
                                      w00[:, 0, g:g + 1], w00[:, 1, g:g + 1], ALU.mult, ALU.add)
            ins.then_inc(gate_s, 1)
            e.wait_ge(ld_bs, 16)
            for j in range(GC):
                e.wait_ge(gate_sp, j + 1)
                if j >= 2:
                    e.wait_ge(gate_u, j - 1)
                e.scalar_tensor_tensor(gtmp[:, j % 2, :].rearrange("p (t f) -> p t f", t=NT),
                                       ps[:, j % 4, :].rearrange("p (t f) -> p t f", t=NT), sgain[:, j:j + 1],
                                       bsg[:, j * P // GCOLS, :].unsqueeze(1).broadcast_to([P, NT, P]),
                                       ALU.mult, ALU.add).then_inc(gate_tmp, 1)
                if j == 5:
                    e.wait_ge(gate_tp, 1)
                    e.tensor_tensor(u[:, :, SEQ:T], ps[:, 4, 0:GC * NB].rearrange("p (j b) -> p j b", b=NB),
                                    u[:, :, SEQ:T], ALU.mult).then_inc(gate_su, 1)

            def add_chunk(n, q):
                e.tensor_tensor(x[:, 0:NT, n], x[:, 0:NT, n], ps[:, 4 + q, :].rearrange("p (t f) -> p t f", t=NT),
                                ALU.add)
                e.tensor_tensor(x[0:NB, NT, n], x[0:NB, NT, n], ps[0:NB, 6 + q, 0:P], ALU.add)\
                    .then_inc(back_add, 1)

            e.wait_ge(again_x, 16 * 5)
            with e.Fori(0, 4) as i:
                for k in range(2):
                    e.wait_ge(back_tp, i * 2 + (k + 1))
                    add_chunk(bass.ds(i * (2 * P) + k * P, P), k)

            def moe_v(layer):
                o, before = ovfs[layer], layer * NE
                grow = 2 + layer
                L, oh, cand = R["l"], R["oh"], R["cand"]

                def first_max(vals, top, onehot, k=NEG):
                    link(e, e.tensor_reduce(top, vals, AX_X, ALU.max))
                    link(e, e.tensor_tensor(cand, vals, top.unsqueeze(2).broadcast_to([P, 5, NEG]), ALU.is_ge))
                    link(e, e.scalar_tensor_tensor(cand, cand, -99.0, iota99, ALU.mult, ALU.add))
                    link(e, e.tensor_reduce(R["least"], cand, AX_X, ALU.min))
                    link(e, e.tensor_tensor(onehot, iota, R["least"].unsqueeze(2).broadcast_to([P, 5, NEG]),
                                            ALU.is_equal))

                iota = c_["iota"].unsqueeze(1).broadcast_to([P, 5, NEG])
                iota99 = c_["iota99"].unsqueeze(1).broadcast_to([P, 5, NEG])
                link(e, e.memset(R["l"][:, NT, :], 0.0))
                e.wait_ge(moe_lg, layer + 1)
                e.tensor_tensor(L[:, 0:NT, :], ps[:, 5, 0:NT * 20].rearrange("p (t k) -> p t k", t=NT),
                                rbias[:, layer, :].unsqueeze(1).broadcast_to([P, NT, 20]), ALU.add)
                link(e, e.tensor_tensor(L[0:NB, NT, :], ps[0:NB, 5, NT * 20:5 * 20], rbias[0:NB, layer, :], ALU.add))
                first_max(L[:, :, 0:NEG], R["gmax"], oh)
                e.tensor_tensor(R["eg"], L[:, :, 0:NEG],
                                R["gmax"].unsqueeze(2).broadcast_to([P, 5, NEG]), ALU.subtract).then_inc(moe_rt, 1)
                link(e, e.tensor_tensor(
                    R["pick"].rearrange("p t (k g) -> p t k g", g=NEG),
                    L[:, :, NEG:20].rearrange("p t (g k) -> p t k g", g=NEG),
                    oh.unsqueeze(2).broadcast_to([P, 5, NEG, NEG]), ALU.mult))
                link(e, e.tensor_reduce(R["el"], R["pick"].rearrange("p t (k g) -> p t k g", g=NEG), AX_X, ALU.add))
                first_max(R["el"], R["m1"], R["oh1"])
                link(e, e.scalar_tensor_tensor(R["el2"], R["oh1"], -BIG, R["el"], ALU.mult, ALU.add))
                first_max(R["el2"], R["m2"], R["oh2"])
                e.tensor_tensor(R["e2"], R["m2"], R["m1"], ALU.subtract).then_inc(moe_rt, 1)
                for j, name in enumerate(("oh1", "oh2")):
                    link(e, e.tensor_tensor(
                        R["mm"][:, j].rearrange("p t (g k) -> p t g k", g=NEG),
                        oh.unsqueeze(3).broadcast_to([P, 5, NEG, NEG]),
                        R[name].unsqueeze(2).broadcast_to([P, 5, NEG, NEG]), ALU.mult))
                for j in range(2):
                    link(e, e.tensor_scalar(R["mm"][:, j, NT, :], R["mm"][:, j, NT, :], c_["valid"], None, ALU.mult))
                e.tensor_tensor(R["m"], R["mm"][:, 0], R["mm"][:, 1], ALU.add).then_inc(moe_mk, 1)
                e.wait_ge(moe_ex, 2 * layer + 2)
                link(e, e.tensor_reduce(R["gs"], R["eg"], AX_X, ALU.add))
                link(e, e.tensor_scalar(R["den"], R["e2"], 1.0, None, ALU.add))
                link(e, e.tensor_tensor(R["den"], R["den"], R["gs"], ALU.mult))
                link(e, e.reciprocal(R["den"], R["den"]))
                e.tensor_copy(pair_w[:, :, 0], R["den"])
                e.tensor_tensor(pair_w[:, :, 1], R["den"], R["e2"], ALU.mult)
                e.wait_ge(moe_cum, layer + 1)
                cnt = ps[:, 6, 5 * NE:6 * NE]
                link(e, e.tensor_scalar(R["ov"], cnt, float(SLOTS), None, ALU.is_gt))
                for q in range(2, MAXT + 1):
                    link(e, e.tensor_scalar(R["ov1"], cnt, float(q * SLOTS), None, ALU.is_gt))
                    link(e, e.tensor_tensor(R["ov"], R["ov"], R["ov1"], ALU.add))
                lt = c_["lt"].rearrange("p (a b) -> p a b", a=NE)
                link(e, e.tensor_tensor(R["big"], lt,
                                        R["ov"].unsqueeze(1).broadcast_to([P, NE, NE]), ALU.mult))
                link(e, e.tensor_reduce(R["ob"], R["big"], AX_X, ALU.add))
                link(e, e.tensor_scalar(R["dl"], R["ob"], float(SLOTS), float((NE - 1) * SLOTS), ALU.mult, ALU.add))
                link(e, e.tensor_tensor(R["dl"], R["dl"], c_["first"], ALU.subtract))
                pos = ps[:, 6, 0:5 * NE].rearrange("p (t k) -> p t k", t=5)
                link(e, e.tensor_scalar(R["ge"], pos, float(SLOTS), None, ALU.is_ge))
                link(e, e.tensor_tensor(R["ge"], R["ge"], R["dl"].unsqueeze(1).broadcast_to([P, 5, NE]), ALU.mult))
                link(e, e.tensor_tensor(R["ge"], R["ge"], c_["first"].unsqueeze(1).broadcast_to([P, 5, NE]), ALU.add))
                link(e, e.tensor_tensor(R["ge"], R["ge"], pos, ALU.add))
                for j in range(2):
                    link(e, e.tensor_tensor(R["mm"][:, j], R["mm"][:, j], R["ge"], ALU.mult))
                    link(e, e.tensor_reduce(slot_f[:, :, j], R["mm"][:, j], AX_X, ALU.add))
                tile_ = c_["tile"][0:1].unsqueeze(2).broadcast_to([1, OVF, NE])
                link(e, e.tensor_tensor(R["oe"], tile_, R["ob"][0:1].unsqueeze(1).broadcast_to([1, OVF, NE]),
                                        ALU.is_ge))
                link(e, e.tensor_tensor(R["oend"], R["ob"][0:1], R["ov"][0:1], ALU.add))
                link(e, e.tensor_tensor(R["oe2"], tile_, R["oend"].unsqueeze(1).broadcast_to([1, OVF, NE]),
                                        ALU.is_lt))
                link(e, e.tensor_tensor(R["oe"], R["oe"], R["oe2"], ALU.mult))
                link(e, e.tensor_tensor(R["oe"], R["oe"], c_["eid"][0:1].unsqueeze(1).broadcast_to([1, OVF, NE]),
                                        ALU.mult))
                link(e, e.tensor_reduce(R["of"][:, 1:1 + OVF], R["oe"], AX_X, ALU.add))
                link(e, e.tensor_reduce(R["of"][:, 0:1], R["ov"][0:1], AX_X, ALU.add))
                link(e, e.tensor_copy(ovf_i[:, :], R["of"]))
                e.tensor_copy(slot_i[:, :].rearrange("p (t j) -> p t j", j=2), slot_f[:, :, :]).then_inc(moe_idx, 1)

                gainx = gains[:, grow, :].rearrange("p (h c) -> p h c", h=2).unsqueeze(3)\
                    .broadcast_to([P, 2, 4, SLOTS])

                def evac_rows(i, k):
                    e.wait_ge(moe_tp, i * 2 + (before + k + 1))
                    if k >= 2:
                        e.wait_ge(moe_gu, i * 2 + (before + k - 1))
                    e.tensor_tensor(xsT[:, k % 2].rearrange("p (h c) s -> p h c s", h=2),
                                    ps[:, 0:2, 0:4 * SLOTS].rearrange("p h (c s) -> p h c s", c=4), gainx,
                                    ALU.mult).then_inc(moe_tev, 1)

                def hidden(i, k):
                    q = k % 2
                    e.wait_ge(moe_silu, i * 2 + (before + k + 1))
                    if k >= 2:
                        e.wait_ge(moe_dn, i * 2 + (before + k - 1))
                    e.tensor_tensor(hid[:, q].rearrange("p f s -> p (f s)"), sg[:, q].rearrange("p f s -> p (f s)"),
                                    ps[:, 2 + q, 2 * SLOTS:4 * SLOTS], ALU.mult).then_inc(moe_hid, 1)

                def y_half(i, k):
                    e.wait_ge(moe_dn, i * 2 + (before + k + 1))
                    e.wait_ge((moe_st0, moe_st1)[k % 2], i * 16 + (8 * before + k // 2 * 16))
                    e.tensor_copy(ye[0:SLOTS, k % 2, 512:1024], ps[0:SLOTS, 5 + 2 * (k % 2), :]).then_inc(moe_yv, 1)

                evac_rows(0, 0)
                hidden(0, 0)
                evac_rows(0, 1)
                for k in (1, 2):
                    hidden(0, k)
                    y_half(0, k - 1)
                    evac_rows(0, k + 1)
                with e.Fori(0, 6) as i:
                    for k in range(2):
                        hidden(i, 3 + k)
                        y_half(i, 2 + k)
                        evac_rows(i, 4 + k)
                hidden(0, 15)
                y_half(0, 14)
                y_half(0, 15)
                n_ovf = e.value_load(ovf_i[0:1, 0:1], min_val=0, max_val=OVF)
                with e.If(n_ovf > 0):
                    with e.Fori(0, OVF) as t:
                        e.wait_ge(o["tp"], t + 1)
                        e.tensor_tensor(xsT[:, 0].rearrange("p (h c) s -> p h c s", h=2),
                                        ps[:, 0:2, 0:4 * SLOTS].rearrange("p h (c s) -> p h c s", c=4), gainx,
                                        ALU.mult).then_inc(o["tev"], 1)
                        e.wait_ge(o["silu"], t + 1)
                        e.tensor_tensor(hid[:, 0].rearrange("p f s -> p (f s)"),
                                        sg[:, 0].rearrange("p f s -> p (f s)"), ps[:, 2, 2 * SLOTS:4 * SLOTS],
                                        ALU.mult).then_inc(o["hid"], 1)
                        e.wait_ge(o["dn"], t + 1)
                        e.tensor_copy(ye[0:SLOTS, 0, 512:1024], ps[0:SLOTS, 5, :]).then_inc(o["y"], 1)
                for t in range(5):
                    r = rows_of(t)
                    e.wait_ge(gathered[t], 32 * (layer + 1))
                    link(e, e.scalar_tensor_tensor(x[0:r, t, :], yg[0:r, t, 0, :], pair_w[0:r, t, 0:1], x[0:r, t, :],
                                                   ALU.mult, ALU.add))
                    e.scalar_tensor_tensor(x[0:r, t, :], yg[0:r, t, 1, :], pair_w[0:r, t, 1:2], x[0:r, t, :],
                                           ALU.mult, ALU.add).then_inc(moe_comb, 1)

            norm_v(1, lambda q, t: q.wait_ge(back_add, DC), [2], [hT])
            moe_v(0)
            norm_v(2, lambda q, t: q.wait_ge(moe_comb, t + 1), [4, 1], [hT, hqT])
            kst = (kvq_kst0, kvq_kst1)

            def sum_page(n):
                b, page = divmod(n, PAGES)
                e.wait_ge(dec_prod, n + 1)
                e.tensor_reduce(sK[:, page, b * 16:(b + 1) * 16],
                                prod[:, n % 2, :].rearrange("p (k d) -> p k d", d=HD), AX_X, ALU.add)\
                    .then_inc(dec_red, 1)

            for n in range(3 * DC):
                kind, h = divmod(n, DC)
                e.wait_ge(kvq_tp, n + 1)
                if kind == 1 and h >= 2:
                    e.wait_ge(kst[n % 2], 16 * (h // 2))
                src = ps[:, 4 + n % 2, :].rearrange("p (t f) -> p t f", t=NT)
                if kind == 1:
                    e.tensor_copy(ktok[:, n % 2].rearrange("p (t f) -> p t f", t=NT), src)
                if kind == 2:
                    e.tensor_copy(vtok[:, :, h * P:(h + 1) * P], src)
                e.tensor_copy(tok8[:, (2, 0, 1)[kind], h * P:(h + 1) * P], ps[0:NB, 6 + n % 2, 0:P])\
                    .then_inc(kvq_ev, 1)
                if n > DC:
                    sum_page(2 * (n - DC - 1))
                    sum_page(2 * (n - DC - 1) + 1)
            e.wait_ge(kvq_ev, 3 * DC)
            own = aT.rearrange("p a s -> p (a s)")[0:NB, :]
            link(e, e.tensor_tensor(own, tok8[:, 2, :], tok8[:, 0, :], ALU.mult))
            e.tensor_reduce(down_, own.rearrange("p (k d) -> p k d", d=HD), AX_X, ALU.add).then_inc(dec_own, 1)
            sum_page(NB * PAGES - 2)
            sum_page(NB * PAGES - 1)
            e.wait_ge(dec_own, 1)
            e.wait_ge(kvq_vst, 16 * (NT + 2))
            e.wait_ge(kvq_qst, 16)
            steps = NH * NT
            for k in range(steps + 1):
                if k < steps:
                    h, q = divmod(k, NT)
                    w = (q + 1) * P
                    e.wait_ge(att_qk, k + 1)
                    e.wait_ge(att_bias, h + 1)
                    if k >= 3:
                        e.wait_ge(att_tp, k - 2)
                    for mp in range(2):
                        ins = e.tensor_tensor_reduce(st[:, k % 3, mp * SEQ:mp * SEQ + w],
                                                     ps[:, 2 * (k % 2) + mp, 0:w], bias8[:, h % 2, SEQ - w:SEQ],
                                                     HD ** -0.5, -3e38, ALU.add, ALU.max, mx[:, k % 2, mp:mp + 1])
                    link(e, ins)
                    e.tensor_scalar(nm[:, k % 2, :], mx[:, k % 2, :], -1.0, None, ALU.mult).then_inc(att_neg, 1)
                if k >= 1:
                    n = k - 1
                    w = (n % NT + 1) * P
                    q = n % 3
                    e.wait_ge(att_ex, n + 1)
                    if n >= 4:
                        e.wait_ge(att_o, n - 3)
                    link(e, e.reciprocal(rz[:, n % 4, :], zz[:, n % 2, :]))
                    link(e, e.scalar_tensor_tensor(rz[:, n % 4, 1:2], rz[:, n % 4, 1:2], neglam[:, 0:1],
                                                   zz[:, n % 2, 0:1], ALU.mult, ALU.mult))
                    e.scalar_tensor_tensor(st[:, q, 0:w], st[:, q, SEQ:SEQ + w], rz[:, n % 4, 1:2], st[:, q, 0:w],
                                           ALU.mult, ALU.add).then_inc(att_a, 1)
                if k == 0:
                    link(e, e.tensor_scalar(dbias, c_["past"], c_["slope"], None, ALU.mult))
                    e.wait_ge(dec_tp, 1)
                    e.tensor_tensor_reduce(dS[:, 0:SEQ], ps[:, 6, :], dbias, HD ** -0.5, -3e38, ALU.add, ALU.max,
                                           dsm[:, 0:1]).then_inc(dec_max0, 1)
                if k == DEC_JOIN - 3:
                    e.wait_ge(dec_max0, 1)
                    e.wait_ge(dec_ownr, 16)
                    link(e, e.tensor_scalar(dS[:, SEQ:SEQ + 1], downc, HD ** -0.5, None, ALU.mult))
                    link(e, e.tensor_tensor(dsm[:, 1:2], dsm[:, 0:1], dS[:, SEQ:SEQ + 1], ALU.max))
                    e.tensor_scalar(dsm[:, 2:3], dsm[:, 1:2], -1.0, None, ALU.mult).then_inc(dec_max, 1)
                if k == DEC_JOIN - 1:
                    link(e, e.scalar_tensor_tensor(dsm[:, 4:5], c_["odd"], neglam[:, 0:1], c_["even"],
                                                   ALU.mult, ALU.add))
                    e.wait_ge(dec_ex, 1)
                    link(e, e.reciprocal(dsm[:, 5:6], dsm[:, 3:4]))
                    link(e, e.tensor_tensor(dsm[:, 6:7], dsm[:, 4:5], dsm[:, 5:6], ALU.mult))
                    e.tensor_scalar(dC, c_["sel"], dsm[:, 6:7], None, ALU.mult).then_inc(dec_c, 1)
            e.wait_ge(att_o, steps)
            e.tensor_scalar(oss, oss, 1.0 / P, EPS, ALU.mult, ALU.add).then_inc(att_var, 1)
            e.wait_ge(att_root, 1)
            link(e, e.reciprocal(orr.rearrange("p t h -> p (t h)"), root[:, 0:NT * NH]))
            for t in range(NT):
                e.tensor_tensor(otok[:, t, :].rearrange("p (h d) -> p h d", h=NH),
                                otok[:, t, :].rearrange("p (h d) -> p h d", h=NH),
                                orr[:, t, :].unsqueeze(2).broadcast_to([P, NH, P]), ALU.mult).then_inc(att_on, 1)
                if t > 0:
                    continue
                e.wait_ge(dec_otp, 1)
                e.wait_ge(dec_vown, 16)
                link(e, e.scalar_tensor_tensor(do64, dvown, daown, ps[0:64, 6, 0:P], ALU.mult, ALU.add))
                link(e, e.tensor_tensor_reduce(dsq, do64, do64, 1.0, 0.0, ALU.mult, ALU.add, dsm[0:64, 7:8]))
                e.tensor_scalar(dsm[0:64, 8:9], dsm[0:64, 7:8], 1.0 / P, EPS, ALU.mult, ALU.add).then_inc(dec_sq, 1)
            e.wait_ge(dec_root, 1)
            link(e, e.reciprocal(dsm[0:64, 10:11], dsm[0:64, 9:10]))
            e.tensor_scalar(do64, do64, dsm[0:64, 10:11], None, ALU.mult).then_inc(dec_o2, 1)
            for n in range(DC):
                e.wait_ge(back_tp, DC + n + 1)
                add_chunk(slice(n * P, (n + 1) * P), n % 2)
            norm_v(3, lambda q, t: q.wait_ge(back_add, 2 * DC), [3], [hT])
            moe_v(1)
            norm_v(4, lambda q, t: q.wait_ge(moe_comb, 5 + t + 1), [], [], normed=False)
            e.wait_ge(norm_rs, 5)
            e.wait_ge(fin_g, 16)
            for t in range(5):
                r = rows_of(t)
                e.scalar_tensor_tensor(xn[0:r, t].rearrange("p c f -> p (c f)"), x[0:r, t, :],
                                       rstd[0:r, t:t + 1], gfin[0:r, :], ALU.mult, ALU.mult).then_inc(fin_y, 1)


INS = ["x_prompt", "x_sample", "cache_k", "cache_v", "page_table", "norm_mix", "norm_ffn", "w_uv", "sgu_gain",
       "w_sgu", "b_sgu", "w_gmlp_o", "norm_kv", "w_k", "w_v", "w_q", "lam_q", "lam_k", "subln_gain", "w_attn_o",
       "w_router_group", "b_router_group", "w_router_expert", "b_router_expert", "w_e_gate", "w_e_up", "w_e_down",
       "norm_final"]
OUTS = {"y_prompt": (1, SEQ, D), "y_sample": (NB, 1, D), "k_prompt": (1, NT, P, NH, 2, HD),
        "v_prompt": (1, NT, P, NH, P), "k_sample": (NB, 1, NH, 2, HD), "v_sample": (NB, 1, NH, P),
        "gmlp_v_sample": (1, NB, 1, DG)}


def kernel(**inputs):
    import numpy as np
    import concourse.bacc as bacc
    from concourse.bass_utils import run_bass_kernel_spmd

    nc = bacc.Bacc("TRN2", target_bir_lowering=False, num_devices=1)
    arrays = {"in_" + n: np.ascontiguousarray(inputs[n]) for n in INS}
    arrays["in_geometry"] = geometry()
    a = {n[3:]: nc.dram_tensor(n, v.shape, mybir.dt.from_np(v.dtype), kind="ExternalInput").ap()
         for n, v in arrays.items()}
    out = {n: nc.dram_tensor("out_" + n, shape, F32, kind="ExternalOutput").ap() for n, shape in OUTS.items()}
    build(nc, a, out)
    r = run_bass_kernel_spmd(nc, [arrays], core_ids=[0])
    return tuple(r.results[0]["out_" + n] for n in OUTS)
```

```python
import math
from contextlib import ExitStack

import concourse.bass as bass
from concourse import mybir

F32 = mybir.dt.float32
F32R = mybir.dt.float32r
I32 = mybir.dt.int32
ALU = mybir.AluOpType
ACT = mybir.ActivationFunctionType
AX_X = mybir.AxisListType.X

P = 128
D = 1024
DC = D // P
SEQ = 512
NB = 8
T = SEQ + NB
HALF = T // 2
NT = SEQ // P
DG = 3 * D
GC = DG // P
NG = 8
GCOLS = DG // NG
NH = 8
HD = 64
NE = 16
NEG = 4
TOPK = 2
DE = 256
EPS = 1e-6
PAGES = 4
BIG = 1e30
LAM_INIT = 0.8 - 0.6 * math.exp(-0.3)
RING = 6
SLOTW = 2048
SLOTS = 128
PAIRS = TOPK * T
OVF = (PAIRS - TOPK) // SLOTS
ROWS = (NE + OVF) * SLOTS
MAXT = (T - 1) // SLOTS

UV0 = 0
GO0 = UV0 + 2 * DG // 256
MOE0 = GO0 + 3 * DC // 2
KVQ0 = MOE0 + 3 * NE
VP0 = KVQ0 + 12 + NB * PAGES // 2
AO0 = VP0 + NB * PAGES // 2
MOE1 = AO0 + 4
END = MOE1 + 3 * NE

UVC, GOC, KVQC, AOC = 0, 2 * GC, 2 * GC + 3 * DC, 2 * GC + 6 * DC

CONSTS = {}
_at = 0
for _name, _n in [("ident", P), ("tri", P), ("ones", P), ("causal", P), ("dist", SEQ), ("sel", 64),
                  ("lt", NE * NE), ("even", 1), ("odd", 1), ("valid", 1), ("iota", NEG),
                  ("iota99", NEG), ("first", NE), ("eid", NE), ("tile", OVF)]:
    CONSTS[_name] = (_at, _at + _n)
    _at += _n
NCONST = _at


EARLY = 24
DEC_TURN = NB * PAGES - EARLY + 1
DEC_JOIN = NH * NT - 2 * NB - 1
DEC_STEPS = [DEC_JOIN + 1 + n for n in range(2 * NB)]
N_SMALL = 15


def geometry():
    import numpy as np

    k = np.zeros((P, NCONST), np.float32)
    p = np.arange(P)[:, None]

    def put(name, value):
        lo, hi = CONSTS[name]
        k[:, lo:hi] = value

    n = np.arange(P)[None]
    put("ident", p == n)
    put("tri", p < n)
    put("ones", 1)
    put("causal", p <= n)
    dist = p + (NT - 1) * P - np.arange(SEQ)[None]
    put("dist", np.where(dist >= 0, dist, BIG))
    put("sel", p // 2 == np.arange(64)[None])
    put("lt", np.tile((np.arange(NE)[None, :] < np.arange(NE)[:, None]).reshape(1, -1), (P, 1)))
    put("even", p % 2 == 0)
    put("odd", p % 2 == 1)
    put("valid", p < NB)
    put("iota", np.arange(NEG)[None])
    put("iota99", np.arange(NEG)[None] + 99)
    put("first", np.arange(NE)[None] * SLOTS)
    put("eid", np.arange(NE)[None])
    put("tile", np.arange(OVF)[None])
    return k


def past_bias():
    import numpy as np

    slope = 2.0 ** -(1.0 + np.arange(P)[:, None] // 2 % NH)
    return (-8.0 * slope * (PAGES * P - np.arange(SEQ)[None])).astype(np.float32)


def bcast_rows(ap, pattern, n, layers):
    flat = ap.rearrange(pattern).rearrange("(o n) -> o n", o=1)
    return flat.broadcast_to([n, flat.shape[1]]).rearrange("p (l k) -> p l k", l=layers)


def kvq_stream():
    blocks, early = [("w", k) for k in range(4)], EARLY // 2
    for k in range(8):
        blocks.append(("w", 4 + k))
        blocks += [("p", n) for n in range(k * early // 8, (k + 1) * early // 8)]
    return blocks + [("p", n) for n in range(early, NB * PAGES // 2)]


def kvq_block(k):
    return KVQ0 + kvq_stream().index(("w", k))


def kpage_block(n):
    return KVQ0 + kvq_stream().index(("p", n // 2))


def kpages(b):
    if not KVQ0 <= b < VP0:
        return []
    kind, n = kvq_stream()[b - KVQ0]
    return [2 * n, 2 * n + 1] if kind == "p" else []


def vector_tiles(n):
    return () if n in (2, 4) else (1, 3)


def scalar_tiles(n):
    return [t for t in range(5) if t not in vector_tiles(n)]


def loads_per_block(b):
    return 32 if kpages(b) or VP0 <= b < AO0 else 16


def loaded_value(b):
    return sum(loads_per_block(c) for c in range(b % RING, b + 1, RING))


def done(chunk):
    return chunk + 2


def plain(ap):
    return ap.bitcast(F32)


def build(nc, a, out):
    ctx = ExitStack()

    placed = {}

    def sb(name, shape, dt=F32):
        placed[name] = -(-nc.sbuf_base // 32) * 32
        return ctx.enter_context(nc.sbuf_tensor(name, shape, dt))

    def parts_in(name, shape):
        return nc.alloc_sbuf_tensor_at(name + "_parts", shape, F32R, offset=placed[name])

    def sem(name):
        return ctx.enter_context(nc.semaphore(name))

    def sems(stage, names):
        return [sem(f"{stage}_{n}") for n in names.split()]

    with ctx:
        x = sb("x", [P, 5, D])
        hT = sb("hT", [P, DC, T])
        ring = sb("ring", [P, RING, SLOTW])
        U = sb("U", [P, GC * T])
        V = sb("V", [P, GC * T])
        wh = sb("wh", [P, 2, DC, P], F32R)
        vd = sb("vd", [P, GC * NB])
        K = sb("K", [P, NCONST])
        c_ = {n: K[:, lo:hi] for n, (lo, hi) in CONSTS.items()}
        ident, ones = c_["ident"], c_["ones"]
        gains = sb("gains", [P, 5, DC])
        sgain = sb("sgain", [P, GC])
        wT = sb("wT", [P, NG, P])
        wr = sb("wr", [P, 2, DC, 20])
        rbias = sb("rbias", [P, 2, 20])
        w00 = sb("w00", [P, 2, NG])
        subg = sb("subg", [P, 1])
        neglam = sb("neglam", [P, 1])
        pt = sb("pt", [1, NB * PAGES], I32)
        ss = sb("ss", [P, 5])
        rstd = sb("rstd", [P, 5])
        root = sb("root", [P, 40])
        vtmp = sb("vtmp", [P, 2, T])
        x_parts = parts_in("x", [P, 5 * D])
        hT_parts = parts_in("hT", [P, DC, T])
        ring_parts = parts_in("ring", [P, RING, SLOTW])
        U_parts = parts_in("U", [P, GC * T])
        V_parts = parts_in("V", [P, GC * T])
        ps = ctx.enter_context(nc.psum_tensor("ps", [P, 8, 512], F32))

        def take(region, at, shape):
            n = math.prod(shape)
            ap = region[:, at:at + n]
            if len(shape) == 2:
                ap = ap.rearrange("p (a b) -> p a b", a=shape[0])
            if len(shape) == 3:
                ap = ap.rearrange("p (a b c) -> p a b c", a=shape[0], b=shape[1])
            return ap

        hTflat = hT[:, :, :].rearrange("p j t -> p (j t)")
        xflat = x[:, :, :].rearrange("p t f -> p (t f)")
        hh = take(x_parts, 0, (DC, T))
        sqs = take(xflat, DC * T, (NT, P))
        gtmp = take(xflat, D, (4, SEQ))
        bsg = take(xflat, DG + 2 * SEQ, (NG, P))
        u = take(U, 0, (GC, T))
        xn = take(U, 0, (5, DC, P))
        e0 = 5 * D
        xs = take(U, e0, (2, DC, P))
        xsT = take(U, e0 + 2 * D, (2, DC, SLOTS))
        e1 = e0 + 2 * D + 2 * DC * SLOTS
        sg = take(U, e1, (2, 2, SLOTS))
        hid = take(U, e1 + 4 * SLOTS, (2, 2, SLOTS))
        ye = take(U, e1 + 8 * SLOTS, (2, D))
        assert e1 + 8 * SLOTS + 2 * D <= GC * T
        vtok = take(U, 0, (NT, D))
        ktok = take(U, NT * D, (2, 512))
        kvqh = take(U_parts, 5 * D, (DC, T))
        tok8 = take(U, 5 * D + DC * T, (3, D))[0:NB]
        assert 5 * D + DC * T + 3 * D <= GC * T
        otok = take(U, NT * D, (NT, D))
        st = take(U, 2 * NT * D, (3, 2 * SEQ))
        s0 = 2 * NT * D + 3 * 2 * SEQ
        dC = U[:, s0:s0 + 64]
        daT = take(U, s0 + 64, (PAGES, NB * NH))
        doT = U[:, s0 + 320:s0 + 384]
        do64 = U[0:NB * NH, s0 + 384:s0 + 512]
        dvown = U[0:NB * NH, s0 + 512:s0 + 640]
        daown = U[0:NB * NH, s0 + 640:s0 + 641]
        dsq = U[0:NB * NH, s0 + 648:s0 + 776]
        assert s0 + 776 <= GC * T
        v = take(V, 0, (NT, DG))
        yg = take(V, 0, (5, TOPK, D))
        ow = take(V, 0, (3, SLOTW))
        kT = take(V, 0, (DC, T))
        qT = take(V, DC * T, (DC, T))
        v0 = 2 * DC * T
        prod = take(V, v0, (2, D))
        aT = take(V, v0 + 2 * D, (2, SEQ))
        sK = take(V, v0 + 3 * D, (PAGES, P))
        v1 = v0 + 3 * D + PAGES * P
        mx = take(V, v1, (2, 2))
        nm = take(V, v1 + 4, (2, 2))
        zz = take(V, v1 + 8, (2, 2))
        rz = take(V, v1 + 12, (4, 2))
        oss = take(V, v1 + 24, (NT, NH))
        orr = take(V, v1 + 56, (NT, NH))
        dsm = V[:, v1 + 88:v1 + 104]
        down_ = V[0:NB, v1 + 104:v1 + 120]
        downc = V[:, v1 + 120:v1 + 121]
        osq = V[:, v1 + 124:v1 + 124 + P]
        assert v1 + 124 + P <= NT * DG
        dS = hTflat[:, 0:SEQ + 1]
        dbias = hTflat[:, 520:520 + SEQ]
        dmk = hTflat[0:4, 1040:1040 + 512]
        dor = take(hTflat, 1552, (2 * NB, P))[0:4]
        qbc = (aT.rearrange("p a s -> p (a s)"), wT[:, :, :].rearrange("p g t -> p (g t)"))
        ul = take(U_parts, 0, (GC, T))
        qbc_late = take(hTflat, 1552, (2, D))

        def q_place(b):
            return qbc[b % 2] if b < EARLY // PAGES else qbc_late[:, b % 2, :]

        uh = take(V_parts, 0, (GC, T))
        oh = take(V_parts, 0, (DC, T))
        bias8 = wT[:, :, :].rearrange("p g t -> p (g t)").rearrange("p (b f) -> p b f", b=2)
        slot_f = sb("slot_f", [P, 5, TOPK])
        slot_i = sb("slot_i", [P, 5 * TOPK], I32)
        pair_w = sb("pair_w", [P, 5, TOPK])
        ovf_i = sb("ovf_i", [1, 1 + OVF], I32)
        zeros = V[:, 4 * D:5 * D]
        vss = sb("vss", [P, NT, GC])
        gss = take(sb("gss", [P, 3 * (NT + NB)]), 0, (3, NT + NB))
        gfin = hTflat[:, 0:D]
        vtflat = vtmp[:, :, :].rearrange("p a t -> p (a t)")
        v8sq, v8n, v8g = (vtflat[:, k * GC * NB:(k + 1) * GC * NB] for k in range(3))
        ws = take(hTflat, 0, (NT, NG, P))
        VS = hTflat[0:NB, 0:DG]
        R, r0 = {}, 10 * D
        for name, shape in (("l", (5, 20)), ("eg", (5, NEG)), ("cand", (5, NEG)), ("oh", (5, NEG)),
                            ("oh1", (5, NEG)), ("oh2", (5, NEG)), ("el", (5, NEG)), ("el2", (5, NEG)),
                            ("gmax", (5,)), ("m1", (5,)), ("m2", (5,)), ("e2", (5,)), ("gs", (5,)), ("den", (5,)),
                            ("least", (5,)), ("pick", (5, NE)), ("m", (6, NE)), ("before", (6, NE)), ("mm", (2, 5, NE)),
                            ("ov", (NE,)), ("ov1", (NE,)), ("ob", (NE,)), ("dl", (NE,)), ("oend", (NE,)),
                            ("big", (NE, NE)), ("ge", (5, NE)), ("oe", (OVF, NE)), ("oe2", (OVF, NE)),
                            ("of", (1 + OVF,))):
            R[name] = take(V, r0, shape)
            r0 += math.prod(shape)
        assert r0 <= NT * DG
        for name in ("oend", "oe", "oe2", "of"):
            R[name] = R[name][0:1]
        w_st = take(V, D, (NG, P))
        wre_st = V[:, 2 * D:2 * D + 256].rearrange("p (l g f) -> p l g f", l=2, g=NEG)
        wrg_st = V[:, 2 * D + 256:2 * D + 320].rearrange("p (l f) -> p l f", l=2)
        sg_st = V[0:GC, 2 * D + 320:2 * D + 448]
        lam_st = take(V, 2 * D + 448, (2, 2 * HD))
        lam_s = V[:, 2 * D + 704:2 * D + 712]

        slots_dram = nc.dram_tensor("slots_dram", [ROWS, D], F32, kind="Internal").ap()
        q_dram = nc.dram_tensor("q_dram", [NB, D], F32, kind="Internal").ap()
        own_dram = nc.dram_tensor("own_dram", [NB, 2 * NH], F32, kind="Internal").ap()

        loaded = [sem(f"loaded{s}") for s in range(RING)]
        ld_x = [sem(f"ld_x{t}") for t in range(5)]
        again_x = sem("again_x")
        ld_c, ld_w, ld_pt, ld_bs = sem("ld_c"), sem("ld_w"), sem("ld_pt"), sem("ld_bs")
        (prep_init, prep_tp, prep_v, prep_lam, prep_lame) = sems(
            "prep", "init tp v lam lame")
        zero_set, zeroed = sem("zero_set"), sem("zeroed")
        chain = sem("chain")
        (norm_sq_a, norm_sq_v, norm_var, norm_root, norm_rs, norm_xn, norm_tp, norm_ev) = sems(
            "norm", "sq_a sq_v var root rs xn tp ev")
        mm = sem("mm")
        split_hi, split_lo = sem("split_hi"), sem("split_lo")
        norm_hi, norm_lo, u_hi, u_lo = sem("norm_hi"), sem("norm_lo"), sem("u_hi"), sem("u_lo")
        ld_past = sem("ld_past")
        rows_out = sem("rows_out")
        att_lo = sem("att_lo")
        (uv_gelu, uv_tp, uv_ev, uv_sq) = sems(
            "uv", "gelu tp ev sq")
        (gate_var, gate_root, gate_rs, gate_vn_v, gate_vn_a, gate_vs, gate_sp, gate_tmp, gate_u,
         gate_uv, gate_su, gate_vt, gate_v8) = sems(
            "gate", "var root rs vn_v vn_a vs sp tmp u uv su vt v8")
        (back_cp, back_tp, back_add) = sems(
            "back", "cp tp add")
        (moe_lg, moe_rt, moe_ex, moe_mk, moe_cum, moe_idx, moe_scat, moe_ld0, moe_ld1, moe_tp, moe_tev, moe_gu,
         moe_silu, moe_hid, moe_dn, moe_ya, moe_yv, moe_st0, moe_st1, moe_gat0, moe_gat1, moe_gat2, moe_gat3,
         moe_gat4, moe_comb, moe_over) = sems(
            "moe", "lg rt ex mk cum idx scat ld0 ld1 tp tev gu silu hid dn ya yv st0 st1 gat0 gat1 gat2 "
            "gat3 gat4 comb over")
        gathered = [moe_gat0, moe_gat1, moe_gat2, moe_gat3, moe_gat4]
        ovfs = [{k: sem(f"ovf{n}_{k}") for k in "ld tp tev gu silu hid dn y st".split()} for n in range(2)]
        (kvq_cp, kvq_tp, kvq_ev, kvq_kst0, kvq_kst1, kvq_vst, kvq_qst, kvq_qld0, kvq_qld1) = sems(
            "kvq", "cp tp ev kst0 kst1 vst qst qld0 qld1")
        (att_bias, att_qk, att_neg, att_ex, att_a, att_tp, att_aT, att_pv, att_o, att_var,
         att_root, att_on, att_tp2, att_ev) = sems(
            "att", "bias qk neg ex a tp aT pv o var root on tp2 ev")
        (dec_prod, dec_red, dec_own, dec_ownr, dec_tp, dec_max0, dec_max, dec_ex, dec_c, dec_aTp, dec_aT, dec_pv,
         dec_o, dec_otp, dec_sq, dec_root, dec_o2, dec_otp2, dec_ev, dec_vown, dec_diag, dec_dt) = sems(
            "dec", "prod red own ownr tp max0 max ex c aTp aT pv o otp sq root o2 otp2 ev vown diag dt")
        fin_y, fin_st = sem("fin_y"), sem("fin_st")

        block = ctx.enter_context(nc.Block())
        chained = [0]

        def link(eng, ins):
            ins.then_inc(chain, 1)
            chained[0] += 1
            eng.wait_ge(chain, chained[0])

        def slot_loaded(eng, b, i=0):
            eng.wait_ge(loaded[b % RING], i * 16 + loaded_value(b))

        def ringslot(b, shape):
            return take(ring[:, b % RING, :], 0, shape)

        def low_parts(b, half):
            return take(ring_parts[:, b % RING, :], 0, (DC, 256))[:, :, half * P:(half + 1) * P]

        def rows_of(t):
            return P if t < NT else NB

        def cols_of(t):
            return slice(t * P, t * P + rows_of(t))

        def last_use(b):
            if b < GO0:
                return mm, done(UVC + 2 * (b - UV0) + 1)
            if b < MOE0:
                return mm, done(GOC + (b - GO0) // 3 * 6 + 3 + (b - GO0) % 3)
            if KVQ0 <= b < VP0:
                if kpages(b):
                    return dec_prod, kpages(b)[1] + 1
                return mm, done(KVQC + 2 * [kvq_block(k) for k in range(12)].index(b) + 1)
            if VP0 <= b < AO0:
                return dec_pv, (b - VP0) // 2 * 2 + 2
            if AO0 <= b < MOE1:
                return mm, done(AOC + 2 * (b - AO0) + 1)
            r, before = (b - MOE0, 0) if b < KVQ0 else (b - MOE1, NE)
            if r < 2:
                return moe_gu, before + 1
            if r >= 44:
                return ((moe_gu, 16), (moe_gu, 16), (moe_dn, 15), (moe_dn, 16))[r - 44][0], \
                    before + (16, 16, 15, 16)[r - 44]
            q, s = divmod(r - 2, 3)
            return (moe_dn, before + q + 1) if s == 2 else (moe_gu, before + q + 2)

        @block.sync
        def _(sp):
            def free(b, i=0, per_loop=0):
                if b >= RING:
                    used, value = last_use(b - RING)
                    sp.wait_ge(used, i * per_loop + value)

            def load(b, src, shape, i=0, per_loop=0):
                free(b, i, per_loop)
                sp.dma_start(ringslot(b, shape), src).then_inc(loaded[b % RING], 16)

            for t in range(5):
                src = a["x_prompt"][0, t * P:(t + 1) * P, :] if t < NT else a["x_sample"][:, 0, :]
                sp.dma_start(x[0:rows_of(t), t, :], src).then_inc(ld_x[t], 16)
            w_uv = a["w_uv"][0].rearrange("(p c) n -> p c n", c=DC)
            for k in range(RING):
                if k == 1:
                    sp.wait_ge(ld_w, 16 * N_SMALL)
                load(UV0 + k, w_uv[:, :, k * 256:(k + 1) * 256], (DC, 256))
            sp.wait_ge(ld_pt, 16)
            pages = [sp.value_load(pt[0:1, n:n + 1], min_val=0, max_val=a["cache_k"].shape[0] - 1)
                     for n in range(NB * PAGES)]
            with sp.Fori(0, 3) as i:
                for k in range(RING):
                    load(UV0 + RING + k, w_uv[:, :, bass.ds(i * (RING * 256) + (RING + k) * 256, 256)],
                         (DC, 256), i, 2 * RING)
            w_go = a["w_gmlp_o"][0].rearrange("(b c p) n -> p b c n", c=DC, p=P)
            for k in range(3 * DC // 2):
                load(GO0 + k, w_go[:, k % 3, :, k // 3 * 256:(k // 3 + 1) * 256], (DC, 256))
            cache_k = a["cache_k"].rearrange("g s h m d -> g s (h m d)")
            cache_v = a["cache_v"].rearrange("g s h d -> g s (h d)")

            def page_load(b, half, cache, n):
                page = pages[n]
                sp.dma_start(ringslot(b, (2, D))[:, half, :],
                             cache[bass.ds(page, 1)].rearrange("o s f -> (o s) f")).then_inc(loaded[b % RING], 16)

            def kvq_load(b):
                free(b)
                if kpages(b):
                    for half, n in enumerate(kpages(b)):
                        page_load(b, half, cache_k, n)
                    return
                k = [kvq_block(k) for k in range(12)].index(b)
                w = (a["w_q"][0], a["w_k"], a["w_v"])[k // 4].rearrange("(p c) n -> p c n", c=DC)
                sp.dma_start(ringslot(b, (DC, 256)), w[:, :, (k % 4) * 256:(k % 4 + 1) * 256])\
                    .then_inc(loaded[b % RING], 16)

            def experts(base, layer, behind):
                wg = a["w_e_gate"][layer].rearrange("e (p c) f -> e p c f", c=DC)
                wu = a["w_e_up"][layer].rearrange("e (p c) f -> e p c f", c=DC)
                wd = a["w_e_down"][layer].rearrange("e (f p) n -> e p f n", p=P)
                before = NE * layer
                ld, stored = (moe_ld0, moe_ld1), (moe_st0, moe_st1)

                def one(w, e):
                    return w[bass.ds(e, 1)].rearrange("o p c f -> (o p) c f")

                def rows(e):
                    return slots_dram[bass.ds(e * SLOTS, SLOTS), :]

                def load_rows(i, k):
                    if not (isinstance(i, int) and k < 2):
                        sp.wait_ge(moe_tp, i * 2 + (before + k - 1))
                    sp.dma_start(xs[0:SLOTS, k % 2].rearrange("p c f -> p (c f)"), rows(i * 2 + k))\
                        .then_inc(ld[k % 2], 16)

                def store_rows(i, k):
                    sp.wait_ge(moe_ya, i * 2 + (before + k + 1))
                    sp.wait_ge(moe_yv, i * 2 + (before + k + 1))
                    sp.dma_start(rows(i * 2 + k), ye[0:SLOTS, k % 2, :]).then_inc(stored[k % 2], 16)

                load(base, wg[0], (DC, DE))
                load(base + 1, wu[0], (DC, DE))
                for k in range(2):
                    b = base + 2 + 3 * k
                    if k == 0:
                        load(b, wg[1], (DC, DE))
                        load(b + 1, wu[1], (DC, DE))
                        load(b + 2, wd[0], (2, D))
                        sp.wait_ge(moe_scat, 160 * (layer + 1))
                        load_rows(0, 0)
                        load_rows(0, 1)
                    else:
                        load(b, wg[2], (DC, DE))
                        load_rows(0, 2)
                        load(b + 1, wu[2], (DC, DE))
                        load(b + 2, wd[1], (2, D))
                with sp.Fori(0, 6) as i:
                    for k in range(2):
                        b = base + 8 + 3 * k
                        load(b, one(wg, i * 2 + (3 + k)), (DC, DE), i, 2)
                        load_rows(i, 3 + k)
                        load(b + 1, one(wu, i * 2 + (3 + k)), (DC, DE), i, 2)
                        load(b + 2, one(wd, i * 2 + (2 + k)), (2, D), i, 2)
                        store_rows(i, k)
                load(base + 44, wg[15], (DC, DE))
                load_rows(0, 15)
                load(base + 45, wu[15], (DC, DE))
                load(base + 46, wd[14], (2, D))
                store_rows(0, 12)
                load(base + 47, wd[15], (2, D))
                store_rows(0, 13)
                behind(0, 4)
                behind(4, 5)
                store_rows(0, 14)
                behind(5, 6)
                store_rows(0, 15)

            experts(MOE0, 0, lambda lo, hi: [kvq_load(KVQ0 + k) for k in range(lo, hi)])
            def load_q(b):
                if b >= 2:
                    sp.wait_ge(dec_prod, PAGES * (b - 1))
                sp.dma_start(q_place(b), q_dram[b:b + 1, :].broadcast_to([P, D]))\
                    .then_inc((kvq_qld0, kvq_qld1)[b % 2], 16)

            for b in range(KVQ0 + 6, VP0):
                kvq_load(b)
                if b == KVQ0 + 9:
                    sp.wait_ge(kvq_qst, 16)
                    load_q(0)
                    load_q(1)
                for q in range(2, EARLY // PAGES):
                    if b == kpage_block(PAGES * (q + 1) - 1):
                        load_q(q)
            sp.wait_ge(mm, done(AOC - 1))
            for q in range(EARLY // PAGES, NB):
                load_q(q)
            for n in range(NB * PAGES):
                b = VP0 + n // 2
                if n % 2 == 0:
                    free(b)
                page_load(b, n % 2, cache_v, n)
            w_ao = a["w_attn_o"][0].rearrange("(c p) n -> p c n", p=P)
            for k in range(4):
                load(AO0 + k, w_ao[:, :, k * 256:(k + 1) * 256], (DC, 256))
            experts(MOE1, 1, lambda lo, hi: None)
            for t in range(5):
                dst = out["y_prompt"][0, t * P:(t + 1) * P, :] if t < NT else out["y_sample"][:, 0, :]
                sp.wait_ge(fin_y, t + 1)
                sp.dma_start(dst, xn[0:rows_of(t), t].rearrange("p c f -> p (c f)")).then_inc(fin_st, 16)
            sp.wait_ge(fin_st, 16 * 5)

        @block.gpsimd
        def _(g):
            g.memset(zeros[:, :], 0.0).then_inc(zero_set, 1)
            g.wait_ge(zero_set, 1)
            g.wait_ge(mm, done(0))
            for r in range(0, ROWS, P):
                n = min(P, ROWS - r)
                g.dma_start(slots_dram[r:r + n, :], zeros[0:n, :]).then_inc(zeroed, 16)
            g.wait_ge(mm, done(GOC - 1))
            g.wait_ge(uv_sq, GC + 1)
            g.dma_start(bsg.rearrange("p g t -> p (g t)"),
                        a["b_sgu"][0].rearrange("(o g) t -> o (g t)", o=1).broadcast_to([P, NG * P]))\
                .then_inc(ld_bs, 16)
            for j in range(GC):
                if j % 3 == 2:
                    continue
                g.wait_ge(gate_tmp, j + 1)
                g.tensor_tensor(u[:, j, 0:SEQ], gtmp[:, j % 4, :], u[:, j, 0:SEQ], ALU.mult)\
                    .then_inc(gate_u, 1)
            g.wait_ge(gate_u, GC // 3 * 2)
            g.wait_ge(gate_uv, GC // 3)
            for t in range(5):
                src = a["x_prompt"][0, t * P:(t + 1) * P, :] if t < NT else a["x_sample"][:, 0, :]
                g.dma_start(x[0:rows_of(t), t, :], src).then_inc(again_x, 16)

            def moe_rows(layer):
                before = layer * NE
                g.wait_ge(moe_idx, layer + 1)
                for t in range(5):
                    for j in range(TOPK):
                        g.indirect_dma_start(
                            slots_dram, bass.IndirectOffsetOnAxis(
                                ap=slot_i[0:rows_of(t), 2 * t + j:2 * t + j + 1], axis=0),
                            xn[0:rows_of(t), t].rearrange("p c f -> p (c f)"), None).then_inc(moe_scat, 16)
                g.wait_ge(moe_st0, 16 * (before + NE) // 2)
                g.wait_ge(moe_st1, 16 * (before + NE) // 2)
                g.wait_ge(moe_over, layer + 1)
                if layer == 1:
                    g.dma_start(gfin, a["norm_final"].rearrange("(o n) -> o n", o=1).broadcast_to([P, D]))\
                        .then_inc(ld_bs, 16)
                for t in range(5):
                    for j in range(TOPK):
                        g.indirect_dma_start(
                            yg[0:rows_of(t), t, j, :], None, slots_dram, bass.IndirectOffsetOnAxis(
                                ap=slot_i[0:rows_of(t), 2 * t + j:2 * t + j + 1], axis=0))\
                            .then_inc(gathered[t], 16)

            moe_rows(0)
            qld = (kvq_qld0, kvq_qld1)
            g.wait_ge(kvq_ev, DC)
            g.dma_start(q_dram, tok8[:, 2, :]).then_inc(kvq_qst, 16)
            def page_product(n):
                b, page = divmod(n, PAGES)
                if page == 0:
                    g.wait_ge(qld[b % 2], 16 * (b // 2 + 1))
                slot_loaded(g, kpage_block(n))
                if n >= 2:
                    g.wait_ge(dec_red, n - 1)
                g.tensor_tensor(prod[:, n % 2, :], ringslot(kpage_block(n), (2, D))[:, n % 2, :],
                                q_place(b), ALU.mult).then_inc(dec_prod, 1)

            for n in range(EARLY):
                page_product(n)
            g.wait_ge(kvq_ev, 3 * DC)
            g.wait_ge(dec_own, 1)
            g.wait_ge(mm, done(AOC - 1))
            g.dma_start(dbias, a["past_bias"]).then_inc(ld_past, 16)
            g.dma_start(own_dram, down_).then_inc(kvq_qst, 16)
            for n in range(EARLY, EARLY + 4):
                page_product(n)
            g.wait_ge(kvq_qst, 32)
            g.dma_start(downc, own_dram.rearrange("b (h o) -> (b h) o", o=1)).then_inc(dec_ownr, 16)
            g.wait_ge(kvq_vst, 16 * 2)
            g.dma_start(dvown, out["v_sample"].rearrange("b o h d -> (b o h) d")).then_inc(dec_vown, 16)
            for n in range(EARLY + 4, NB * PAGES):
                page_product(n)
            moe_rows(1)

        @block.scalar
        def _(s):
            s.dma_start(K[:, :], a["geometry"]).then_inc(ld_c, 16)
            mats = [(gains[:, 0:2, :], a["norm_mix"].rearrange("l (p c) -> p l c", c=DC)),
                    (gains[:, 2:4, :], a["norm_ffn"].rearrange("l (p c) -> p l c", c=DC)),
                    (gains[:, 4, :], a["norm_kv"].rearrange("(p c) -> p c", c=DC)),
                    (sg_st, a["sgu_gain"].rearrange("o (j p) -> (o j) p", p=P)),
                    (w_st, a["w_sgu"][0].rearrange("g t s -> t g s")),
                    (wrg_st, a["w_router_group"].rearrange("l (p c) g -> p l (c g)", c=DC)),
                    (wre_st[:, 0], a["w_router_expert"][0].rearrange("g (p c) e -> p g (c e)", c=DC)),
                    (wre_st[:, 1], a["w_router_expert"][1].rearrange("g (p c) e -> p g (c e)", c=DC)),
                    (rbias[:, :, 0:NEG], bcast_rows(a["b_router_group"], "l g -> (l g)", P, 2)),
                    (rbias[:, :, NEG:20], bcast_rows(a["b_router_expert"], "l g e -> (l g e)", P, 2)),
                    (w00[:, 0, :], a["w_sgu"][0, :, 0, 0:1].rearrange("g o -> o g").broadcast_to([P, NG])),
                    (w00[:, 1, :], a["b_sgu"][0, :, 0:1].rearrange("g o -> o g").broadcast_to([P, NG])),
                    (lam_st[:, 0, :], a["lam_q"][0].rearrange("(o m) d -> o (m d)", o=1).broadcast_to([P, 2 * HD])),
                    (lam_st[:, 1, :], a["lam_k"][0].rearrange("(o m) d -> o (m d)", o=1).broadcast_to([P, 2 * HD])),
                    (subg[:, :], a["subln_gain"].rearrange("o p -> p o"))]
            for dst, src in mats:
                s.dma_start(dst, src, allow_slow_non_contiguous=True).then_inc(ld_w, 16)
            assert len(mats) == N_SMALL
            s.dma_start(pt[:, :], a["page_table"].rearrange("(o b) p -> o (b p)", o=1)).then_inc(ld_pt, 16)

            def high(chunk, b, half, i=0, per=0, gain=None):
                slot_loaded(s, b, i)
                if not (isinstance(i, int) and chunk < 2):
                    s.wait_ge(mm, i * per + done(chunk - 2))
                w = ringslot(b, (DC, 256))[:, :, half * P:(half + 1) * P]
                if gain is None:
                    s.activation(wh[:, chunk % 2], w, ACT.Copy).then_inc(split_hi, 1)
                    return
                for c in range(DC):
                    ins = s.activation(wh[:, chunk % 2, c, :], w[:, c, :], ACT.Copy,
                                       scale=gains[:, gain, c:c + 1])
                ins.then_inc(split_hi, 1)

            def norm_high(n, evs, to):
                for t in range(5):
                    s.wait_ge(norm_ev, evs + min(2 * t + 2, 9))
                    s.activation(to[:, :, cols_of(t)], hT[:, :, cols_of(t)], ACT.Copy).then_inc(norm_hi, 1)

            def norm_a(n, ready, normed=True):
                for t in scalar_tiles(n):
                    ready(s, t)
                    r = rows_of(t)
                    s.activation(xn[0:r, t].rearrange("p c f -> p (c f)"), x[0:r, t, :], ACT.Square,
                                 accum_out=ss[0:r, t:t + 1]).then_inc(norm_sq_a, 1)
                s.wait_ge(norm_var, n + 1)
                s.activation(root[:, 0:5], ss[:, :], ACT.Sqrt).then_inc(norm_root, 1)
                if normed:
                    s.wait_ge(norm_rs, n + 1)
                    for t in range(5):
                        r = rows_of(t)
                        s.activation(xn[0:r, t], x[0:r, t, :].rearrange("p (f c) -> p c f", c=DC), ACT.Copy,
                                     scale=rstd[0:r, t:t + 1]).then_inc(norm_xn, 1)

            s.wait_ge(prep_init, 1)
            norm_a(0, lambda e, t: e.wait_ge(ld_x[t], 16))

            s.wait_ge(norm_xn, 5)
            s.wait_ge(norm_sq_v, 2)
            norm_high(0, 0, hh)
            high(UVC, UV0, 0)
            s.wait_ge(prep_lam, 1)
            s.activation(lam_s[:, 2:4], lam_s[:, 0:2], ACT.Exp).then_inc(prep_lame, 1)
            s.sem_inc(uv_gelu, 1)
            s.sem_inc(uv_sq, 1)
            for part in range(2):
                with s.Fori(0, 2) as i:
                    def squares(c):
                        s.wait_ge(uv_ev, i * 12 + (c + 2))
                        s.wait_ge(uv_sq, i * 12 + (c + 1))
                        for t in range(NT):
                            ins = s.activation(sqs[:, t, :], v[:, t, bass.ds(i * (12 * P) + c * P, P)], ACT.Square,
                                               accum_out=vss[:, t, bass.ds(i * 12 + c, 1)])
                        ins.then_inc(uv_sq, 1)

                    for c in range(12):
                        n = 24 * part + c + 1
                        high(n, UV0 + n // 2, n % 2, i, 12)
                        s.wait_ge(mm, i * 12 + done(24 * part + c))
                        if part == 1:
                            s.wait_ge(uv_ev, i * 12 + (max(c - 1, 0) + 1))
                        bank = 2 * (c % 2)
                        dst = vtmp[:, c % 2, :] if part else u[:, bass.ds(i * 12 + c, 1), :]\
                            .rearrange("p o t -> p (o t)")
                        s.activation(dst.rearrange("p (h t) -> p h t", h=2), ps[:, bank:bank + 2, 0:HALF],
                                     ACT.Gelu_apprx_tanh).then_inc(uv_gelu, 1)
                        if part == 1 and c >= 1:
                            squares(c - 1)
                    if part == 1:
                        squares(11)
            s.wait_ge(gate_var, 1)
            s.activation(gss[:, 1], gss[:, 0], ACT.Sqrt).then_inc(gate_root, 1)
            s.wait_ge(gate_rs, 1)
            for t in (1, 3):
                s.activation(ws[:, t], wT[:, :, :], ACT.Copy, scale=gss[:, 2, t:t + 1]).then_inc(gate_vn_a, 1)
            s.wait_ge(gate_sp, GC)
            s.wait_ge(gate_su, 1)
            for j in range(GC):
                if j % 3 == 2:
                    s.wait_ge(gate_uv, j // 3 + 1)
                else:
                    s.wait_ge(gate_u, j // 3 * 2 + j % 3 + 1)
                s.activation(uh[:, j, :], u[:, j, :], ACT.Copy).then_inc(u_hi, 1)
                if j in (7, 15):
                    high(GOC + 1 + j // 8, GO0 + 1 + j // 8, 0)
            s.wait_ge(gate_v8, 2)
            s.dma_start(out["gmlp_v_sample"][0, :, 0, :], VS).then_inc(rows_out, 16)

            def copy_out(chunk, n, before):
                s.wait_ge(mm, done(chunk))
                if before + n >= 2:
                    s.wait_ge(back_tp, before + n - 1)
                s.activation(vtmp[:, n % 2, :].rearrange("p (h t) -> p h t", h=2),
                             ps[:, 2 * (n % 2):2 * (n % 2) + 2, 0:HALF], ACT.Copy).then_inc(back_cp, 1)

            for m in range(2, 3 * DC):
                if m + 1 < 3 * DC:
                    high(GOC + m + 1, GO0 + (m + 1) // 6 * 3 + (m + 1) % 3, (m + 1) // 3 % 2)
                if m % 3 == 2:
                    copy_out(GOC + m, m // 3, 0)

            def moe_a(layer):
                o, before = ovfs[layer], layer * NE
                s.wait_ge(moe_rt, 2 * layer + 1)
                s.activation(R["eg"], R["eg"], ACT.Exp).then_inc(moe_ex, 1)
                s.wait_ge(moe_rt, 2 * layer + 2)
                s.activation(R["e2"], R["e2"], ACT.Exp).then_inc(moe_ex, 1)

                def silu(i, k):
                    s.wait_ge(moe_gu, i * 2 + (before + k + 1))
                    s.activation(sg[:, k % 2].rearrange("p f s -> p (f s)"), ps[:, 2 + k % 2, 0:2 * SLOTS], ACT.Silu)\
                        .then_inc(moe_silu, 1)

                def y_half(i, k):
                    s.wait_ge(moe_dn, i * 2 + (before + k + 1))
                    s.wait_ge((moe_st0, moe_st1)[k % 2], i * 16 + (8 * before + k // 2 * 16))
                    s.activation(ye[0:SLOTS, k % 2, 0:512], ps[0:SLOTS, 4 + 2 * (k % 2), :], ACT.Copy)\
                        .then_inc(moe_ya, 1)

                silu(0, 0)
                for k in (1, 2):
                    silu(0, k)
                    y_half(0, k - 1)
                with s.Fori(0, 6) as i:
                    for k in range(2):
                        silu(i, 3 + k)
                        y_half(i, 2 + k)
                silu(0, 15)
                y_half(0, 14)
                y_half(0, 15)
                s.wait_ge(moe_tev, before + 1)
                n_ovf = s.value_load(ovf_i[0:1, 0:1], min_val=0, max_val=OVF)
                with s.If(n_ovf > 0):
                    wg = a["w_e_gate"][layer].rearrange("e (p c) f -> e p (c f)", c=DC)
                    wu = a["w_e_up"][layer].rearrange("e (p c) f -> e p (c f)", c=DC)
                    wd = a["w_e_down"][layer].rearrange("e (f p) n -> e p f n", p=P)
                    s.wait_ge(moe_st0, 16 * (before + NE) // 2)
                    with s.Fori(0, OVF) as t:
                        e = s.value_load(ovf_i[0:1, bass.ds(t + 1, 1)], min_val=0, max_val=NE - 1)
                        s.dma_start(ow[:, 0, :], wg[bass.ds(e, 1)].rearrange("o p f -> (o p) f")).then_inc(o["ld"], 16)
                        s.dma_start(ow[:, 1, :], wu[bass.ds(e, 1)].rearrange("o p f -> (o p) f")).then_inc(o["ld"], 16)
                        s.dma_start(ow[:, 2, :].rearrange("p (f n) -> p f n", f=2),
                                    wd[bass.ds(e, 1)].rearrange("o p f n -> (o p) f n")).then_inc(o["ld"], 16)
                        here = slots_dram[bass.ds(t * SLOTS + NE * SLOTS, SLOTS), :]
                        s.dma_start(xs[0:SLOTS, 0].rearrange("p c f -> p (c f)"), here).then_inc(o["ld"], 16)
                        s.wait_ge(o["gu"], t + 1)
                        s.activation(sg[:, 0].rearrange("p f s -> p (f s)"), ps[:, 2, 0:2 * SLOTS], ACT.Silu)\
                            .then_inc(o["silu"], 1)
                        s.wait_ge(o["dn"], t + 1)
                        s.activation(ye[0:SLOTS, 0, 0:512], ps[0:SLOTS, 4, :], ACT.Copy).then_inc(o["y"], 1)
                        s.wait_ge(o["y"], t * 2 + 2)
                        s.dma_start(here, ye[0:SLOTS, 0, :]).then_inc(o["st"], 16)
                        s.wait_ge(o["st"], t * 16 + 16)
                s.sem_inc(moe_over, 1)

            norm_a(1, lambda e, t: e.wait_ge(back_add, DC) if t == 0 else None)
            moe_a(0)
            norm_a(2, lambda e, t: e.wait_ge(moe_comb, t + 1))
            norm_high(2, 18, kvqh)
            high(KVQC, KVQ0, 0, gain=1)
            kout = out["k_prompt"].rearrange("b g s h m d -> (b g) s (h m d)")
            kst = (kvq_kst0, kvq_kst1)
            for n in range(3 * DC):
                kind, h = divmod(n, DC)
                if n + 1 < 3 * DC:
                    high(KVQC + n + 1, kvq_block((n + 1) // 2), (n + 1) % 2, gain=1 if n + 1 < DC else 4)
                if DC + 2 <= n < 2 * DC + 2:
                    kh = n - DC - 2
                    s.wait_ge(kvq_ev, DC + kh + 1)
                    s.dma_start(kout[:, :, kh * P:(kh + 1) * P].rearrange("g s f -> s g f"),
                                ktok[:, kh % 2].rearrange("p (t f) -> p t f", t=NT)).then_inc(kst[kh % 2], 16)
                s.wait_ge(mm, done(KVQC + n))
                if n >= 2 * DC + 2:
                    s.wait_ge(kvq_tp, n - 1)
                dst = (qT[:, h, :], kT[:, h, :], vtmp[:, n % 2, :])[kind]
                bank = 2 * (n % 2)
                s.activation(dst.rearrange("p (h t) -> p h t", h=2), ps[:, bank:bank + 2, 0:HALF], ACT.Copy)\
                    .then_inc(kvq_cp, 1)
            s.wait_ge(kvq_ev, 3 * DC)
            s.dma_start(out["k_sample"].rearrange("b o h m d -> (b o) (h m d)"), tok8[:, 0, :]).then_inc(kvq_vst, 16)
            s.dma_start(out["v_sample"].rearrange("b o h d -> (b o) (h d)"), tok8[:, 1, :]).then_inc(kvq_vst, 16)
            vout = out["v_prompt"].rearrange("b g s h d -> (b g) s (h d)")
            for t in range(NT):
                s.dma_start(vout[t], vtok[:, t, :]).then_inc(rows_out, 16)

            def make_bias(h):
                if h >= 2:
                    s.wait_ge(att_neg, 4 * (h - 1))
                s.activation(bias8[:, h % 2, :], c_["dist"], ACT.Copy, scale=-8.0 * 2.0 ** -(h + 1))\
                    .then_inc(att_bias, 1)

            s.wait_ge(dec_prod, EARLY)
            s.wait_ge(kvq_kst0, 16 * DC // 2)
            s.wait_ge(kvq_kst1, 16 * DC // 2)
            make_bias(0)
            steps = NH * NT
            for k in range(steps + 2):
                if k < steps:
                    h, q = divmod(k, NT)
                    w = (q + 1) * P
                    if q == 1 and h + 1 < NH:
                        make_bias(h + 1)
                    s.wait_ge(att_neg, k + 1)
                    for mp in range(2):
                        ins = s.activation(st[:, k % 3, mp * SEQ:mp * SEQ + w], st[:, k % 3, mp * SEQ:mp * SEQ + w],
                                           ACT.Exp, bias=nm[:, k % 2, mp:mp + 1],
                                           accum_out=zz[:, k % 2, mp:mp + 1])
                    ins.then_inc(att_ex, 1)
                if k == DEC_JOIN:
                    s.wait_ge(dec_aTp, 1)
                    s.activation(daT.rearrange("p g c -> p (g c)"), ps[:, 5, 0:PAGES * NB * NH], ACT.Copy)
                    s.activation(daown, ps[0:NB * NH, 5, 256:257], ACT.Copy).then_inc(dec_aT, 1)
                if k >= 2:
                    n = k - 2
                    h, q = divmod(n, NT)
                    s.wait_ge(att_pv, n + 1)
                    s.activation(otok[:, q, h * P:(h + 1) * P], ps[:, 6 + n % 2, 0:P], ACT.Copy,
                                 scale=rz[:, n % 4, 0:1])
                    if n >= 1:
                        s.wait_ge(att_o, n)
                    s.activation(osq, ps[:, 6 + n % 2, 0:P], ACT.Square, scale=rz[:, n % 4, 0:1],
                                 accum_out=oss[:, q, h:h + 1]).then_inc(att_o, 1)
                if 1 <= k <= steps:
                    n = k - 1
                    w = (n % NT + 1) * P
                    s.wait_ge(att_tp, n + 1)
                    if n >= 2:
                        s.wait_ge(att_pv, n - 1)
                    s.activation(aT[:, n % 2, 0:w], ps[:, 4, 0:w], ACT.Copy).then_inc(att_aT, 1)
                if k == DEC_JOIN - 2:
                    s.wait_ge(dec_max, 1)
                    s.activation(dS, dS, ACT.Exp, bias=dsm[:, 2:3], accum_out=dsm[:, 3:4]).then_inc(dec_ex, 1)
            s.wait_ge(dec_dt, 1)
            s.activation(doT, ps[:, 4, 0:NB * NH], ACT.Copy).then_inc(dec_o, 1)
            s.wait_ge(att_var, 1)
            s.activation(root[:, 0:NT * NH], oss.rearrange("p t h -> p (t h)"), ACT.Sqrt).then_inc(att_root, 1)
            for t in range(NT):
                for half in range(2):
                    s.wait_ge(att_tp2, 2 * t + half + 1)
                    s.activation(oh[:, 4 * half:4 * half + 4, t * P:(t + 1) * P],
                                 ps[:, (2 * t + half) % 4, :].rearrange("p (c f) -> p c f", c=4), ACT.Copy,
                                 scale=subg[:, 0:1]).then_inc(att_ev, 1)
                if t == 0:
                    s.wait_ge(dec_sq, 1)
                    s.activation(dsm[0:64, 9:10], dsm[0:64, 8:9], ACT.Sqrt).then_inc(dec_root, 1)
            s.wait_ge(dec_otp2, 1)
            s.activation(oh[:, :, SEQ:T], ps[:, 7, 0:NB * NH].rearrange("p (b h) -> p h b", b=NB), ACT.Copy,
                         scale=subg[:, 0:1]).then_inc(dec_ev, 1)
            high(AOC, AO0, 0)
            for n in range(DC):
                if n + 1 < DC:
                    high(AOC + n + 1, AO0 + (n + 1) // 2, (n + 1) % 2)
                copy_out(AOC + n, n, DC)
            s.wait_ge(rows_out, 16 * (1 + NT))
            norm_a(3, lambda e, t: e.wait_ge(back_add, 2 * DC) if t == 0 else None)
            moe_a(1)
            norm_a(4, lambda e, t: e.wait_ge(moe_comb, 5 + t + 1), normed=False)

        @block.tensor
        def _(pe):
            def product(chunk, pair, w, rhs_h, rhs_l, i=0, first=True, last=True):
                pe.wait_ge(split_lo, i * 12 + (chunk + 1))
                for c in range(DC):
                    for half in range(2):
                        to = ps[:, 2 * pair + half, 0:HALF]
                        x_h = rhs_h(c, half)
                        pe.matmul(to, wh[:, chunk % 2, c, :], x_h, start=first and c == 0, stop=False)
                        pe.matmul(to, w[:, c, :], x_h, start=False, stop=False)
                        ins = pe.matmul(to, wh[:, chunk % 2, c, :], rhs_l(c, half),
                                        start=False, stop=last and c == DC - 1)
                ins.then_inc(mm, 1)

            def of(t):
                return lambda c, half: t[:, c, half * HALF:(half + 1) * HALF]

            def turn(src, bank, sbank, prompt=True):
                if prompt:
                    for t in range(NT):
                        pe.transpose(ps[:, bank, t * P:(t + 1) * P], src[:, t * P:(t + 1) * P], ident)
                return pe.transpose(ps[0:NB, sbank, 0:P], src[:, SEQ:T], ident)

            def norm_t(n, evs, layer=None):
                def logits(t):
                    pe.wait_ge(norm_ev, evs + min(2 * t + 2, 9))
                    for c in range(DC):
                        ins = pe.matmul(ps[0:rows_of(t), 5, t * 20:(t + 1) * 20], hT[:, c, cols_of(t)],
                                        wr[:, layer, c, :], start=c == 0, stop=c == DC - 1)
                    if t == NT:
                        ins.then_inc(moe_lg, 1)

                for t in range(5):
                    if layer is not None and t >= 2:
                        logits(t - 2)
                    pe.wait_ge(norm_xn, 5 * n + t + 1)
                    r = rows_of(t)
                    if t == NT:
                        for c in range(DC):
                            ins = pe.transpose(ps[:, 4, c * NB:(c + 1) * NB], xn[0:r, t, c, :], ident[0:r, 0:r])
                        ins.then_inc(norm_tp, 1)
                        continue
                    for half in range(2):
                        if t >= 2:
                            pe.wait_ge(norm_ev, evs + 2 * (t - 2) + half + 1)
                        for c in range(4):
                            ins = pe.transpose(ps[:, 2 * (t % 2) + half, c * P:(c + 1) * P],
                                               xn[:, t, 4 * half + c, :], ident)
                        ins.then_inc(norm_tp, 1)
                if layer is not None:
                    logits(NT - 1)
                    logits(NT)

            pe.wait_ge(ld_c, 16)
            norm_t(0, 0)
            pe.wait_ge(ld_w, 16 * N_SMALL)
            for g in range(NG):
                ins = pe.transpose(ps[:, 5 + g // 4, (g % 4) * P:(g % 4 + 1) * P], w_st[:, g, :], ident)
            ins = pe.transpose(ps[:, 7, 0:GC], sg_st, ident[0:GC, 0:GC])
            ins.then_inc(prep_tp, 1)
            pe.wait_ge(norm_lo, 5)
            pe.sem_inc(mm, 1)
            for part in range(2):
                if part == 1:
                    pe.wait_ge(prep_v, 1)
                with pe.Fori(0, 2) as i:
                    def turn_v(c):
                        pe.wait_ge(uv_gelu, i * 12 + (24 + c + 2))
                        pe.wait_ge(uv_ev, i * 12 + (max(c - 1, 0) + 1))
                        for t in range(NT):
                            ins = pe.transpose(ps[:, 4 + c % 2, t * P:(t + 1) * P],
                                               vtmp[:, c % 2, t * P:(t + 1) * P], ident)
                        ins.then_inc(uv_tp, 1)

                    for c in range(12):
                        pe.wait_ge(uv_gelu, i * 12 + (max(c - 1, 0) + 1 if part == 0 else 24 + c))
                        product(24 * part + c, c % 2, low_parts(UV0 + 12 * part + c // 2, c % 2),
                                of(hh), of(hT_parts), i)
                        if part == 1 and c >= 1:
                            turn_v(c - 1)
                    if part == 1:
                        turn_v(11)
            pe.wait_ge(gate_v8, 1)
            pe.matmul(ps[:, 5, 0:GC * NB], ones, v8sq, start=True, stop=True).then_inc(gate_vt, 1)
            pe.wait_ge(gate_vn_v, 2)
            pe.wait_ge(gate_vn_a, 2)
            for j in range(GC):
                if j >= 4:
                    pe.wait_ge(gate_tmp, j - 3)
                for t in range(NT):
                    ins = pe.matmul(ps[:, j % 4, t * P:(t + 1) * P], v[:, t, j * P:(j + 1) * P],
                                    ws[:, t, j * P // GCOLS, :], start=True, stop=True)
                ins.then_inc(gate_sp, 1)

            def turn_back(n, before):
                pe.wait_ge(back_cp, before + n + 1)
                if n >= 2:
                    pe.wait_ge(back_add, before + n - 1)
                turn(vtmp[:, n % 2, :], 4 + n % 2, 6 + n % 2).then_inc(back_tp, 1)

            pe.wait_ge(gate_tmp, GC)
            pe.wait_ge(gate_vs, 1)
            for k in range(GC):
                ins = pe.transpose(ps[0:NB, 2 + k // 4, (k % 4) * P:(k % 4 + 1) * P], v8n[:, k * NB:(k + 1) * NB],
                                   ident)
            ins.then_inc(gate_vt, 1)
            for n in range(DC):
                if n >= 2:
                    pe.wait_ge(back_cp, n - 1)
                if n == 1:
                    pe.wait_ge(gate_v8, 2)
                for kb in range(3):
                    if n == 0:
                        pe.wait_ge(u_lo, 8 * kb + 8)
                    product(GOC + 3 * n + kb, n % 2, low_parts(GO0 + n // 2 * 3 + kb, n % 2),
                            lambda c, half: uh[:, 8 * kb + c, half * HALF:(half + 1) * HALF],
                            lambda c, half: ul[:, 8 * kb + c, half * HALF:(half + 1) * HALF],
                            first=kb == 0, last=kb == 2)
                if n >= 1:
                    turn_back(n - 1, 0)
            turn_back(DC - 1, 0)

            def moe_t(layer):
                o, before = ovfs[layer], layer * NE
                pe.wait_ge(moe_mk, layer + 1)
                counts = ps[:, 6, 0:6 * NE]
                pe.matmul(counts, c_["tri"], R["m"].rearrange("p t e -> p (t e)"), start=True, stop=False)
                pe.matmul(counts, ones, R["before"].rearrange("p t e -> p (t e)"), start=False, stop=True)\
                    .then_inc(moe_cum, 1)

                def turn_rows(i, k):
                    pe.wait_ge((moe_ld0, moe_ld1)[k % 2], i * 16 + (8 * before + k // 2 * 16 + 16))
                    if not (isinstance(i, int) and k == 0):
                        pe.wait_ge(moe_tev, i * 2 + (before + k))
                    for c in range(DC):
                        ins = pe.transpose(ps[:, c // 4, (c % 4) * SLOTS:(c % 4 + 1) * SLOTS],
                                           xs[0:SLOTS, k % 2, c, :], ident[0:SLOTS, 0:SLOTS])
                    ins.then_inc(moe_tp, 1)

                def gate_up(i, k, b):
                    q = k % 2
                    slot_loaded(pe, b, i)
                    slot_loaded(pe, b + 1, i)
                    pe.wait_ge(moe_tev, i * 2 + (before + k + 1))
                    if k >= 1:
                        pe.wait_ge(moe_hid, i * 2 + (before + k - 1))
                    for f in range(4):
                        w = ringslot(b + f // 2, (DC, DE))
                        for c in range(DC):
                            ins = pe.matmul(ps[:, 2 + q, f * SLOTS:(f + 1) * SLOTS],
                                            w[:, c, (f % 2) * P:(f % 2 + 1) * P], xsT[:, q, c, :],
                                            start=c == 0, stop=c == DC - 1)
                    ins.then_inc(moe_gu, 1)

                def down(i, k, b):
                    q = k % 2
                    slot_loaded(pe, b, i)
                    pe.wait_ge(moe_hid, i * 2 + (before + k + 1))
                    if isinstance(i, int) and k >= 2:
                        pe.wait_ge(moe_ya, before + k - 1)
                        pe.wait_ge(moe_yv, before + k - 1)
                    if not isinstance(i, int):
                        pe.wait_ge(moe_ya, i * 2 + (before + max(k - 1, 0)))
                        pe.wait_ge(moe_yv, i * 2 + (before + max(k - 1, 0)))
                    w = ringslot(b, (2, D))
                    for half in range(2):
                        for f in range(2):
                            ins = pe.matmul(ps[0:SLOTS, 4 + 2 * q + half, :], hid[:, q, f, :],
                                            w[:, f, half * 512:(half + 1) * 512], start=f == 0, stop=f == 1)
                    ins.then_inc(moe_dn, 1)

                base = MOE0 if layer == 0 else MOE1
                turn_rows(0, 0)
                gate_up(0, 0, base)
                turn_rows(0, 1)
                pe.wait_ge(moe_idx, layer + 1)
                gate_up(0, 1, base + 2)
                down(0, 0, base + 4)
                turn_rows(0, 2)
                gate_up(0, 2, base + 5)
                down(0, 1, base + 7)
                turn_rows(0, 3)
                with pe.Fori(0, 6) as i:
                    for k in range(2):
                        b = base + 8 + 3 * k
                        gate_up(i, 3 + k, b)
                        down(i, 2 + k, b + 2)
                        turn_rows(i, 4 + k)
                gate_up(0, 15, base + 44)
                down(0, 14, base + 46)
                down(0, 15, base + 47)
                n_ovf = pe.value_load(ovf_i[0:1, 0:1], min_val=0, max_val=OVF)
                with pe.If(n_ovf > 0):
                    with pe.Fori(0, OVF) as t:
                        pe.wait_ge(o["ld"], t * 64 + 64)
                        for c in range(DC):
                            ins = pe.transpose(ps[:, c // 4, (c % 4) * SLOTS:(c % 4 + 1) * SLOTS],
                                               xs[0:SLOTS, 0, c, :], ident[0:SLOTS, 0:SLOTS])
                        ins.then_inc(o["tp"], 1)
                        pe.wait_ge(o["tev"], t + 1)
                        for f in range(4):
                            w = ow[:, f // 2, :].rearrange("p (c n) -> p c n", c=DC)
                            for c in range(DC):
                                ins = pe.matmul(ps[:, 2, f * SLOTS:(f + 1) * SLOTS],
                                                w[:, c, (f % 2) * P:(f % 2 + 1) * P], xsT[:, 0, c, :],
                                                start=c == 0, stop=c == DC - 1)
                        ins.then_inc(o["gu"], 1)
                        pe.wait_ge(o["hid"], t + 1)
                        w = ow[:, 2, :].rearrange("p (f n) -> p f n", f=2)
                        for half in range(2):
                            for f in range(2):
                                ins = pe.matmul(ps[0:SLOTS, 4 + half, :], hid[:, 0, f, :],
                                                w[:, f, half * 512:(half + 1) * 512], start=f == 0, stop=f == 1)
                        ins.then_inc(o["dn"], 1)

            norm_t(1, 9, 0)
            pe.wait_ge(norm_ev, 18)
            moe_t(0)
            norm_t(2, 18)
            pe.wait_ge(norm_lo, 10)

            def turn_kvq(n):
                kind, h = divmod(n, DC)
                pe.wait_ge(kvq_cp, n + 1)
                if n >= 2:
                    pe.wait_ge(kvq_ev, n - 1)
                src = (qT[:, h, :], kT[:, h, :], vtmp[:, n % 2, :])[kind]
                turn(src, 4 + n % 2, 6 + n % 2, kind > 0).then_inc(kvq_tp, 1)

            for n in range(3 * DC):
                if n >= 2:
                    pe.wait_ge(kvq_cp, n - 1)
                product(KVQC + n, n % 2, low_parts(kvq_block(n // 2), n % 2), of(kvqh), of(hT_parts))
                if n >= 1:
                    turn_kvq(n - 1)
            turn_kvq(3 * DC - 1)
            pe.wait_ge(kvq_cp, 3 * DC)
            pe.wait_ge(kvq_ev, 3 * DC)
            steps = NH * NT
            for k in range(steps + 3):
                if k < steps:
                    h, q = divmod(k, NT)
                    if k >= 2:
                        pe.wait_ge(att_neg, k - 1)
                    for mp in range(2):
                        ins = pe.matmul(ps[:, 2 * (k % 2) + mp, 0:(q + 1) * P],
                                        qT[mp * HD:(mp + 1) * HD, h, q * P:(q + 1) * P],
                                        kT[mp * HD:(mp + 1) * HD, h, 0:(q + 1) * P], start=True, stop=True)
                    ins.then_inc(att_qk, 1)
                if k >= 3:
                    n = k - 3
                    h, q = divmod(n, NT)
                    pe.wait_ge(att_aT, n + 1)
                    if n >= 2:
                        pe.wait_ge(att_o, n - 1)
                    for c in range(q + 1):
                        ins = pe.matmul(ps[:, 6 + n % 2, 0:P], aT[:, n % 2, c * P:(c + 1) * P],
                                        vtok[:, c, h * P:(h + 1) * P], start=c == 0, stop=c == q)
                    ins.then_inc(att_pv, 1)
                if 2 <= k < steps + 2:
                    n = k - 2
                    pe.wait_ge(att_a, n + 1)
                    if n >= 1:
                        pe.wait_ge(att_aT, n)
                    for c in range(n % NT + 1):
                        ins = pe.transpose(ps[:, 4, c * P:(c + 1) * P], st[:, n % 3, c * P:(c + 1) * P],
                                           ident)
                    ins.then_inc(att_tp, 1)
                if k == DEC_TURN:
                    pe.wait_ge(dec_red, NB * PAGES)
                    for c in range(PAGES):
                        ins = pe.transpose(ps[:, 5, c * P:(c + 1) * P], sK[:, c, :], ident)
                    ins.then_inc(dec_tp, 1)
                if k == DEC_JOIN:
                    pe.wait_ge(dec_c, 1)
                    for c in range(PAGES):
                        pe.matmul(ps[:, 5, c * 64:(c + 1) * 64], dS[:, c * P:(c + 1) * P], dC,
                                  start=True, stop=True)
                    pe.matmul(ps[0:64, 5, 256:257], dC, dS[:, SEQ:SEQ + 1], start=True, stop=True)\
                        .then_inc(dec_aTp, 1)
                if k in DEC_STEPS:
                    n = DEC_STEPS.index(k)
                    b, half = divmod(n, 2)
                    pe.wait_ge(dec_aT, 1)
                    if n >= 1:
                        pe.wait_ge(dec_diag, n)
                    slot_loaded(pe, VP0 + 2 * b)
                    slot_loaded(pe, VP0 + 2 * b + 1)
                    for c in range(PAGES):
                        ins = pe.matmul(ps[0:4, 5, :], daT[:, c, 4 * n:4 * n + 4],
                                        ringslot(VP0 + 2 * b + c // 2, (2, D))[:, c % 2, half * 512:(half + 1) * 512],
                                        start=c == 0, stop=c == PAGES - 1)
                    ins.then_inc(dec_pv, 1)
            pe.wait_ge(dec_diag, 2 * NB)
            for n in range(2 * NB):
                ins = pe.transpose(ps[:, 4, 4 * n:4 * n + 4], dor[:, n, :], ident[0:4, 0:4])
            ins.then_inc(dec_dt, 1)
            pe.wait_ge(dec_o, 1)
            pe.wait_ge(att_o, steps)
            pe.transpose(ps[0:64, 6, 0:P], doT, ident).then_inc(dec_otp, 1)
            pe.wait_ge(att_neg, steps)
            for t in range(NT):
                pe.wait_ge(att_on, t + 1)
                for half in range(2):
                    if t >= 2:
                        pe.wait_ge(att_lo, 2 * (t - 2) + half + 1)
                    for c in range(4):
                        ins = pe.transpose(ps[:, (2 * t + half) % 4, c * P:(c + 1) * P],
                                           otok[:, t, (4 * half + c) * P:(4 * half + c + 1) * P], ident)
                    ins.then_inc(att_tp2, 1)
            pe.wait_ge(dec_o2, 1)
            pe.transpose(ps[:, 7, 0:64], do64, ident[0:64, 0:64]).then_inc(dec_otp2, 1)
            pe.wait_ge(att_lo, 2 * NT + 1)
            for n in range(DC):
                if n >= 2:
                    pe.wait_ge(back_cp, DC + n - 1)
                product(AOC + n, n % 2, low_parts(AO0 + n // 2, n % 2), of(oh), of(hT_parts))
                if n >= 1:
                    turn_back(n - 1, DC)
            turn_back(DC - 1, DC)
            norm_t(3, 27, 1)
            pe.wait_ge(norm_ev, 36)
            moe_t(1)

        @block.vector
        def _(e):
            def norm_v(n, ready, gain, into, normed=True):
                for t in vector_tiles(n):
                    ready(e, t)
                    e.tensor_tensor_reduce(xn[:, t].rearrange("p c f -> p (c f)"), x[:, t, :], x[:, t, :], 1.0, 0.0,
                                           ALU.mult, ALU.add, ss[:, t:t + 1]).then_inc(norm_sq_v, 1)
                e.wait_ge(norm_sq_a, sum(len(scalar_tiles(m)) for m in range(n + 1)))
                e.wait_ge(norm_sq_v, sum(len(vector_tiles(m)) for m in range(n + 1)))
                e.tensor_scalar(ss[:, :], ss[:, :], 1.0 / D, EPS, ALU.mult, ALU.add).then_inc(norm_var, 1)
                e.wait_ge(norm_root, n + 1)
                e.reciprocal(rstd[:, :], root[:, 0:5]).then_inc(norm_rs, 1)
                if not normed:
                    return
                if n == 1:
                    e.wait_ge(rows_out, 16)
                if n == 0:
                    e.wait_ge(ld_w, 16 * N_SMALL)
                before = 9 * n
                for t in range(5):
                    for half in range(2 if t < NT else 1):
                        e.wait_ge(norm_tp, before + 2 * t + half + 1)
                        for g_row, dst in zip(gain, into):
                            if t < NT:
                                src = ps[:, 2 * (t % 2) + half, :].rearrange("p (c f) -> p c f", c=4)
                                to = dst[:, 4 * half:4 * half + 4, t * P:(t + 1) * P]
                                gb = gains[:, g_row or 0, 4 * half:4 * half + 4].unsqueeze(2)\
                                    .broadcast_to([P, 4, P])
                            else:
                                src = ps[:, 4, 0:DC * NB].rearrange("p (c f) -> p c f", c=DC)
                                to = dst[:, :, SEQ:T]
                                gb = gains[:, g_row or 0, :].unsqueeze(2).broadcast_to([P, DC, NB])
                            if g_row is None:
                                e.tensor_copy(to, src).then_inc(norm_ev, 1)
                            else:
                                e.tensor_tensor(to, src, gb, ALU.mult).then_inc(norm_ev, 1)

            def low(chunk, b, half, i=0, per=0, gain=None):
                e.wait_ge(split_hi, i * per + (chunk + 1))
                w = ringslot(b, (DC, 256))[:, :, half * P:(half + 1) * P]
                if gain is None:
                    e.tensor_tensor(low_parts(b, half), w, plain(wh[:, chunk % 2]), ALU.subtract).then_inc(split_lo, 1)
                    return
                for c in range(DC):
                    ins = e.scalar_tensor_tensor(low_parts(b, half)[:, c, :], w[:, c, :], gains[:, gain, c:c + 1],
                                                 plain(wh[:, chunk % 2, c, :]), ALU.mult, ALU.subtract)
                ins.then_inc(split_lo, 1)

            def norm_low(his, high):
                for t in range(5):
                    e.wait_ge(norm_hi, his + t + 1)
                    e.tensor_tensor(hT_parts[:, :, cols_of(t)], hT[:, :, cols_of(t)], plain(high[:, :, cols_of(t)]),
                                    ALU.subtract).then_inc(norm_lo, 1)

            e.memset(ss[:, :], 1.0)
            e.memset(vss[:, :, :], 0.0).then_inc(prep_init, 1)
            e.wait_ge(prep_init, 1)
            norm_v(0, lambda q, t: q.wait_ge(ld_x[t], 16), [0], [hT])
            norm_low(0, hh)
            low(UVC, UV0, 0)
            e.wait_ge(ld_c, 16)
            e.wait_ge(prep_tp, 1)
            for half in range(2):
                e.tensor_tensor(wT[:, 4 * half:4 * half + 4, :],
                                ps[:, 5 + half, :].rearrange("p (g t) -> p g t", g=4),
                                c_["causal"].unsqueeze(1).broadcast_to([P, 4, P]), ALU.mult)
            e.tensor_copy(sgain[:, :], ps[:, 7, 0:GC])
            for layer in range(2):
                e.tensor_copy(wr[:, layer, :, 0:NEG], wrg_st[:, layer, :].rearrange("p (c g) -> p c g", c=DC))
                for q in range(NEG):
                    e.tensor_copy(wr[:, layer, :, NEG + 4 * q:NEG + 4 * q + 4],
                                  wre_st[:, layer, q, :].rearrange("p (c k) -> p c k", c=DC))
            link(e, e.tensor_tensor(lam_st[:, 0, :], lam_st[:, 0, :], lam_st[:, 1, :], ALU.mult))
            e.tensor_reduce(lam_s[:, 0:2], lam_st[:, 0, :].rearrange("p (m d) -> p m d", m=2), AX_X, ALU.add)\
                .then_inc(prep_lam, 1)
            e.wait_ge(prep_lame, 1)
            link(e, e.tensor_tensor(lam_s[:, 4:5], lam_s[:, 3:4], lam_s[:, 2:3], ALU.subtract))
            e.tensor_scalar(neglam[:, :], lam_s[:, 4:5], -LAM_INIT, None, ALU.add)
            e.tensor_scalar(subg[:, :], subg[:, :], 1.0 - LAM_INIT, None, ALU.mult).then_inc(prep_v, 1)

            e.sem_inc(uv_ev, 1)
            for part in range(2):
                if part == 1:
                    e.wait_ge(zeroed, 16 * -(-ROWS // P))
                with e.Fori(0, 2) as i:
                    def evac(c):
                        e.wait_ge(uv_tp, i * 12 + (c + 1))
                        e.tensor_copy(v[:, :, bass.ds(i * (12 * P) + c * P, P)],
                                      ps[:, 4 + c % 2, :].rearrange("p (t f) -> p t f", t=NT))
                        e.tensor_copy(vd[:, bass.ds(i * (12 * NB) + c * NB, NB)], vtmp[:, c % 2, SEQ:T])\
                            .then_inc(uv_ev, 1)

                    for c in range(12):
                        n = 24 * part + c + 1
                        low(n, UV0 + n // 2, n % 2, i, 12)
                        if part == 1 and c >= 1:
                            evac(c - 1)
                    if part == 1:
                        evac(11)
            e.wait_ge(uv_ev, GC + 1)
            e.tensor_tensor(v8sq, vd[:, :], vd[:, :], ALU.mult).then_inc(gate_v8, 1)
            e.wait_ge(uv_sq, GC + 1)
            e.tensor_reduce(gss[:, 0, 0:NT], vss[:, :, :], AX_X, ALU.add)
            e.wait_ge(gate_vt, 1)
            link(e, e.tensor_reduce(gss[:, 0, NT:NT + NB], ps[:, 5, 0:GC * NB].rearrange("p (j b) -> p b j", b=NB),
                                    AX_X, ALU.add))
            e.tensor_scalar(gss[:, 0], gss[:, 0], 1.0 / DG, EPS, ALU.mult, ALU.add).then_inc(gate_var, 1)
            e.wait_ge(gate_root, 1)
            e.reciprocal(gss[:, 2], gss[:, 1]).then_inc(gate_rs, 1)
            e.wait_ge(gate_rs, 1)
            for t in (0, 2):
                e.tensor_scalar(ws[:, t], wT[:, :, :], gss[:, 2, t:t + 1], None, ALU.mult).then_inc(gate_vn_v, 1)
            link(e, e.tensor_tensor(v8n.rearrange("p (j b) -> p j b", b=NB),
                                    vd[:, :].rearrange("p (j b) -> p j b", b=NB),
                                    sgain[:, :].unsqueeze(2).broadcast_to([P, GC, NB]), ALU.mult))
            e.tensor_tensor(v8n.rearrange("p (j b) -> p j b", b=NB), v8n.rearrange("p (j b) -> p j b", b=NB),
                            gss[:, 2, NT:NT + NB].unsqueeze(1).broadcast_to([P, GC, NB]), ALU.mult)\
                .then_inc(gate_vs, 1)
            e.wait_ge(gate_vs, 1)
            for k, op in enumerate((ALU.mult, ALU.add)):
                link(e, e.tensor_tensor(v8g.rearrange("p (g r) -> p g r", g=NG),
                                        (v8n, v8g)[k].rearrange("p (g r) -> p g r", g=NG),
                                        w00[:, k, :].unsqueeze(2).broadcast_to([P, NG, GC * NB // NG]), op))
            e.tensor_tensor(u[:, :, SEQ:T], v8g.rearrange("p (j b) -> p j b", b=NB), u[:, :, SEQ:T], ALU.mult)\
                .then_inc(gate_su, 1)
            e.wait_ge(ld_bs, 16)
            for j in range(GC):
                e.wait_ge(gate_sp, j + 1)
                if j >= 4:
                    if (j - 4) % 3 == 2:
                        e.wait_ge(gate_uv, (j - 4) // 3 + 1)
                    else:
                        e.wait_ge(gate_u, (j - 4) // 3 * 2 + (j - 4) % 3 + 1)
                e.scalar_tensor_tensor(gtmp[:, j % 4, :].rearrange("p (t f) -> p t f", t=NT),
                                       ps[:, j % 4, :].rearrange("p (t f) -> p t f", t=NT), sgain[:, j:j + 1],
                                       bsg[:, j * P // GCOLS, :].unsqueeze(1).broadcast_to([P, NT, P]),
                                       ALU.mult, ALU.add).then_inc(gate_tmp, 1)
                if j % 3 == 2:
                    e.wait_ge(gate_tmp, j + 1)
                    e.tensor_tensor(u[:, j, 0:SEQ], gtmp[:, j % 4, :], u[:, j, 0:SEQ], ALU.mult).then_inc(gate_uv, 1)

            def add_chunk(n, q):
                e.tensor_tensor(x[:, 0:NT, n], x[:, 0:NT, n], ps[:, 4 + q, :].rearrange("p (t f) -> p t f", t=NT),
                                ALU.add)
                e.tensor_tensor(x[0:NB, NT, n], x[0:NB, NT, n], ps[0:NB, 6 + q, 0:P], ALU.add)\
                    .then_inc(back_add, 1)

            def back_chunk(n, before):
                e.wait_ge(back_tp, before + n + 1)
                add_chunk(slice(n * P, (n + 1) * P), n % 2)

            for j in range(GC):
                e.wait_ge(u_hi, j + 1)
                e.tensor_tensor(ul[:, j, :], u[:, j, :], plain(uh[:, j, :]), ALU.subtract).then_inc(u_lo, 1)
                if j in (7, 15):
                    low(GOC + 1 + j // 8, GO0 + 1 + j // 8, 0)
                if 8 <= j < 14:
                    if j == 8:
                        e.wait_ge(gate_vt, 2)
                    ins = e.tensor_copy(VS[:, (j - 8) * 512:(j - 7) * 512], ps[0:NB, 2 + j - 8, :])
                    if j == 13:
                        ins.then_inc(gate_v8, 1)
            e.wait_ge(again_x, 16 * 5)
            for m in range(2, 3 * DC):
                if m + 1 < 3 * DC:
                    low(GOC + m + 1, GO0 + (m + 1) // 6 * 3 + (m + 1) % 3, (m + 1) // 3 % 2)
                if m % 3 == 2 and m > 2:
                    back_chunk(m // 3 - 1, 0)
            back_chunk(DC - 1, 0)

            def moe_v(layer):
                o, before = ovfs[layer], layer * NE
                grow = 2 + layer
                L, oh, cand = R["l"], R["oh"], R["cand"]

                def first_max(vals, top, onehot, k=NEG):
                    link(e, e.tensor_reduce(top, vals, AX_X, ALU.max))
                    link(e, e.tensor_tensor(cand, vals, top.unsqueeze(2).broadcast_to([P, 5, NEG]), ALU.is_ge))
                    link(e, e.scalar_tensor_tensor(cand, cand, -99.0, iota99, ALU.mult, ALU.add))
                    link(e, e.tensor_reduce(R["least"], cand, AX_X, ALU.min))
                    link(e, e.tensor_tensor(onehot, iota, R["least"].unsqueeze(2).broadcast_to([P, 5, NEG]),
                                            ALU.is_equal))

                iota = c_["iota"].unsqueeze(1).broadcast_to([P, 5, NEG])
                iota99 = c_["iota99"].unsqueeze(1).broadcast_to([P, 5, NEG])
                e.memset(R["m"][:, 5, :], 0.0)
                e.memset(R["before"][:, 0, :], 0.0)
                link(e, e.memset(R["l"][:, NT, :], 0.0))
                e.wait_ge(moe_lg, layer + 1)
                e.tensor_tensor(L[:, 0:NT, :], ps[:, 5, 0:NT * 20].rearrange("p (t k) -> p t k", t=NT),
                                rbias[:, layer, :].unsqueeze(1).broadcast_to([P, NT, 20]), ALU.add)
                link(e, e.tensor_tensor(L[0:NB, NT, :], ps[0:NB, 5, NT * 20:5 * 20], rbias[0:NB, layer, :], ALU.add))
                first_max(L[:, :, 0:NEG], R["gmax"], oh)
                e.tensor_tensor(R["eg"], L[:, :, 0:NEG],
                                R["gmax"].unsqueeze(2).broadcast_to([P, 5, NEG]), ALU.subtract).then_inc(moe_rt, 1)
                link(e, e.tensor_tensor(
                    R["pick"].rearrange("p t (k g) -> p t k g", g=NEG),
                    L[:, :, NEG:20].rearrange("p t (g k) -> p t k g", g=NEG),
                    oh.unsqueeze(2).broadcast_to([P, 5, NEG, NEG]), ALU.mult))
                link(e, e.tensor_reduce(R["el"], R["pick"].rearrange("p t (k g) -> p t k g", g=NEG), AX_X, ALU.add))
                first_max(R["el"], R["m1"], R["oh1"])
                link(e, e.scalar_tensor_tensor(R["el2"], R["oh1"], -BIG, R["el"], ALU.mult, ALU.add))
                first_max(R["el2"], R["m2"], R["oh2"])
                e.tensor_tensor(R["e2"], R["m2"], R["m1"], ALU.subtract).then_inc(moe_rt, 1)
                for j, name in enumerate(("oh1", "oh2")):
                    link(e, e.tensor_tensor(
                        R["mm"][:, j].rearrange("p t (g k) -> p t g k", g=NEG),
                        oh.unsqueeze(3).broadcast_to([P, 5, NEG, NEG]),
                        R[name].unsqueeze(2).broadcast_to([P, 5, NEG, NEG]), ALU.mult))
                for j in range(2):
                    link(e, e.tensor_scalar(R["mm"][:, j, NT, :], R["mm"][:, j, NT, :], c_["valid"], None, ALU.mult))
                link(e, e.tensor_tensor(R["m"][:, 0:5], R["mm"][:, 0], R["mm"][:, 1], ALU.add))
                for t in range(5):
                    ins = e.tensor_tensor(R["before"][:, t + 1], R["before"][:, t], R["m"][:, t], ALU.add)
                    if t < 4:
                        link(e, ins)
                ins.then_inc(moe_mk, 1)
                e.wait_ge(moe_cum, layer + 1)
                cnt = ps[:, 6, 5 * NE:6 * NE]
                link(e, e.tensor_scalar(R["ov"], cnt, float(SLOTS), None, ALU.is_gt))
                for q in range(2, MAXT + 1):
                    link(e, e.tensor_scalar(R["ov1"], cnt, float(q * SLOTS), None, ALU.is_gt))
                    link(e, e.tensor_tensor(R["ov"], R["ov"], R["ov1"], ALU.add))
                lt = c_["lt"].rearrange("p (a b) -> p a b", a=NE)
                link(e, e.tensor_tensor(R["big"], lt,
                                        R["ov"].unsqueeze(1).broadcast_to([P, NE, NE]), ALU.mult))
                link(e, e.tensor_reduce(R["ob"], R["big"], AX_X, ALU.add))
                link(e, e.tensor_scalar(R["dl"], R["ob"], float(SLOTS), float((NE - 1) * SLOTS), ALU.mult, ALU.add))
                link(e, e.tensor_tensor(R["dl"], R["dl"], c_["first"], ALU.subtract))
                pos = ps[:, 6, 0:5 * NE].rearrange("p (t k) -> p t k", t=5)
                link(e, e.tensor_scalar(R["ge"], pos, float(SLOTS), None, ALU.is_ge))
                link(e, e.tensor_tensor(R["ge"], R["ge"], R["dl"].unsqueeze(1).broadcast_to([P, 5, NE]), ALU.mult))
                link(e, e.tensor_tensor(R["ge"], R["ge"], c_["first"].unsqueeze(1).broadcast_to([P, 5, NE]), ALU.add))
                link(e, e.tensor_tensor(R["ge"], R["ge"], pos, ALU.add))
                for j in range(2):
                    link(e, e.tensor_tensor(R["mm"][:, j], R["mm"][:, j], R["ge"], ALU.mult))
                    link(e, e.tensor_reduce(slot_f[:, :, j], R["mm"][:, j], AX_X, ALU.add))
                e.tensor_copy(slot_i[:, :].rearrange("p (t j) -> p t j", j=2), slot_f[:, :, :]).then_inc(moe_idx, 1)
                e.wait_ge(moe_ex, 2 * layer + 2)
                link(e, e.tensor_reduce(R["gs"], R["eg"], AX_X, ALU.add))
                link(e, e.tensor_scalar(R["den"], R["e2"], 1.0, None, ALU.add))
                link(e, e.tensor_tensor(R["den"], R["den"], R["gs"], ALU.mult))
                link(e, e.reciprocal(R["den"], R["den"]))
                e.tensor_copy(pair_w[:, :, 0], R["den"])
                e.tensor_tensor(pair_w[:, :, 1], R["den"], R["e2"], ALU.mult)
                tile_ = c_["tile"][0:1].unsqueeze(2).broadcast_to([1, OVF, NE])
                link(e, e.tensor_tensor(R["oe"], tile_, R["ob"][0:1].unsqueeze(1).broadcast_to([1, OVF, NE]),
                                        ALU.is_ge))
                link(e, e.tensor_tensor(R["oend"], R["ob"][0:1], R["ov"][0:1], ALU.add))
                link(e, e.tensor_tensor(R["oe2"], tile_, R["oend"].unsqueeze(1).broadcast_to([1, OVF, NE]),
                                        ALU.is_lt))
                link(e, e.tensor_tensor(R["oe"], R["oe"], R["oe2"], ALU.mult))
                link(e, e.tensor_tensor(R["oe"], R["oe"], c_["eid"][0:1].unsqueeze(1).broadcast_to([1, OVF, NE]),
                                        ALU.mult))
                link(e, e.tensor_reduce(R["of"][:, 1:1 + OVF], R["oe"], AX_X, ALU.add))
                link(e, e.tensor_reduce(R["of"][:, 0:1], R["ov"][0:1], AX_X, ALU.add))
                e.tensor_copy(ovf_i[:, :], R["of"])

                gainx = gains[:, grow, :].rearrange("p (h c) -> p h c", h=2).unsqueeze(3)\
                    .broadcast_to([P, 2, 4, SLOTS])

                def evac_rows(i, k):
                    e.wait_ge(moe_tp, i * 2 + (before + k + 1))
                    if k >= 2:
                        e.wait_ge(moe_gu, i * 2 + (before + k - 1))
                    e.tensor_tensor(xsT[:, k % 2].rearrange("p (h c) s -> p h c s", h=2),
                                    ps[:, 0:2, 0:4 * SLOTS].rearrange("p h (c s) -> p h c s", c=4), gainx,
                                    ALU.mult).then_inc(moe_tev, 1)

                def hidden(i, k):
                    q = k % 2
                    e.wait_ge(moe_silu, i * 2 + (before + k + 1))
                    if k >= 2:
                        e.wait_ge(moe_dn, i * 2 + (before + k - 1))
                    e.tensor_tensor(hid[:, q].rearrange("p f s -> p (f s)"), sg[:, q].rearrange("p f s -> p (f s)"),
                                    ps[:, 2 + q, 2 * SLOTS:4 * SLOTS], ALU.mult).then_inc(moe_hid, 1)

                def y_half(i, k):
                    e.wait_ge(moe_dn, i * 2 + (before + k + 1))
                    e.wait_ge((moe_st0, moe_st1)[k % 2], i * 16 + (8 * before + k // 2 * 16))
                    e.tensor_copy(ye[0:SLOTS, k % 2, 512:1024], ps[0:SLOTS, 5 + 2 * (k % 2), :]).then_inc(moe_yv, 1)

                evac_rows(0, 0)
                hidden(0, 0)
                evac_rows(0, 1)
                for k in (1, 2):
                    hidden(0, k)
                    y_half(0, k - 1)
                    evac_rows(0, k + 1)
                with e.Fori(0, 6) as i:
                    for k in range(2):
                        hidden(i, 3 + k)
                        y_half(i, 2 + k)
                        evac_rows(i, 4 + k)
                hidden(0, 15)
                y_half(0, 14)
                y_half(0, 15)
                n_ovf = e.value_load(ovf_i[0:1, 0:1], min_val=0, max_val=OVF)
                with e.If(n_ovf > 0):
                    with e.Fori(0, OVF) as t:
                        e.wait_ge(o["tp"], t + 1)
                        e.tensor_tensor(xsT[:, 0].rearrange("p (h c) s -> p h c s", h=2),
                                        ps[:, 0:2, 0:4 * SLOTS].rearrange("p h (c s) -> p h c s", c=4), gainx,
                                        ALU.mult).then_inc(o["tev"], 1)
                        e.wait_ge(o["silu"], t + 1)
                        e.tensor_tensor(hid[:, 0].rearrange("p f s -> p (f s)"),
                                        sg[:, 0].rearrange("p f s -> p (f s)"), ps[:, 2, 2 * SLOTS:4 * SLOTS],
                                        ALU.mult).then_inc(o["hid"], 1)
                        e.wait_ge(o["dn"], t + 1)
                        e.tensor_copy(ye[0:SLOTS, 0, 512:1024], ps[0:SLOTS, 5, :]).then_inc(o["y"], 1)
                for t in range(5):
                    r = rows_of(t)
                    e.wait_ge(gathered[t], 32 * (layer + 1))
                    link(e, e.scalar_tensor_tensor(x[0:r, t, :], yg[0:r, t, 0, :], pair_w[0:r, t, 0:1], x[0:r, t, :],
                                                   ALU.mult, ALU.add))
                    e.scalar_tensor_tensor(x[0:r, t, :], yg[0:r, t, 1, :], pair_w[0:r, t, 1:2], x[0:r, t, :],
                                           ALU.mult, ALU.add).then_inc(moe_comb, 1)

            norm_v(1, lambda q, t: q.wait_ge(back_add, DC), [2], [hT])
            moe_v(0)
            norm_v(2, lambda q, t: q.wait_ge(moe_comb, t + 1), [None], [hT])
            norm_low(5, kvqh)
            low(KVQC, KVQ0, 0, gain=1)
            kst = (kvq_kst0, kvq_kst1)

            def early_pages(n):
                return max(n - DC - 1, 0) * EARLY // (2 * DC - 1)

            def sum_page(n):
                b, page = divmod(n, PAGES)
                e.wait_ge(dec_prod, n + 1)
                e.tensor_reduce(sK[:, page, b * 16:(b + 1) * 16],
                                prod[:, n % 2, :].rearrange("p (k d) -> p k d", d=HD), AX_X, ALU.add)\
                    .then_inc(dec_red, 1)

            for m in range(3 * DC + 1):
                if m + 1 < 3 * DC:
                    low(KVQC + m + 1, kvq_block((m + 1) // 2), (m + 1) % 2, gain=1 if m + 1 < DC else 4)
                if m == 0:
                    continue
                n = m - 1
                kind, h = divmod(n, DC)
                e.wait_ge(kvq_tp, n + 1)
                if kind == 1 and h >= 2:
                    e.wait_ge(kst[n % 2], 16 * (h // 2))
                src = ps[:, 4 + n % 2, :].rearrange("p (t f) -> p t f", t=NT)
                if kind == 1:
                    e.tensor_copy(ktok[:, n % 2].rearrange("p (t f) -> p t f", t=NT), src)
                if kind == 2:
                    e.tensor_copy(vtok[:, :, h * P:(h + 1) * P], src)
                e.tensor_copy(tok8[:, (2, 0, 1)[kind], h * P:(h + 1) * P], ps[0:NB, 6 + n % 2, 0:P])\
                    .then_inc(kvq_ev, 1)
                for page in range(early_pages(n), early_pages(n + 1)):
                    sum_page(page)
            e.wait_ge(kvq_ev, 3 * DC)
            own = aT.rearrange("p a s -> p (a s)")[0:NB, :]
            link(e, e.tensor_tensor(own, tok8[:, 2, :], tok8[:, 0, :], ALU.mult))
            e.tensor_reduce(down_, own.rearrange("p (k d) -> p k d", d=HD), AX_X, ALU.add).then_inc(dec_own, 1)
            e.wait_ge(dec_own, 1)
            steps = NH * NT
            for k in range(steps + 1):
                if k - 1 in DEC_STEPS:
                    n = DEC_STEPS.index(k - 1)
                    e.wait_ge(dec_pv, n + 1)
                    link(e, e.tensor_tensor(dmk.rearrange("p (h d) -> p h d", h=4),
                                            ps[0:4, 5, :].rearrange("p (h d) -> p h d", h=4),
                                            ident[0:4, 0:4].unsqueeze(2).broadcast_to([4, 4, P]), ALU.mult))
                    e.tensor_reduce(dor[:, n, :], dmk.rearrange("p (h d) -> p d h", h=4), AX_X, ALU.add)\
                        .then_inc(dec_diag, 1)
                if k < steps:
                    h, q = divmod(k, NT)
                    w = (q + 1) * P
                    e.wait_ge(att_qk, k + 1)
                    e.wait_ge(att_bias, h + 1)
                    if k >= 3:
                        e.wait_ge(att_tp, k - 2)
                    if k == 1:
                        e.wait_ge(kvq_vst, 16 * 2)
                        e.wait_ge(kvq_qst, 16)
                    for mp in range(2):
                        ins = e.tensor_tensor_reduce(st[:, k % 3, mp * SEQ:mp * SEQ + w],
                                                     ps[:, 2 * (k % 2) + mp, 0:w], bias8[:, h % 2, SEQ - w:SEQ],
                                                     HD ** -0.5, -3e38, ALU.add, ALU.max, mx[:, k % 2, mp:mp + 1])
                    link(e, ins)
                    e.tensor_scalar(nm[:, k % 2, :], mx[:, k % 2, :], -1.0, None, ALU.mult).then_inc(att_neg, 1)
                if k >= 1:
                    n = k - 1
                    w = (n % NT + 1) * P
                    q = n % 3
                    e.wait_ge(att_ex, n + 1)
                    if n >= 4:
                        e.wait_ge(att_o, n - 3)
                    link(e, e.reciprocal(rz[:, n % 4, :], zz[:, n % 2, :]))
                    link(e, e.scalar_tensor_tensor(rz[:, n % 4, 1:2], rz[:, n % 4, 1:2], neglam[:, 0:1],
                                                   zz[:, n % 2, 0:1], ALU.mult, ALU.mult))
                    e.scalar_tensor_tensor(st[:, q, 0:w], st[:, q, SEQ:SEQ + w], rz[:, n % 4, 1:2], st[:, q, 0:w],
                                           ALU.mult, ALU.add).then_inc(att_a, 1)
                if k < NB * PAGES - EARLY:
                    sum_page(EARLY + k)
                if k == DEC_TURN:
                    e.wait_ge(ld_past, 16)
                    e.wait_ge(dec_tp, 1)
                    e.tensor_tensor_reduce(dS[:, 0:SEQ], ps[:, 5, :], dbias, HD ** -0.5, -3e38, ALU.add, ALU.max,
                                           dsm[:, 0:1]).then_inc(dec_max0, 1)
                if k == DEC_JOIN - 3:
                    e.wait_ge(dec_max0, 1)
                    e.wait_ge(dec_ownr, 16)
                    link(e, e.tensor_scalar(dS[:, SEQ:SEQ + 1], downc, HD ** -0.5, None, ALU.mult))
                    link(e, e.tensor_tensor(dsm[:, 1:2], dsm[:, 0:1], dS[:, SEQ:SEQ + 1], ALU.max))
                    e.tensor_scalar(dsm[:, 2:3], dsm[:, 1:2], -1.0, None, ALU.mult).then_inc(dec_max, 1)
                if k == DEC_JOIN - 1:
                    link(e, e.scalar_tensor_tensor(dsm[:, 4:5], c_["odd"], neglam[:, 0:1], c_["even"],
                                                   ALU.mult, ALU.add))
                    e.wait_ge(dec_ex, 1)
                    link(e, e.reciprocal(dsm[:, 5:6], dsm[:, 3:4]))
                    link(e, e.tensor_tensor(dsm[:, 6:7], dsm[:, 4:5], dsm[:, 5:6], ALU.mult))
                    e.tensor_scalar(dC, c_["sel"], dsm[:, 6:7], None, ALU.mult).then_inc(dec_c, 1)
            e.wait_ge(att_o, steps)
            e.tensor_scalar(oss, oss, 1.0 / P, EPS, ALU.mult, ALU.add).then_inc(att_var, 1)
            e.wait_ge(att_root, 1)
            link(e, e.reciprocal(orr.rearrange("p t h -> p (t h)"), root[:, 0:NT * NH]))
            for t in range(NT):
                e.tensor_tensor(otok[:, t, :].rearrange("p (h d) -> p h d", h=NH),
                                otok[:, t, :].rearrange("p (h d) -> p h d", h=NH),
                                orr[:, t, :].unsqueeze(2).broadcast_to([P, NH, P]), ALU.mult).then_inc(att_on, 1)
                if t > 0:
                    continue
                e.wait_ge(dec_otp, 1)
                e.wait_ge(dec_vown, 16)
                link(e, e.scalar_tensor_tensor(do64, dvown, daown, ps[0:64, 6, 0:P], ALU.mult, ALU.add))
                link(e, e.tensor_tensor_reduce(dsq, do64, do64, 1.0, 0.0, ALU.mult, ALU.add, dsm[0:64, 7:8]))
                e.tensor_scalar(dsm[0:64, 8:9], dsm[0:64, 7:8], 1.0 / P, EPS, ALU.mult, ALU.add).then_inc(dec_sq, 1)
            e.wait_ge(dec_root, 1)
            link(e, e.reciprocal(dsm[0:64, 10:11], dsm[0:64, 9:10]))
            e.tensor_scalar(do64, do64, dsm[0:64, 10:11], None, ALU.mult).then_inc(dec_o2, 1)
            for t in range(NT):
                for half in range(2):
                    e.wait_ge(att_ev, 2 * t + half + 1)
                    at = (slice(None), slice(4 * half, 4 * half + 4), slice(t * P, (t + 1) * P))
                    e.scalar_tensor_tensor(hT_parts[at],
                                           ps[:, (2 * t + half) % 4, :].rearrange("p (c f) -> p c f", c=4),
                                           subg[:, 0:1], plain(oh[at]), ALU.mult, ALU.subtract).then_inc(att_lo, 1)
            e.wait_ge(dec_ev, 1)
            e.scalar_tensor_tensor(hT_parts[:, :, SEQ:T], ps[:, 7, 0:NB * NH].rearrange("p (b h) -> p h b", b=NB),
                                   subg[:, 0:1], plain(oh[:, :, SEQ:T]), ALU.mult, ALU.subtract).then_inc(att_lo, 1)
            low(AOC, AO0, 0)
            for n in range(DC):
                if n + 1 < DC:
                    low(AOC + n + 1, AO0 + (n + 1) // 2, (n + 1) % 2)
                if n >= 1:
                    back_chunk(n - 1, DC)
            back_chunk(DC - 1, DC)
            e.wait_ge(rows_out, 16 * (1 + NT))
            norm_v(3, lambda q, t: q.wait_ge(back_add, 2 * DC), [3], [hT])
            moe_v(1)
            norm_v(4, lambda q, t: q.wait_ge(moe_comb, 5 + t + 1), [], [], normed=False)
            e.wait_ge(norm_rs, 5)
            e.wait_ge(ld_bs, 32)
            for t in range(5):
                r = rows_of(t)
                e.scalar_tensor_tensor(xn[0:r, t].rearrange("p c f -> p (c f)"), x[0:r, t, :],
                                       rstd[0:r, t:t + 1], gfin[0:r, :], ALU.mult, ALU.mult).then_inc(fin_y, 1)


INS = ["x_prompt", "x_sample", "cache_k", "cache_v", "page_table", "norm_mix", "norm_ffn", "w_uv", "sgu_gain",
       "w_sgu", "b_sgu", "w_gmlp_o", "norm_kv", "w_k", "w_v", "w_q", "lam_q", "lam_k", "subln_gain", "w_attn_o",
       "w_router_group", "b_router_group", "w_router_expert", "b_router_expert", "w_e_gate", "w_e_up", "w_e_down",
       "norm_final"]
OUTS = {"y_prompt": (1, SEQ, D), "y_sample": (NB, 1, D), "k_prompt": (1, NT, P, NH, 2, HD),
        "v_prompt": (1, NT, P, NH, P), "k_sample": (NB, 1, NH, 2, HD), "v_sample": (NB, 1, NH, P),
        "gmlp_v_sample": (1, NB, 1, DG)}


def kernel(**inputs):
    import numpy as np
    import concourse.bacc as bacc
    from concourse.bass_utils import run_bass_kernel_spmd

    nc = bacc.Bacc("TRN2", target_bir_lowering=False, num_devices=1)
    arrays = {"in_" + n: np.ascontiguousarray(inputs[n]) for n in INS}
    arrays["in_geometry"], arrays["in_past_bias"] = geometry(), past_bias()
    a = {n[3:]: nc.dram_tensor(n, v.shape, mybir.dt.from_np(v.dtype), kind="ExternalInput").ap()
         for n, v in arrays.items()}
    out = {n: nc.dram_tensor("out_" + n, shape, F32, kind="ExternalOutput").ap() for n, shape in OUTS.items()}
    build(nc, a, out)
    r = run_bass_kernel_spmd(nc, [arrays], core_ids=[0])
    return tuple(r.results[0]["out_" + n] for n in OUTS)
```
